# Optimizing a Trainium2 kernel written in Bass

```python
import math
import jax, jax.numpy as jnp
from jax import lax
import numpy as np

D_MODEL = 1024
BATCH = 1
SEQ = 256
DEPTH = 1

HEAD_DIM = 64
N_HEADS_DIL = 8
N_HEADS_MOBA = 8
N_HEADS_SELF = N_HEADS_DIL + N_HEADS_MOBA
DIL_WIDTH = N_HEADS_DIL * HEAD_DIM
MOBA_WIDTH = N_HEADS_MOBA * HEAD_DIM
MIX_WIDTH = DIL_WIDTH + MOBA_WIDTH
DILATION_PAIRS = ((128, 1), (512, 4), (2048, 16))
MOBA_BLOCK = 256
MOBA_TOPK = 3
MOBA_QCHUNK = 16
N_BUCKETS = 32
MAX_DISTANCE = 2048
N_MEM = 256
N_HEADS_MEM = 4
HEAD_DIM_MEM = D_MODEL // N_HEADS_MEM
D_FF = 2816
CONV_WIDTH = 3
EPS = 1e-6
NEG_INF = -1e30


def rmsnorm(x, g):
    xf = x.astype(jnp.float32)
    y = xf * lax.rsqrt(jnp.mean(xf * xf, axis=-1, keepdims=True) + EPS)
    return (y * g.astype(jnp.float32)).astype(x.dtype)

def rel_bucket(dist):
    max_exact = N_BUCKETS // 2
    n = jnp.maximum(dist, 0)
    nf = jnp.maximum(n, 1).astype(jnp.float32)
    large = max_exact + (jnp.log(nf / max_exact) / math.log(MAX_DISTANCE / max_exact)
                         * (N_BUCKETS - max_exact)).astype(jnp.int32)
    large = jnp.minimum(large, N_BUCKETS - 1)
    return jnp.where(n < max_exact, n, large)

def dilated_attention(q, k, v, bias_table):
    B, H, S, hd = q.shape
    scale = hd ** -0.5
    outs, lses = [], []
    for window, dil in DILATION_PAIRS:
        w_sub = window // dil
        L = S // dil
        nblk = -(-L // w_sub)
        Lp = nblk * w_sub

        def to_sub(t):
            t = t.reshape(B, H, L, dil, hd).transpose(0, 1, 3, 2, 4)
            t = jnp.pad(t, ((0, 0), (0, 0), (0, 0), (0, Lp - L), (0, 0)))
            return t.reshape(B, H, dil, nblk, w_sub, hd)

        def with_prev(t):
            prev = jnp.pad(t, ((0, 0), (0, 0), (0, 0), (1, 0), (0, 0), (0, 0)))[:, :, :, :-1]
            return jnp.concatenate([prev, t], axis=4)

        qs = to_sub(q)
        kb = with_prev(to_sub(k))
        vb = with_prev(to_sub(v))
        s = jnp.einsum('bhrnqd,bhrnkd->bhrnqk', qs, kb).astype(jnp.float32) * scale
        i = jnp.arange(w_sub)[:, None]
        j = jnp.arange(2 * w_sub)[None, :]
        diff = w_sub + i - j
        bias = bias_table[:, rel_bucket(diff * dil)].astype(jnp.float32)
        blk = jnp.arange(nblk)[:, None, None]
        valid = (diff >= 0) & (diff <= w_sub) & ((blk - 1) * w_sub + j >= 0)
        s = jnp.where(valid, s + bias[:, None, None], NEG_INF)
        m = jnp.max(s, axis=-1, keepdims=True)
        p = jnp.exp(s - m)
        den = jnp.sum(p, axis=-1, keepdims=True)
        o = jnp.einsum('bhrnqk,bhrnkd->bhrnqd', (p / den).astype(v.dtype), vb)
        lse = (m + jnp.log(den))[..., 0]
        o = o.reshape(B, H, dil, Lp, hd)[:, :, :, :L].transpose(0, 1, 3, 2, 4).reshape(B, H, S, hd)
        lse = lse.reshape(B, H, dil, Lp)[:, :, :, :L].transpose(0, 1, 3, 2).reshape(B, H, S)
        outs.append(o)
        lses.append(lse)
    wts = jax.nn.softmax(jnp.stack(lses), axis=0)
    out = jnp.einsum('pbhs,pbhsd->bhsd', wts, jnp.stack(outs).astype(jnp.float32))
    return out.astype(q.dtype)

def moba_attention(q, k, v, bias_table):
    B, H, S, hd = q.shape
    scale = hd ** -0.5
    nb = -(-S // MOBA_BLOCK)
    Sp = nb * MOBA_BLOCK
    pad = lambda t: jnp.pad(t, ((0, 0), (0, 0), (0, Sp - S), (0, 0)))
    qp, kp, vp = pad(q), pad(k), pad(v)
    kb = kp.reshape(B, H, nb, MOBA_BLOCK, hd)
    vb = vp.reshape(B, H, nb, MOBA_BLOCK, hd)
    k_mean = jnp.mean(kb.astype(jnp.float32), axis=3).astype(q.dtype)
    topk = min(MOBA_TOPK, nb)
    n_chunks = Sp // MOBA_QCHUNK
    qc = qp.reshape(B, H, n_chunks, MOBA_QCHUNK, hd).transpose(2, 0, 1, 3, 4)
    bi = jnp.arange(B)[:, None, None, None]
    hi = jnp.arange(H)[None, :, None, None]
    hi5 = jnp.arange(H)[None, :, None, None, None]
    bias_f = bias_table.astype(jnp.float32)

    def one_chunk(args):
        q_c, c = args
        t = c * MOBA_QCHUNK + jnp.arange(MOBA_QCHUNK)
        own = (c * MOBA_QCHUNK) // MOBA_BLOCK
        gate = jnp.einsum('bhqd,bhnd->bhqn', q_c, k_mean).astype(jnp.float32)
        gate = jnp.where(jnp.arange(nb) < own, gate, NEG_INF)
        _, idx = lax.top_k(gate, topk)
        sel_valid = jnp.arange(topk) < own
        k_sel = kb[bi, hi, idx]
        v_sel = vb[bi, hi, idx]
        s_sel = jnp.einsum('bhqd,bhqnkd->bhqnk', q_c, k_sel).astype(jnp.float32) * scale
        key_pos = idx[..., None] * MOBA_BLOCK + jnp.arange(MOBA_BLOCK)
        dist = t[:, None, None] - key_pos
        s_sel = jnp.where(sel_valid[:, None], s_sel + bias_f[hi5, rel_bucket(dist)], NEG_INF)
        k_own = lax.dynamic_slice_in_dim(kp, own * MOBA_BLOCK, MOBA_BLOCK, axis=2)
        v_own = lax.dynamic_slice_in_dim(vp, own * MOBA_BLOCK, MOBA_BLOCK, axis=2)
        s_own = jnp.einsum('bhqd,bhkd->bhqk', q_c, k_own).astype(jnp.float32) * scale
        dist_own = t[:, None] - (own * MOBA_BLOCK + jnp.arange(MOBA_BLOCK))[None, :]
        s_own = jnp.where(dist_own >= 0, s_own + bias_f[:, rel_bucket(dist_own)][None], NEG_INF)
        nsel = topk * MOBA_BLOCK
        s_all = jnp.concatenate([s_sel.reshape(B, H, MOBA_QCHUNK, nsel), s_own], axis=-1)
        p = jax.nn.softmax(s_all, axis=-1).astype(v.dtype)
        p_sel = p[..., :nsel].reshape(B, H, MOBA_QCHUNK, topk, MOBA_BLOCK)
        o = (jnp.einsum('bhqnk,bhqnkd->bhqd', p_sel, v_sel)
             + jnp.einsum('bhqk,bhkd->bhqd', p[..., nsel:], v_own))
        return o

    out = lax.map(one_chunk, (qc, jnp.arange(n_chunks)))
    return out.transpose(1, 2, 0, 3, 4).reshape(B, H, Sp, hd)[:, :, :S]

def memory_cross_attention(c, m, w_q, w_kv, w_o):
    B, S, D = c.shape
    qm = (c @ w_q).reshape(B, S, N_HEADS_MEM, HEAD_DIM_MEM)
    km, vm = jnp.split(m @ w_kv, 2, axis=-1)
    km = km.reshape(B, N_MEM, N_HEADS_MEM, HEAD_DIM_MEM)
    vm = vm.reshape(B, N_MEM, N_HEADS_MEM, HEAD_DIM_MEM)
    s = jnp.einsum('bqhd,bkhd->bhqk', qm, km).astype(jnp.float32) * (HEAD_DIM_MEM ** -0.5)
    p = jax.nn.softmax(s, axis=-1).astype(c.dtype)
    o = jnp.einsum('bhqk,bkhd->bqhd', p, vm).reshape(B, S, D)
    return o @ w_o

def conv_ffn(f, w_gate, w_up, conv_w, conv_b, w_down):
    S = f.shape[1]
    a = f @ w_gate
    ap = jnp.pad(a, ((0, 0), (CONV_WIDTH - 1, 0), (0, 0)))
    conv = conv_b
    for tap in range(CONV_WIDTH):
        conv = conv + ap[:, tap:tap + S] * conv_w[tap]
    return (jax.nn.silu(conv) * (f @ w_up)) @ w_down

def first_inputs(seed: int = 0) -> dict:
    key = jax.random.key(seed)
    ks = jax.random.split(key, 20)
    f32 = jnp.float32
    nrm = lambda k, shape, scale: jax.random.normal(k, shape, f32) * scale
    gain = lambda k, shape: 1.0 + 0.02 * jax.random.normal(k, shape, f32)
    return {
        "x": nrm(ks[0], (BATCH, SEQ, D_MODEL), 1.0),
        "mem": nrm(ks[1], (BATCH, N_MEM, D_MODEL), 1.0),
        "w_in": nrm(ks[2], (DEPTH, D_MODEL, 3 * MIX_WIDTH), D_MODEL ** -0.5),
        "g_mix": gain(ks[3], (DEPTH, D_MODEL)),
        "g_out_dil": gain(ks[4], (DEPTH, DIL_WIDTH)),
        "g_out_moba": gain(ks[5], (DEPTH, MOBA_WIDTH)),
        "w_out": nrm(ks[6], (DEPTH, MIX_WIDTH, D_MODEL), MIX_WIDTH ** -0.5),
        "rel_bias": nrm(ks[7], (N_HEADS_SELF, N_BUCKETS), 0.5),
        "g_cross": gain(ks[8], (DEPTH, D_MODEL)),
        "g_mem": gain(ks[9], (DEPTH, D_MODEL)),
        "w_q_mem": nrm(ks[10], (DEPTH, D_MODEL, D_MODEL), D_MODEL ** -0.5),
        "w_kv_mem": nrm(ks[11], (DEPTH, D_MODEL, 2 * D_MODEL), D_MODEL ** -0.5),
        "w_o_mem": nrm(ks[12], (DEPTH, D_MODEL, D_MODEL), D_MODEL ** -0.5),
        "g_ffn": gain(ks[13], (DEPTH, D_MODEL)),
        "w_gate": nrm(ks[14], (DEPTH, D_MODEL, D_FF), D_MODEL ** -0.5),
        "w_up": nrm(ks[15], (DEPTH, D_MODEL, D_FF), D_MODEL ** -0.5),
        "conv_w": nrm(ks[16], (DEPTH, CONV_WIDTH, D_FF), CONV_WIDTH ** -0.5),
        "conv_b": nrm(ks[17], (DEPTH, D_FF), 0.02),
        "w_down": nrm(ks[18], (DEPTH, D_FF, D_MODEL), D_FF ** -0.5),
        "g_final": gain(ks[19], (D_MODEL,)),
    }

def first_block(x, mem, w_in, g_mix, g_out_dil, g_out_moba, w_out, rel_bias, g_cross, g_mem,
              w_q_mem, w_kv_mem, w_o_mem, g_ffn, w_gate, w_up, conv_w, conv_b, w_down, g_final):
    B, S, _ = x.shape
    heads = lambda t, n: t.reshape(B, S, n, HEAD_DIM).transpose(0, 2, 1, 3)
    merge = lambda t, w: t.transpose(0, 2, 1, 3).reshape(B, S, w)
    h = x
    for l in range(DEPTH):
        u = rmsnorm(h, g_mix[l])
        qa, ka, va, qb, kb, vb = jnp.split(u @ w_in[l], 6, axis=-1)
        ya = dilated_attention(heads(qa, N_HEADS_DIL), heads(ka, N_HEADS_DIL),
                               heads(va, N_HEADS_DIL), rel_bias[:N_HEADS_DIL])
        yb = moba_attention(heads(qb, N_HEADS_MOBA), heads(kb, N_HEADS_MOBA),
                            heads(vb, N_HEADS_MOBA), rel_bias[N_HEADS_DIL:])
        y = jnp.concatenate([rmsnorm(merge(ya, DIL_WIDTH), g_out_dil[l]),
                             rmsnorm(merge(yb, MOBA_WIDTH), g_out_moba[l])], axis=-1)
        h = h + y @ w_out[l]
        h = h + memory_cross_attention(rmsnorm(h, g_cross[l]), rmsnorm(mem, g_mem[l]),
                                       w_q_mem[l], w_kv_mem[l], w_o_mem[l])
        h = h + conv_ffn(rmsnorm(h, g_ffn[l]), w_gate[l], w_up[l], conv_w[l], conv_b[l], w_down[l])
    return rmsnorm(h, g_final)


DEPTH_2 = 2

GRID_W = 64
CTX_LEN = 256
N_Q_HEADS = 8
N_KV_HEADS = 2
GQA_GROUP = N_Q_HEADS // N_KV_HEADS
HEAD_DIM_2 = 128
ATTN_WIDTH = N_Q_HEADS * HEAD_DIM_2
KV_WIDTH = N_KV_HEADS * HEAD_DIM_2
ROPE_THETA = 10000.0
ROPE_FREQS = HEAD_DIM_2 // 4
Q_BLOCK = 128
ATTN_SCALE = 1.0 / math.sqrt(HEAD_DIM_2)
GMLP_WIDTH = D_MODEL
GMLP_GROUPS = 4
GMLP_GROUP_DIM = GMLP_WIDTH // GMLP_GROUPS
CHUNK = 128
CONV_WIDTH_2 = D_MODEL
CONV_KERNEL = 31
CONV_PAD = CONV_KERNEL // 2
N_BRANCHES = 3
D_FF_2 = 4 * D_MODEL
Q_OFF = 0
K_OFF = Q_OFF + ATTN_WIDTH
V_OFF = K_OFF + KV_WIDTH
GU_OFF = V_OFF + KV_WIDTH
GV_OFF = GU_OFF + GMLP_WIDTH
CG_OFF = GV_OFF + GMLP_WIDTH
GATE_OFF = CG_OFF + 2 * CONV_WIDTH_2
IN_COLS = GATE_OFF + N_BRANCHES * D_MODEL


def rms_norm(x, g):
    xf = x.astype(jnp.float32)
    y = xf * lax.rsqrt(jnp.mean(xf * xf, axis=-1, keepdims=True) + EPS)
    return (y * g.astype(jnp.float32)).astype(x.dtype)

def layer_norm(x, g, b):
    xf = x.astype(jnp.float32)
    mu = jnp.mean(xf, axis=-1, keepdims=True)
    var = jnp.mean(jnp.square(xf - mu), axis=-1, keepdims=True)
    y = (xf - mu) * lax.rsqrt(var + EPS)
    return (y * g.astype(jnp.float32) + b.astype(jnp.float32)).astype(x.dtype)

def modulate(h, shift, scale):
    return h * (1.0 + scale) + shift

def axial_rope_tables(n_rows):
    row = jnp.repeat(jnp.arange(n_rows), GRID_W).astype(jnp.float32)
    col = jnp.tile(jnp.arange(GRID_W), n_rows).astype(jnp.float32)
    inv = ROPE_THETA ** (-jnp.arange(ROPE_FREQS, dtype=jnp.float32) / ROPE_FREQS)
    ang = jnp.concatenate([row[:, None] * inv, col[:, None] * inv], axis=-1)
    return jnp.cos(ang), jnp.sin(ang)

def apply_rope(x, cos, sin):
    half = HEAD_DIM_2 // 2
    x1, x2 = x[..., :half], x[..., half:]
    c = cos[None, :, None, :].astype(x.dtype)
    s = sin[None, :, None, :].astype(x.dtype)
    return jnp.concatenate([x1 * c - x2 * s, x2 * c + x1 * s], axis=-1)

def q_heads(p, q_norm_g):
    B, L, _ = p.shape
    return rms_norm(p[..., Q_OFF:K_OFF].reshape(B, L, N_Q_HEADS, HEAD_DIM_2), q_norm_g)

def kv_heads(pkv, k_norm_g):
    B, L, _ = pkv.shape
    k = rms_norm(pkv[..., :KV_WIDTH].reshape(B, L, N_KV_HEADS, HEAD_DIM_2), k_norm_g)
    v = pkv[..., KV_WIDTH:].reshape(B, L, N_KV_HEADS, HEAD_DIM_2)
    return k, v

def gqa_attend(q, k, v):
    s = jnp.einsum('bqhgd,bkhd->bhgqk', q, k).astype(jnp.float32) * ATTN_SCALE
    p = jax.nn.softmax(s, axis=-1).astype(v.dtype)
    return jnp.einsum('bhgqk,bkhd->bqhgd', p, v)

def latent_attention(q, k_all, v_all):
    B, S = q.shape[0], q.shape[1]
    nb = S // Q_BLOCK
    qb = q.reshape(B, nb, Q_BLOCK, N_KV_HEADS, GQA_GROUP, HEAD_DIM_2).transpose(1, 0, 2, 3, 4, 5)
    ob = lax.map(lambda qi: gqa_attend(qi, k_all, v_all), qb)
    return ob.transpose(1, 0, 2, 3, 4, 5).reshape(B, S, ATTN_WIDTH)

def chunk_spatial_gate(u, v, ws, bs):
    B, L, _ = v.shape
    nc = L // CHUNK
    vg = v.reshape(B, nc, CHUNK, GMLP_GROUPS, GMLP_GROUP_DIM)
    sv = jnp.einsum('gpq,bnqgc->bnpgc', ws, vg) + bs.T[None, None, :, :, None]
    return u * sv.reshape(B, L, GMLP_WIDTH)

def conformer_conv(a, conv_w, conv_b, norm_g, norm_b, w_o):
    gl = a[..., :CONV_WIDTH_2] * jax.nn.sigmoid(a[..., CONV_WIDTH_2:])
    y = lax.conv_general_dilated(gl, conv_w[:, None, :], window_strides=(1,),
                                 padding=[(CONV_PAD, CONV_PAD)],
                                 dimension_numbers=('NWC', 'WIO', 'NWC'),
                                 feature_group_count=CONV_WIDTH_2) + conv_b
    y = jax.nn.silu(layer_norm(y, norm_g, norm_b))
    return y @ w_o

def mixer_merge(p, attn, w_attn_o, gmlp_norm_g, gmlp_ws, gmlp_bs, w_gmlp_o,
                conv_w, conv_b, conv_norm_g, conv_norm_b, w_conv_o, w_out):
    a_out = attn @ w_attn_o
    gu = jax.nn.gelu(p[..., GU_OFF:GV_OFF])
    gv = rms_norm(jax.nn.gelu(p[..., GV_OFF:CG_OFF]), gmlp_norm_g)
    g_out = chunk_spatial_gate(gu, gv, gmlp_ws, gmlp_bs) @ w_gmlp_o
    c_out = conformer_conv(p[..., CG_OFF:GATE_OFF], conv_w, conv_b, conv_norm_g, conv_norm_b, w_conv_o)
    gates = jax.nn.sigmoid(p[..., GATE_OFF:])
    ga = gates[..., :D_MODEL]
    gg = gates[..., D_MODEL:2 * D_MODEL]
    gc = gates[..., 2 * D_MODEL:]
    return (ga * a_out + gg * g_out + gc * c_out) @ w_out

def sq_relu_mlp(h, w1, w2):
    return jnp.square(jax.nn.relu(h @ w1)) @ w2

def second_inputs(seed: int = 0) -> dict:
    key = jax.random.key(seed)
    ks = jax.random.split(key, 32)
    f32 = jnp.float32

    def nrm(k, shape, scale):
        return jax.random.normal(k, shape, f32) * scale

    def gain(k, shape):
        return 1.0 + 0.1 * jax.random.normal(k, shape, f32)

    L = DEPTH_2
    return {
        'x': nrm(ks[0], (BATCH, SEQ, D_MODEL), 1.0),
        'c': nrm(ks[1], (BATCH, D_MODEL), 1.0),
        'ctx': nrm(ks[2], (BATCH, CTX_LEN, D_MODEL), 1.0),
        'c_ctx': nrm(ks[3], (D_MODEL,), 1.0),
        'ada_w': nrm(ks[4], (L, D_MODEL, 6 * D_MODEL), 0.5 * D_MODEL ** -0.5),
        'ada_b': nrm(ks[5], (L, 6 * D_MODEL), 0.02),
        'mix_pre_g': gain(ks[6], (L, D_MODEL)),
        'mix_post_g': gain(ks[7], (L, D_MODEL)),
        'w_in': nrm(ks[8], (L, D_MODEL, IN_COLS), D_MODEL ** -0.5),
        'q_norm_g': gain(ks[9], (L, HEAD_DIM_2)),
        'k_norm_g': gain(ks[10], (L, HEAD_DIM_2)),
        'w_attn_o': nrm(ks[11], (L, ATTN_WIDTH, D_MODEL), ATTN_WIDTH ** -0.5),
        'gmlp_norm_g': gain(ks[12], (L, GMLP_WIDTH)),
        'gmlp_ws': nrm(ks[13], (L, GMLP_GROUPS, CHUNK, CHUNK), CHUNK ** -0.5),
        'gmlp_bs': gain(ks[14], (L, GMLP_GROUPS, CHUNK)),
        'w_gmlp_o': nrm(ks[15], (L, GMLP_WIDTH, D_MODEL), GMLP_WIDTH ** -0.5),
        'conv_w': nrm(ks[16], (L, CONV_KERNEL, CONV_WIDTH_2), CONV_KERNEL ** -0.5),
        'conv_b': nrm(ks[17], (L, CONV_WIDTH_2), 0.02),
        'conv_norm_g': gain(ks[18], (L, CONV_WIDTH_2)),
        'conv_norm_b': nrm(ks[19], (L, CONV_WIDTH_2), 0.02),
        'w_conv_o': nrm(ks[20], (L, CONV_WIDTH_2, D_MODEL), CONV_WIDTH_2 ** -0.5),
        'w_out': nrm(ks[21], (L, D_MODEL, D_MODEL), D_MODEL ** -0.5),
        'ffn_pre_g': gain(ks[22], (L, D_MODEL)),
        'ffn_post_g': gain(ks[23], (L, D_MODEL)),
        'w_ff1': nrm(ks[24], (L, D_MODEL, D_FF_2), D_MODEL ** -0.5),
        'w_ff2': nrm(ks[25], (L, D_FF_2, D_MODEL), D_FF_2 ** -0.5),
    }

def second_block(x, c, ctx, c_ctx, ada_w, ada_b, mix_pre_g, mix_post_g, w_in, q_norm_g, k_norm_g,
              w_attn_o, gmlp_norm_g, gmlp_ws, gmlp_bs, w_gmlp_o, conv_w, conv_b, conv_norm_g,
              conv_norm_b, w_conv_o, w_out, ffn_pre_g, ffn_post_g, w_ff1, w_ff2):
    B, S, _ = x.shape
    n_ctx = ctx.shape[1]
    ROWS = S // GRID_W
    cos, sin = axial_rope_tables(ROWS)
    xc = ctx
    for l in range(DEPTH_2):
        last = l == DEPTH_2 - 1
        mod = (jax.nn.silu(c) @ ada_w[l] + ada_b[l])[:, None, :]
        sh1, sc1, g1, sh2, sc2, g2 = jnp.split(mod, 6, axis=-1)
        modc = jax.nn.silu(c_ctx) @ ada_w[l] + ada_b[l]
        shc1, scc1, gc1, shc2, scc2, gc2 = jnp.split(modc, 6, axis=-1)

        h = modulate(rms_norm(x, mix_pre_g[l]), sh1, sc1)
        hc = modulate(rms_norm(xc, mix_pre_g[l]), shc1, scc1)
        p = h @ w_in[l]
        q = apply_rope(q_heads(p, q_norm_g[l]), cos, sin)
        k, v = kv_heads(p[..., K_OFF:GU_OFF], k_norm_g[l])
        k = apply_rope(k, cos, sin)
        if last:
            kc, vc = kv_heads(hc @ w_in[l][:, K_OFF:GU_OFF], k_norm_g[l])
        else:
            pc = hc @ w_in[l]
            qc = q_heads(pc, q_norm_g[l])
            kc, vc = kv_heads(pc[..., K_OFF:GU_OFF], k_norm_g[l])
        k_all = jnp.concatenate([kc, k], axis=1)
        v_all = jnp.concatenate([vc, v], axis=1)
        attn = latent_attention(q.reshape(B, S, N_KV_HEADS, GQA_GROUP, HEAD_DIM_2), k_all, v_all)
        y = mixer_merge(p, attn, w_attn_o[l], gmlp_norm_g[l], gmlp_ws[l], gmlp_bs[l], w_gmlp_o[l],
                        conv_w[l], conv_b[l], conv_norm_g[l], conv_norm_b[l], w_conv_o[l], w_out[l])
        x = x + g1 * rms_norm(y, mix_post_g[l])

        h2 = modulate(rms_norm(x, ffn_pre_g[l]), sh2, sc2)
        x = x + g2 * rms_norm(sq_relu_mlp(h2, w_ff1[l], w_ff2[l]), ffn_post_g[l])

        if not last:
            attn_c = gqa_attend(qc.reshape(B, n_ctx, N_KV_HEADS, GQA_GROUP, HEAD_DIM_2), kc, vc)
            yc = mixer_merge(pc, attn_c.reshape(B, n_ctx, ATTN_WIDTH), w_attn_o[l], gmlp_norm_g[l],
                             gmlp_ws[l], gmlp_bs[l], w_gmlp_o[l], conv_w[l], conv_b[l],
                             conv_norm_g[l], conv_norm_b[l], w_conv_o[l], w_out[l])
            xc = xc + gc1 * rms_norm(yc, mix_post_g[l])
            hc2 = modulate(rms_norm(xc, ffn_pre_g[l]), shc2, scc2)
            xc = xc + gc2 * rms_norm(sq_relu_mlp(hc2, w_ff1[l], w_ff2[l]), ffn_post_g[l])
    return x


def setup_inputs(seed=0):
    out = dict(first_inputs(seed))
    for name, value in second_inputs(seed + 1).items():
        if name != "x":
            out[name + "_2"] = value
    return out


def reference(
    x, mem, w_in, g_mix, g_out_dil, g_out_moba, w_out, rel_bias, g_cross, g_mem, w_q_mem,
    w_kv_mem, w_o_mem, g_ffn, w_gate, w_up, conv_w, conv_b, w_down, g_final, c_2, ctx_2,
    c_ctx_2, ada_w_2, ada_b_2, mix_pre_g_2, mix_post_g_2, w_in_2, q_norm_g_2, k_norm_g_2,
    w_attn_o_2, gmlp_norm_g_2, gmlp_ws_2, gmlp_bs_2, w_gmlp_o_2, conv_w_2, conv_b_2,
    conv_norm_g_2, conv_norm_b_2, w_conv_o_2, w_out_2, ffn_pre_g_2, ffn_post_g_2, w_ff1_2,
    w_ff2_2,
):
    x = first_block(
        x, mem, w_in, g_mix, g_out_dil, g_out_moba, w_out, rel_bias, g_cross, g_mem, w_q_mem,
        w_kv_mem, w_o_mem, g_ffn, w_gate, w_up, conv_w, conv_b, w_down, g_final,
    )
    return second_block(
        x, c_2, ctx_2, c_ctx_2, ada_w_2, ada_b_2, mix_pre_g_2, mix_post_g_2, w_in_2, q_norm_g_2,
        k_norm_g_2, w_attn_o_2, gmlp_norm_g_2, gmlp_ws_2, gmlp_bs_2, w_gmlp_o_2, conv_w_2,
        conv_b_2, conv_norm_g_2, conv_norm_b_2, w_conv_o_2, w_out_2, ffn_pre_g_2, ffn_post_g_2,
        w_ff1_2, w_ff2_2,
    )


_drawn_inputs = setup_inputs


def setup_inputs(seed=0):
    import zlib

    import numpy as np

    out = dict(_drawn_inputs(seed))
    spreads = {}
    factors = {'g_out_dil': 4.975,
     'g_out_moba': 4.935,
     'g_cross': 8.0,
     'g_mem': 8.0,
     'g_ffn': 4.575,
     'conv_b': 6.783,
     'ctx_2': 2.95,
     'q_norm_g_2': 8.0,
     'k_norm_g_2': 8.0,
     'conv_b_2': 7.782,
     'conv_norm_b_2': 8.0}
    for name, (base, spread) in spreads.items():
        noise = np.random.default_rng([zlib.crc32(name.encode()), seed]).standard_normal(out[name].shape)
        drawn = base * np.exp(spread * noise) if base else spread * noise
        out[name] = __import__('jax').numpy.asarray(drawn.astype(out[name].dtype))
    for name, factor in factors.items():
        out[name] = (out[name] * factor).astype(out[name].dtype)
    return out
```

```python
import math
from contextlib import ExitStack

import numpy as np
import concourse.bass as bass
from concourse import mybir

F32 = mybir.dt.float32
F32R = mybir.dt.float32r
I32 = mybir.dt.int32
ALU = mybir.AluOpType
ACT = mybir.ActivationFunctionType
AX = mybir.AxisListType

P = 128
S = 256
D = 1024
KT = D // P
NQ = 4
NW = 512
EPS = 1e-6
NEG = -1e30
MAGIC = 1597463007.0

N_BUCKETS, MAX_DISTANCE = 32, 2048
HEADS1, HD1 = 16, 64
FF1 = 2816
NT1 = FF1 // P
HEADS_MEM, HD_MEM = 4, 256
GRID_W, ROPE_THETA = 64, 10000.0
HD2, QH, KVH = 128, 8, 2
Q_OFF, K_OFF = 0, 1024
GU_OFF, GV_OFF, CG_OFF, GATE_OFF = 1536, 2560, 3584, 5632
TAPS2, PAD2 = 31, 15
GELU_A, GELU_B = 0.7978845608028654, 0.044715
LAYERS = 2


class Step:

    def __init__(self, kind, after=None, **args):
        self.kind, self.after = kind, after or {}
        self.of = args.get("of")
        self.l, self.s, self.h, self.g = args.get("l"), args.get("s"), args.get("h"), args.get("g")
        self.c, self.j, self.half = args.get("c"), args.get("j"), args.get("half")
        self.res, self.xn, self.src, self.dst = args.get("res"), args.get("xn"), args.get("src"), args.get("dst")
        self.slot, self.own, self.out = args.get("slot"), args.get("own"), args.get("out")
        self.scale, self.shift, self.imm, self.banks = (args.get(k) for k in ("scale", "shift", "imm", "banks"))
        self.ready, self.wait, self.tab, self.tk = (args.get(k) for k in ("ready", "wait", "tab", "tk"))
        self.rq, self.rk, self.gv, self.gu = (args.get(k) for k in ("rq", "rk", "gv", "gu"))
        self.job, self.taps, self.rb_free = (args.get(k) for k in ("job", "taps", "rb_free"))
        self.gate, self.first = args.get("gate"), args.get("first")
        self.evac, self.w, self.n0, self.typ = (args.get(k) for k in ("evac", "w", "n0", "typ"))
        self.k0, self.nk, self.cols, self.units, self.aux = (args.get(k) for k in ("k0", "nk", "cols", "units", "aux"))


def toeplitz_constants():
    d = np.arange(384) - (P - 1)
    n = np.maximum(d, 0)
    exact = N_BUCKETS // 2
    nf = np.maximum(n, 1).astype(np.float32)
    large = exact + (np.log(nf / np.float32(exact)).astype(np.float32)
                     / np.float32(math.log(MAX_DISTANCE / exact)) * np.float32(N_BUCKETS - exact)).astype(np.int32)
    bucket = np.where(n < exact, n, np.minimum(large, N_BUCKETS - 1))
    onehot = (np.arange(N_BUCKETS)[:, None] == bucket[None, :]).astype(np.float32)
    times = (d <= 128).astype(int) + (d % 4 == 0) + (d % 16 == 0)
    dil = np.where((d >= 0) & (times > 0), np.log(np.maximum(times, 1)), NEG)
    moba = np.where(d >= 0, 0.0, NEG)
    mask = np.concatenate([np.tile(dil, (8, 1)), np.tile(moba, (8, 1))]).astype(np.float32)
    return onehot, mask


def rope_constants():
    freqs = HD2 // 4
    row = np.repeat(np.arange(S // GRID_W), GRID_W).astype(np.float32)
    col = np.tile(np.arange(GRID_W), S // GRID_W).astype(np.float32)
    inv = (np.float32(ROPE_THETA) ** (-np.arange(freqs, dtype=np.float32) / np.float32(freqs))).astype(np.float32)
    ang = np.concatenate([row[:, None] * inv, col[:, None] * inv], axis=-1)
    c, s = np.cos(ang).astype(np.float32), np.sin(ang).astype(np.float32)
    return np.concatenate([c, c], axis=-1), np.concatenate([-s, s], axis=-1)


def make_plan():
    jobs = []

    def job(evac, w, n0, typ, slot, k0=0, nk=KT, n=NW, ready=None, **args):
        units = [[0, 1], [2, 3], [4, 5], [6, 7]] if nk == 8 else [[0, 1], [2, 3], [4], [5]]
        jb = Step("job", evac=evac, w=w, n0=n0, typ=typ, slot=slot, k0=k0, nk=nk, cols=n, units=units,
                             ready=ready or {}, aux=[[], [], [], []], **args)
        jobs.append(jb)
        return jb

    def put(jb, q, kind, **args):
        p = Step(kind, **args)
        jb.aux[q].append(p)
        return p

    def lo_of(t, i=4):
        return ("t_lo", t, 4, i)

    def transposed(jb, q, src, slot, ready, scale=None, shift=None, imm=1.0, banks=(0, 1, 2, 3)):
        return put(jb, q, "T", src=src, slot=slot, scale=scale, shift=shift, imm=imm, banks=banks,
                   after={"pe": ready})

    ada = [dict(l=l, c=c) for l in range(LAYERS) for c in range(6 * D // NW)]
    n_ada = [0]

    def ada_job():
        a = ada[n_ada[0]]
        n_ada[0] += 1
        return job("ada", f"ada{a['l']}", a["c"] * NW, "C", None, l=a["l"], c=a["c"], ready={0: [("pp_c4", None, 0, 1)]})

    a0 = ada_job()
    put(a0, 0, "pp_c")
    st_x = put(a0, 1, "pn_stat", res="x", xn="RB", after={"act": [("x_in", None, 0, 16)], "dve": [("x_in", None, 0, 16)]})
    a1 = ada_job()
    put(a1, 0, "pp")
    t_x = transposed(a1, 2, "RB", 0, [("pn_xn", st_x, 1, 1)], scale=("C1", 0))
    st_m = put(a1, 3, "pn_stat", res="c", xn="RA", after={"act": [("m_in", None, 0, 16)], "dve": [("m_in", None, 0, 16)]})
    a2 = ada_job()
    put(a2, 0, "toep")
    t_m = transposed(a2, 2, "RA", 1, [("pn_xn", st_m, 1, 1)], scale=("C1", 8))
    u = {0: [lo_of(t_x)]}
    j_qa = job("cp", "w_in", 0, "W", 0, ready=u, dst=("qT", 0))
    j_ka = job("cp", "w_in", 512, "W", 0, ready=u, dst=("qT", 1))
    j_va = job("cp", "w_in", 1024, "A", 0, ready=u, dst=("Yc", 0))
    j_va.after = {"act": [("pp_cols", None, 0, 1)]}
    j_qb = job("cp", "w_in", 1536, "W", 0, ready=u, dst=("RA", 0))
    j_qb.after = {"act": [("t_pe", t_m, 4, 4)]}
    j_kb = job("cp", "w_in", 2048, "W", 0, ready=u, dst=("RA", 1))
    j_vb = job("cp", "w_in", 2560, "A", 0, ready=u, dst=("Yc", 1))
    a3 = ada_job()
    um = {0: [lo_of(t_m)]}
    j_km0 = job("cp", "w_kv", 0, "W", 1, ready=um, dst=("TT", 0))
    j_km1 = job("cp", "w_kv", 512, "W", 1, ready=um, dst=("TT", 1))
    a4 = ada_job()
    j_vm0 = job("cp", "w_kv", 1024, "A", 1, ready=um, dst=("cres", 0))
    j_vm0.after = {"act": [("pn_xn", st_m, 1, 1)]}
    j_vm1 = job("cp", "w_kv", 1536, "A", 1, ready=um, dst=("cres", 1))
    hosts = [j_qb, j_kb, j_vb, j_km0, j_km1, j_vm0, j_vm1]
    hosts = [j_qb, j_kb, j_vb, a3, j_km0, j_km1, j_vm0, j_vm1]
    srcs = {0: [("cp_done", j_va, 1, 1)], 1: [("cp_done", j_vb, 1, 1)]}
    last = None
    for g in range(8):
        h = hosts[g]
        last = put(h, 0, "ba", g=g, ready=srcs[g // 4])
        put(h, 2, "baT", of=last)
        put(h, 3, "baV", of=last)
    a5 = ada_job()
    a6 = ada_job()
    yn = put(a5, 0, "y_norm", slot=2)
    y_ready = {0: [("yn_lo", None, 0, 2)]}
    j_o0 = job("res", "w_out", 0, "A", 2, ready=y_ready, res="x")
    j_o1 = job("res", "w_out", 512, "A", 2, res="x")

    def cross_norm(col, jb, wait_job, q0=0, jt=None, qt=2, slot=0):
        st = put(jb, q0, "pn_stat", res="x", xn="RB",
                 after={"act": [("res_done", wait_job, 1, 1)], "dve": []})
        return transposed(jt or jb, qt, "RB", slot, [("pn_xn", st, 1, 1)], scale=("C1", col))

    a7, a8 = ada_job(), ada_job()
    t_c = cross_norm(24, a7, j_o1, jt=a8, qt=0)
    j_q0 = job("cp", "w_q", 0, "W", 0, ready={0: [lo_of(t_c)]}, dst=("qT", 0))
    j_q1 = job("cp", "w_q", 512, "W", 0, dst=("qT", 1))
    mh = [ada_job() for _ in range(5)]
    mas = []
    for h in range(HEADS_MEM):
        m = put(mh[h], 0, "ma", h=h, slot=1, ready=[("cp_done", j_q1, 1, 1)])
        put(mh[h], 3, "maT", of=m)
        put(mh[h + 1], 1, "maV", of=m)
        mas.append(m)
    j_mo0 = job("res", "w_o", 0, "A", 1, ready={q: [("ma_lo", mas[q], 1, 1)] for q in range(4)}, res="x")
    j_mo1 = job("res", "w_o", 512, "A", 1, res="x")
    put(mh[4], 3, "ctx_load", after={"pool": [("ma_pv", mas[3], 1, 1)]})
    a14, a15 = ada_job(), ada_job()
    t_f = cross_norm(32, a14, j_mo1, jt=a15, qt=0)

    def gate_up(c):
        n = min(NW, FF1 - c * NW)
        slot = 1 + (c // 2) % 2
        gj = job("cgate", "w_gate", c * NW, "W", 0, n=n, ready={0: [lo_of(t_f)]}, c=c)
        uj = job("up", "w_up", c * NW, "W", 0, n=n, c=c, out=slot)
        uj.gate = gj
        return uj

    def down(k, ups, nk):
        r = {0: [("up_lo", ups[0], 1, 1)], 2: [("up_lo", ups[1], 1, 1)]}
        return [job("res", "w_down", n * NW, "A", 1 + k % 2, k0=k * KT, nk=nk, ready=r, res="x") for n in range(2)]

    ups = [gate_up(c) for c in range(4)]
    ada_job()
    ada_job()
    d0 = down(0, ups[0:2], 8)
    ada_job()
    ups += [gate_up(c) for c in range(4, 6)]
    while n_ada[0] < len(ada):
        aj = ada_job()
    d1 = down(1, ups[2:4], 8)
    d2 = down(2, ups[4:6], 6)

    def mods(jb, q, l, s):
        return put(jb, q, "modfin", l=l, s=s)

    def prenorm(jb, q, jt, qt, l, s, which, res, xn, act, slot=0):
        st = put(jb, q, "pn_stat", res=res, xn=xn, after=act)
        return transposed(jt, qt, xn, slot, [("pn_xn", st, 1, 1)], scale=("gs", l, s, which), shift=("sh", l, s, which))

    mf = {}
    mf[0, "c"] = mods(d1[0], 0, 0, "c")
    mf[0, "x"] = mods(d1[1], 0, 0, "x")
    mf[1, "c"] = mods(d2[0], 0, 1, "c")
    mf[1, "x"] = mods(d2[1], 2, 1, "x")
    t_next = prenorm(d1[1], 2, d2[0], 2, 0, "c", 0, "c", "RA",
                     {"act": [("ctx_in", None, 0, 16), ("cp_done", j_q0, 1, 1)], "dve": [("ctx_in", None, 0, 16)]})
    put(d2[1], 1, "gb", src=("g_final",))
    fin_after = [("res_done", d2[1], 1, 1)]

    def mixer(l, s, t_h, first_job_aux=None, ctxkv=None):
        w = f"win{l}"
        res = s
        own = 4 if s == "x" else 2 * l
        r = {0: [lo_of(t_h)]}
        q0 = job("q", w, Q_OFF, "A", 0, ready=r, c=0)
        q1 = job("q", w, Q_OFF + NW, "A", 0, c=1)
        kv = job("kv", w, K_OFF, "A", 0, own=own)
        tab = put(q0, 1, "tab", l=l, s=s)
        put(q0, 2, "gb", src=("gmlp_g", l))
        rq0 = put(q1, 0, "rq", of=q0, s=s, tab=tab)
        q1.after = {"act": [("rq_done", rq0, 1, 1)]}
        put(kv, 0, "tq", of=rq0)
        rq1 = put(kv, 1, "rq", of=q1, s=s, tab=tab)
        ga0 = job("glu_a", w, CG_OFF, "W", 0, half=0)
        put(ga0, 0, "tq", of=rq1)
        rk = put(ga0, 1, "rk", of=kv, s=s, tab=tab)
        tk = put(ga0, 3, "tk", of=rk, own=own)
        gg0 = job("glu_g", w, CG_OFF + D, "W", 0, half=0, of=ga0)
        ga0.after = {"act": [("rk_done", rk, 1, 1)]}
        gv = [job("gelu", w, GV_OFF + c * NW, "A", 0, dst=("RA", c)) for c in range(2)]
        gv[0].after = {"dve": []}
        gu = [job("gelu", w, GU_OFF + c * NW, "A", 0, dst=("RB", c)) for c in range(2)]
        ga1 = job("glu_a", w, CG_OFF + NW, "W", 0, half=1)
        gg1 = job("glu_g", w, CG_OFF + D + NW, "W", 0, half=1, of=ga1)
        ga1.after = {"act": [("gl_o", gg0, 1, 1)]}
        if (l, s) != (0, "x"):
            put(q0, 3, "wsT", l=l)
        gvn = put(gu[0], 0, "gv_norm", gv=gv)
        put(gu[0], 1, "gb", src=("grow", l, s, 0), after={"pool": [("gn_done", gvn, 1, 1)]})
        sp = put(ga1, 0, "spatial", l=l, of=gvn, gu=gu)
        t_g = transposed(ga1, 2, "RB", 2, [("sp_done", sp, 1, 1)], imm=0.5)
        slots = [(j, q) for j in (gv[0], gv[1], gu[0], gu[1], ga1) for q in range(4)]
        for i, (j, q) in enumerate(slots):
            put(j, q, "conv", half=0, l=l, job=gg0, tk=tk, taps=range(TAPS2 * i // len(slots), TAPS2 * (i + 1) // len(slots)))
        mg = []
        order = [("gmlp", 1, 2, lo_of(t_g)), ("attn", 0, 1, None), ("conv", 2, 2, None)]
        gates = []

        def gate(b, j):
            gj = job("gate", w, GATE_OFF + b * D + j * NW, "A", 0)
            gates.append(gj)
            return gj

        def branch(name, slot, j, gj, ready, first):
            bj = job("branch", f"{name}{l}", j * NW, "A", slot, ready={0: [ready]} if ready else {}, j=j, gate=gj, first=first)
            mg.append(bj)
            return bj

        seq = []
        for j in range(2):
            gj = gate(1, j)
            seq += [gj, branch("gmlp", 2, j, gj, lo_of(t_g), True)]
        seq[0].after = {"act": [("gl_o", gg1, 1, 1)]}
        at = []
        hosts = [gg0, gv[0], gv[1], gu[0], gu[1], ga1, gg1, seq[0]]
        for h in range(QH):
            p = put(hosts[h], 0, "at", h=h, s=s, own=own, l=l, slot=1, tk=tk, rk=rk, rq=rq1)
            put(hosts[h], 2, "atT", of=p)
            put(hosts[h], 3, "atV", of=p)
            at.append(p)
        for j in range(2):
            gj = gate(0, j)
            seq += [gj, branch("attn", 1, j, gj, ("at_lo", at[-1], 1, 1), False)]
        slots = [(j, q) for j in seq for q in range(4)]
        for i, (j, q) in enumerate(slots):
            put(j, q, "conv", half=1, l=l, job=gg1, tk=tk, taps=range(TAPS2 * i // len(slots), TAPS2 * (i + 1) // len(slots)))
        gc = [gate(2, j) for j in range(2)]
        lm = put(gc[0], 0, "ln_mu", l=l, rb_free=("t_pe", t_g, 4, 4))
        put(gc[0], 2, "ln_var", of=lm)
        lo = put(gc[1], 0, "ln_out", of=lm, l=l, slot=2)
        co = [branch("conv", 2, j, gc[j], ("ln_lo", lo, 1, 1), False) for j in range(2)]
        t1 = transposed(co[1], 2, "RA", 1, [("br_out", co[0], 1, 1)], imm=0.5, banks=(0, 1))
        wo0 = job("ycp", f"out{l}", 0, "A", 1, ready={0: [], 2: []}, j=0)
        t2 = transposed(wo0, 0, "RA", 1, [("br_out", co[1], 1, 1)], imm=0.5, banks=(2, 3))
        wo0.ready = {0: [lo_of(t1, 2)], 2: [lo_of(t2, 4)]}
        wo1 = job("ycp", f"out{l}", NW, "A", 1, j=1)
        wo0.after = {"act": [("ln_lo", lo, 1, 1)]}
        return co, (wo0, wo1), lo, t2

    def ffn(l, s, host, wait, t2):
        po = put(host, 0, "po", res=s, wait=wait, after={"act": [lo_of(t2)]})
        put(host, 0, "gb", src=("grow", l, s, 1), after={"pool": [("po_x", po, 1, 1)]})
        t = prenorm(host, 0, host, 0, l, s, 1, s, "RB", {"act": [("po_x", po, 1, 1)], "dve": [("po_x", po, 1, 1)]}, slot=0)
        return po, t

    def mlp_jobs(l, s, t, f10):
        f1 = [f10]
        r = {0: [lo_of(t)]}
        f10.ready = r
        f2 = []

        def up2(c):
            f1.append(job("relu2", f"ff1{l}", c * NW, "W", 0, c=c, out=1 + (c // 2) % 2))

        def dn(k):
            rr = {0: [("r2_lo", f1[2 * k], 1, 1)], 2: [("r2_lo", f1[2 * k + 1], 1, 1)]}
            for n in range(2):
                f2.append(job("acc0" if k == 0 else "acc", f"ff2{l}", n * NW, "A", 1 + k % 2, k0=k * KT, ready=rr, j=n))
                f2[-1].first_of = f2[n]

        up2(1)
        up2(2)
        up2(3)
        dn(0)
        up2(4)
        up2(5)
        dn(1)
        up2(6)
        up2(7)
        dn(2)
        dn(3)
        return f1, f2

    def f1_first(l):
        return job("relu2", f"ff1{l}", 0, "W", 0, c=0, out=1)

    first_ctx = len(jobs)
    co, wo, lo, t2 = mixer(0, "c", t_next)
    jobs[first_ctx].aux[0].insert(0, Step("final", after={"act": fin_after, "dve": fin_after}))
    f10 = f1_first(0)
    po, t = ffn(0, "c", f10, wo[1], t2)
    f1, f2 = mlp_jobs(0, "c", t, f10)
    t_next = prenorm(f2[4], 0, f2[5], 0, 0, "x", 0, "x", "RA",
                     {"act": [("fin_x", None, 0, 1)], "dve": []})
    last_f2 = f2[-1]
    first_x = len(jobs)
    co, wo, lo, t2 = mixer(0, "x", t_next)
    po_c = Step("po", res="c", wait=last_f2, after={})
    jobs[first_x].aux[0].insert(0, po_c)
    st = put(co[0], 2, "pn_stat", res="c", xn="RB",
             after={"act": [("po_x", po_c, 1, 1), ("ln_lo", lo, 1, 1)], "dve": [("po_x", po_c, 1, 1)]})
    t_c1 = transposed(co[1], 1, "RB", 0, [("pn_xn", st, 1, 1)], scale=("gs", 1, "c", 0), shift=("sh", 1, "c", 0))
    wo[0].after["act"].append(("t_pe", t_c1, 4, 4))
    kvc = job("kv", "win1", K_OFF, "A", 0, ready={0: [lo_of(t_c1)]}, own=2)
    f10 = f1_first(0)
    po = put(kvc, 0, "po", res="x", wait=wo[1], after={"act": [lo_of(t2)]})
    put(kvc, 0, "gb", src=("grow", 0, "x", 1), after={"pool": [("po_x", po, 1, 1)]})
    t = prenorm(kvc, 1, f10, 0, 0, "x", 1, "x", "RB", {"act": [("po_x", po, 1, 1)], "dve": [("po_x", po, 1, 1)]}, slot=0)
    f1, f2 = mlp_jobs(0, "x", t, f10)
    tab = put(f10, 1, "tab", l=1, s="c")
    rk = put(f10, 2, "rk", of=kvc, s="c", tab=tab)
    put(f1[1], 0, "tk", of=rk, own=2)
    n0 = len(jobs)
    t_slot = Step("T", src="RB", slot=0, scale=("gs", 1, "x", 0), shift=("sh", 1, "x", 0), imm=1.0,
                             banks=(0, 1, 2, 3), after={})
    co, wo, lo, t2 = mixer(1, "x", t_slot)
    po = Step("po", res="x", wait=f2[-1], after={})
    st = Step("pn_stat", res="x", xn="RB", after={"act": [("po_x", po, 1, 1)], "dve": [("po_x", po, 1, 1)]})
    t_slot.after = {"pe": [("pn_xn", st, 1, 1)]}
    jobs[n0].aux[0][0:0] = [po, st, t_slot]
    f10 = f1_first(1)
    po, t = ffn(1, "x", f10, wo[1], t2)
    f1, f2 = mlp_jobs(1, "x", t, f10)
    tail = [Step("po", res="x", wait=f2[-1], after={})]

    count = {}
    frees = dict(cp="cp_done", q="q_cp", kv="kv_cp", res="res_done", gelu="ge_out", glu_a="gl_a", glu_g="gl_th",
                 gate="ga_th", branch="br_out", relu2="r2_relu", acc0="ac_cp", acc="ac_add", ycp="y_cp",
                 cgate="cg_cp", up="up_mul", ada="ad_cp")
    bank = {}

    def number(x, kind):
        x.n = count.get(kind, 0)
        count[kind] = x.n + 1

    def use(p, banks, after):
        p.bank_free = {b: bank[b] for b in banks if b in bank}
        for b in banks:
            bank[b] = after

    gb_reader, gb_count, conv_ops = None, 0, 0
    for jb in jobs + [None]:
        for p in ([x for q in jb.aux for x in q] if jb else tail):
            number(p, p.kind)
            k = p.kind
            if k == "gb":
                p.free, gb_count = gb_reader, gb_count + 1
            elif k in ("final", "gv_norm", "po"):
                p.gb = gb_count
                gb_reader = {"final": ("fin_x", None, 0, 1), "gv_norm": ("gn_done", p, 1, 1), "po": ("po_x", p, 1, 1)}[k]
            elif k == "T":
                p.bank_free = {b: bank[b] for b in p.banks if b in bank}
                for b in p.banks:
                    bank[b] = ("t_lo", p, 4, b + 1)
            elif k == "pp_c":
                use(p, (3,), ("pp_c4", None, 0, 1))
            elif k == "pp":
                use(p, (0, 1, 2), ("pp_cols", None, 0, 1))
            elif k == "toep":
                use(p, (3,), ("tp_r", None, 0, 1))
            elif k == "ba":
                use(p, (0, 1), ("ba_sb", p, 2, 2))
            elif k == "baT":
                use(p, (2, 3), ("ba_pt", p.of, 2, 2))
            elif k == "baV":
                use(p, (0,), ("ba_y", p.of, 1, 1))
            elif k == "y_norm":
                use(p, (2, 3), ("yn_y", None, 0, 2))
            elif k == "ma":
                use(p, (0,), ("ma_p", p, 1, 1))
            elif k == "maT":
                use(p, (1,), ("ma_pt", p.of, 1, 1))
            elif k == "maV":
                use(p, (2,), ("ma_lo", p.of, 1, 1))
            elif k == "modfin":
                use(p, (3,), ("mf_c", p, 1, 1))
            elif k == "tq":
                use(p, (0, 1), ("tq_cp", p, 1, 1))
            elif k == "tk":
                use(p, (2,), ("tk_cp", p, 1, 1))
            elif k == "at":
                use(p, (0, 1), ("at_p", p, 2, 2))
            elif k == "atT":
                use(p, (2, 3), ("at_pt", p.of, 1, 1))
            elif k == "atV":
                use(p, (0,), ("at_lo", p.of, 1, 1))
            elif k == "spatial":
                use(p, (0, 1, 2, 3), ("sp_done", p, 1, 1))
            elif k == "wsT":
                p.at_before = count.get("atT", 0)
                use(p, (3,), ("ws_cp", p, 1, 1))
            elif k == "conv":
                conv_ops += 4 * len(p.taps)
            elif k == "ln_mu":
                p.conv_after = conv_ops
                use(p, (2,), ("ln_d", p, 1, 1))
            elif k == "ln_var":
                use(p, (3,), ("ln_n", p.of, 1, 1))
        if jb:
            number(jb, jb.evac)
            jb.po_before = count.get("po", 0)
            jb.free = (frees[jb.evac], jb, 1, 1)
    for i, jb in enumerate(jobs):
        jb.i = i
        jb.two_back = jobs[i - 2] if i >= 2 else None
    return jobs, tail


SEMS = """x_in m_in ctx_in pr_in c_in rb_in cst_in tables_in ident_ready ones_ready c4_zeroed glp_zeroed
pp_pc pp_th pp_c4 pp_pe pp_cols pp_cp tp_tab tp_pe tp_r tp_st bias_in0 bias_in1
pn_ss pn_xn t_pe t_hi t_lo
ba_s ba_sb ba_nm ba_p ba_pn ba_tp ba_pt ba_pv ba_y yn_sq yn_ss yn_y yn_hi yn_lo
ma_s ma_nm ma_p ma_pn ma_tp ma_pt ma_pv ma_hi ma_lo
cp_done res_done cg_cp cg_v cg_t cg_s up_mul up_hi up_lo ad_cp ad_st fin_ss fin_x
mf_in mf_sum mf_pe mf_c mf_r mf_st gb_in q_cp kv_cp gqk_in tab_done rq_done rk_done tq_pe tq_cp tk_pe tk_cp
at_s at_nb at_p at_pn at_tp at_pt at_pv at_hi at_lo
ge_sq ge_z ge_t ge_out gl_a gl_th gl_o gn_ss gn_done sp_pe sp_done
ln_mean ln_d ln_sq ln_vs ln_n ln_s ln_th ln_r ln_hi ln_lo ga_th br_out cv_done ws_in ws_pe ws_cp
r2_relu r2_sq r2_hi r2_lo ac_cp ac_add y_cp po_ss po_x out_st
act_step dve_step""".split()


def value(e):
    name, x, per, i = e
    return i if x is None else x.n * per + i


def build(nc, A, out):
    jobs, tail = make_plan()
    with ExitStack() as ctx:
        def sb(name, shape, dt=F32):
            return ctx.enter_context(nc.sbuf_tensor(name, shape, dt))

        sem = {n: ctx.enter_context(nc.semaphore(n)) for n in SEMS}
        loaded = [ctx.enter_context(nc.semaphore(f"unit_loaded{q}")) for q in range(NQ)]
        hi_done = [ctx.enter_context(nc.semaphore(f"unit_hi{q}")) for q in range(NQ)]
        lo_done = [ctx.enter_context(nc.semaphore(f"unit_lo{q}")) for q in range(NQ)]
        used = [ctx.enter_context(nc.semaphore(f"unit_used{q}")) for q in range(NQ)]

        raw = sb("raw", [P, NQ, 2, NW])
        whi = sb("whi", [P, NQ, 2, NW], F32R)
        wlo = sb("wlo", [P, NQ, 2, NW], F32R)
        ohi = sb("ohi", [P, 3, KT, S], F32R)
        olo = sb("olo", [P, 3, KT, S], F32R)
        chi = sb("chi", [P, KT, P], F32R)
        res = {"x": sb("xres", [P, 2 * D]), "c": sb("cres", [P, 2 * D])}
        RA, RB = sb("RA", [P, 2 * D]), sb("RB", [P, 2 * D])
        qT = sb("qT", [P, 8 * S])
        kvb = sb("kvb", [P, 6, 2 * S])
        Pb, PTb = sb("Pb", [P, 2, 2 * S]), sb("PTb", [P, 4 * S])
        AB = sb("AB", [P, 4 * S])
        GLP = sb("GLP", [P, 4, S + 2 * PAD2])
        Yc = sb("Yc", [P, 8 * S])
        TT = sb("TT", [P, 2, 4 * S])
        GB = sb("GB", [P, D])
        ident, ones = sb("ident", [P, P]), sb("ones", [P, P])
        C1, C2, CW = sb("C1", [P, P]), sb("C2", [P, 88]), sb("CW", [P, LAYERS, TAPS2 * KT])
        wsT = sb("wsT", [P, 4, P])
        cos2, sinpm = sb("cos_rows", [P, 2, HD2]), sb("sin_rows", [P, 2, HD2])
        GQK = sb("GQK", [P, 2, HD2])
        stage = sb("stage", [4, NW])
        csb = sb("csb", [P, 2, 16])
        MF = sb("MF", [48, 4, P])
        modc = sb("modc", [P, 4, 48])
        gsc = sb("gsc", [P, 4, 16])
        st = sb("st", [P, 16, 16])
        den = sb("den", [P, 64])
        tabT = sb("tabT", [N_BUCKETS, HEADS1])

        gps = ctx.enter_context(nc.psum_tensor("gps", [P, 2, 2 * NW], F32))
        aps = ctx.enter_context(nc.psum_tensor("aps", [P, 4, NW], F32))
        mod_dram = nc.dram_tensor("mod_dram", [LAYERS, 4, 6 * D], F32)
        grow_dram = nc.dram_tensor("grow_dram", [LAYERS, 2, 2, D], F32)
        toep_dram = nc.dram_tensor("toep_dram", [HEADS1, 384], F32)

        flat = {"RA": RA, "RB": RB, "qT": qT, "Yc": Yc, "xres": res["x"], "cres": res["c"]}

        def rows(t):
            return t[:, :].rearrange("p (m d) -> p m d", m=2)

        def bank(b):
            return aps[:, b, :]

        PR = Yc[:, 0:7 * P].rearrange("p (i c) -> p i c", i=7)
        bias = kvb[:, :, :].rearrange("p a b -> p (a b)")[:, 0:2 * 4 * S].rearrange("p (g h j) -> p g h j", g=2, h=4)
        kmT, vm = TT, rows(res["c"])
        OH = AB[0:N_BUCKETS, 0:384]
        MSK = GB[0:HEADS1, 0:384]
        TR = GB[0:HEADS1, 384:768]
        MODS = {(0, "c"): 0, (0, "x"): 1, (1, "c"): 2, (1, "x"): 3}

        def column(spec, kt):
            if spec is None:
                return None
            if spec[0] == "C1":
                return C1[:, spec[1] + kt:spec[1] + kt + 1]
            _, l, s, which = spec
            i = MODS[l, s]
            if spec[0] == "gs":
                return gsc[:, i, 8 * which + kt:8 * which + kt + 1]
            return modc[:, i, 24 * which + kt:24 * which + kt + 1]

        def wait(eng, *events):
            for e in events:
                eng.wait_ge(sem[e[0]], value(e))

        def ev(name, x, per=1, i=1):
            return (name, x, per, i)

        def weight(jb, q):
            ks = jb.units[q]
            r0 = (jb.k0 + ks[0]) * P
            return A[jb.w][r0:r0 + len(ks) * P, jb.n0:jb.n0 + jb.cols].rearrange("(k p) n -> p k n", p=P)

        def part(t, jb, q):
            return t[:, q, 0:len(jb.units[q]), 0:jb.cols]

        def psum_job(jb):
            return gps[:, jb.i % 2, :]

        def tiles(ap, a):
            return ap.rearrange("p (a b) -> p a b", a=a)

        def t_step(p, b):
            if len(p.banks) == 4:
                return 1
            return 1 if b in (0, 3) else 3

        block = ctx.enter_context(nc.Block())

        @block.sync
        def _(sp):
            for jb in jobs:
                for q in range(NQ):
                    if jb.i:
                        sp.wait_ge(lo_done[q], jb.i)
                    sp.dma_start(part(raw, jb, q), weight(jb, q)).then_inc(loaded[q], 16)
            wait(sp, ev("po_x", tail[0]))
            sp.dma_start(out[0].rearrange("(m p) d -> p m d", p=P), rows(res["x"])).then_inc(sem["out_st"], 16)
            sp.wait_ge(sem["out_st"], 16)

        @block.gpsimd
        def _(pool):
            def load(dst, src, name):
                pool.dma_start(dst, src).then_inc(sem[name], 16)

            pool.memset(ident[:], 0.0).then_inc(sem["ident_ready"], 1)
            pool.wait_ge(sem["ident_ready"], 1)
            pool.affine_select(out=ident[:], in_=ident[:], compare_op=ALU.not_equal, fill=1.0, base=0,
                               pattern=[[-1, P]], channel_multiplier=1).then_inc(sem["ident_ready"], 1)
            load(PR[0:8, 6, :], A["c"][0].rearrange("(k p) -> k p", p=P), "c_in")
            load(PR[8:16, 6, :], A["c_ctx"].rearrange("(k p) -> k p", p=P), "c_in")
            load(rows(res["x"]), A["x"].rearrange("(m p) d -> p m d", p=P), "x_in")
            pool.memset(ones[:], 1.0 / D).then_inc(sem["ones_ready"], 1)
            r = 0
            for name in ("g_mix", "g_mem", "g_out_dil", "g_out_moba", "g_cross", "g_ffn", "conv_b"):
                n = A[name].shape[0] // P
                load(PR[r:r + n, 0, :], A[name].rearrange("(k p) -> k p", p=P), "pr_in")
                r += n
            load(PR[r:r + 3 * NT1, 0, :], A["conv_w"].rearrange("t (k p) -> (t k) p", p=P), "pr_in")
            load(rows(res["c"]), A["mem"].rearrange("(m p) d -> p m d", p=P), "m_in")
            for l in range(LAYERS):
                r = 44 * l
                for name in ("mix_pre_g", "ffn_pre_g", "conv_norm_g", "conv_norm_b", "conv_b_2"):
                    load(PR[r:r + 8, 1, :], A[name][l].rearrange("(k p) -> k p", p=P), "pr_in")
                    r += 8
                load(PR[r:r + 4, 1, :], A["gmlp_bs"][l], "pr_in")
                cw = A["conv_w_2"][l].rearrange("t (k p) -> (t k) p", p=P)
                for h in range(2):
                    load(PR[0:124, 2 + 2 * l + h, :], cw[124 * h:124 * h + 124, :], "pr_in")
            pool.dma_start(tabT[:], A["rel_bias"].rearrange("h b -> b h"),
                           allow_slow_non_contiguous=True).then_inc(sem["rb_in"], 16)
            load(OH, A["onehot"], "rb_in")
            load(MSK, A["mask"], "rb_in")
            load(cos2[:], A["cos2"].rearrange("(m p) d -> p m d", p=P), "cst_in")
            load(sinpm[:], A["sinpm"].rearrange("(m p) d -> p m d", p=P), "cst_in")

            def toep(p):
                pool.wait_ge(sem["tp_r"], 1)
                pool.dma_start(toep_dram.ap(), TR).then_inc(sem["tp_st"], 16)
                pool.wait_ge(sem["tp_st"], 16)
                for g in range(2):
                    bias_load(g)

            def bias_load(g):
                src = bass.AP(tensor=toep_dram, offset=g * 4 * 384, ap=[[1, P], [384, 4], [1, S]])
                load(bias[:, g % 2], src, f"bias_in{g % 2}")

            def ba(p):
                if p.g in (2, 4):
                    g = p.g // 2 + 1
                    pool.wait_ge(sem["ba_sb"], 4 * (g - 1))
                    bias_load(g)

            def ctx_load(p):
                wait(pool, *p.after["pool"])
                load(rows(res["c"]), A["ctx"].rearrange("(m p) d -> p m d", p=P), "ctx_in")

            def modfin(p):
                pool.wait_ge(sem["ad_st"], 16 * 12 * (p.l + 1))
                if p.n:
                    pool.wait_ge(sem["mf_st"], 32 * p.n)
                v = 1 if p.s == "c" else 0
                load(MF[:, 0, :], mod_dram.ap()[p.l, v].rearrange("(r c) -> r c", c=P), "mf_in")
                load(MF[:, 1, :], mod_dram.ap()[p.l, 2 + v].rearrange("(r c) -> r c", c=P), "mf_in")
                load(MF[:, 2, :], A["ada_b"][p.l].rearrange("(r c) -> r c", c=P), "mf_in")
                load(MF[16:24, 3, :], A["mix_post_g"][p.l].rearrange("(r c) -> r c", c=P), "mf_in")
                load(MF[40:48, 3, :], A["ffn_post_g"][p.l].rearrange("(r c) -> r c", c=P), "mf_in")
                wait(pool, ev("mf_r", p))
                for k in range(2):
                    pool.dma_start(grow_dram.ap()[p.l, v, k].rearrange("(r c) -> r c", c=P),
                                   MF[16 + 24 * k:24 + 24 * k, 3, :]).then_inc(sem["mf_st"], 16)
                pool.wait_ge(sem["mf_st"], 32 * (p.n + 1))

            def gb(p):
                if p.free:
                    wait(pool, p.free)
                if p.src[0] == "g_final":
                    src = A["g_final"]
                elif p.src[0] == "gmlp_g":
                    src = A["gmlp_norm_g"][p.src[1]]
                else:
                    _, l, s, k = p.src
                    src = grow_dram.ap()[l, 1 if s == "c" else 0, k]
                load(GB[:], src.partition_broadcast(P), "gb_in")

            def tab(p):
                if p.n:
                    pool.wait_ge(sem["rk_done"], p.n)
                load(GQK[:, 0, :], A["q_norm_g"][p.l].partition_broadcast(P), "gqk_in")
                load(GQK[:, 1, :], A["k_norm_g"][p.l].partition_broadcast(P), "gqk_in")

            def ws_load(p):
                if p.n:
                    pool.wait_ge(sem["at_tp"], p.at_before)
                else:
                    pool.wait_ge(sem["ma_tp"], HEADS_MEM)
                load(tiles(Pb[:, 0, :], 4), A["gmlp_ws"][p.l].rearrange("g p q -> p g q"), "ws_in")

            stages = dict(wsT=ws_load, toep=toep, ba=ba, ctx_load=ctx_load, modfin=modfin, gb=gb, tab=tab)
            for jb in jobs:
                for q in range(NQ):
                    for p in jb.aux[q]:
                        if p.kind in stages:
                            stages[p.kind](p)
                if jb.evac == "ada":
                    wait(pool, ev("ad_cp", jb))
                    pool.dma_start(mod_dram.ap()[jb.l, :, jb.n0:jb.n0 + NW], stage[:]).then_inc(sem["ad_st"], 16)

        @block.tensor
        def _(pe):
            mm = nc.tensor.matmul

            def free(p):
                for e in p.bank_free.values():
                    wait(pe, e)

            def pp_c(p):
                pe.wait_ge(sem["ident_ready"], 2)
                pe.wait_ge(sem["c_in"], 32)
                nc.tensor.transpose(aps[:, 3, 0:16], PR[0:16, 6, :], ident[0:16, 0:16]).then_inc(sem["pp_pc"], 1)

            def pp(p):
                free(p)
                pe.wait_ge(sem["pr_in"], 16 * 24)
                for i, n in enumerate((P, 88)):
                    nc.tensor.transpose(aps[:, 0, i * P:i * P + n], PR[0:n, i, :], ident[0:n, 0:n])
                for i in range(4):
                    t = nc.tensor.transpose(aps[:, 1 + i // 2, 124 * (i % 2):124 * (i % 2) + 124], PR[0:124, 2 + i, :],
                                            ident[0:124, 0:124])
                t.then_inc(sem["pp_pe"], 1)

            def toep(p):
                free(p)
                pe.wait_ge(sem["rb_in"], 48)
                mm(aps[0:HEADS1, 3, 0:384], tabT[:], OH, start=True, stop=True).then_inc(sem["tp_pe"], 1)

            def T(p):
                wait(pe, *p.after["pe"])
                src = rows(flat[p.src])
                for b in p.banks:
                    if b in p.bank_free:
                        wait(pe, p.bank_free[b])
                    for i in range(2):
                        for m in range(2):
                            t = nc.tensor.transpose(aps[:, b, i * S + m * P:i * S + m * P + P],
                                                    src[:, m, (2 * b + i) * P:(2 * b + i + 1) * P], ident[:])
                    t.then_inc(sem["t_pe"], t_step(p, b))

            def ba(p):
                free(p)
                wait(pe, *p.ready)
                q_, k_ = (qT[:, 0:4 * S], qT[:, 4 * S:8 * S]) if p.g < 4 else (RA[:, 0:4 * S], RA[:, 4 * S:8 * S])
                c = (p.g % 4) * S
                for hh in range(2):
                    r = slice(HD1 * hh, HD1 * hh + HD1)
                    mm(aps[:, hh, 0:P], q_[r, c:c + P], k_[r, c:c + P], start=True, stop=True)
                    mm(aps[:, hh, P:3 * P], q_[r, c + P:c + S], k_[r, c:c + S], start=True,
                       stop=True).then_inc(sem["ba_s"], 1)

            def baT(p):
                free(p)
                for hh in range(2):
                    wait(pe, ev("ba_pn", p.of, 2, hh + 1))
                    for k in range(3):
                        t = nc.tensor.transpose(aps[:, 2 + hh, k * P:(k + 1) * P], Pb[:, hh, k * P:(k + 1) * P], ident[:])
                    t.then_inc(sem["ba_tp"], 1)

            def baV(p):
                free(p)
                v = tiles(Yc[:, (p.of.g // 4) * 4 * S:(p.of.g // 4 + 1) * 4 * S], 2)
                for hh in range(2):
                    wait(pe, ev("ba_pt", p.of, 2, hh + 1))
                    h = 2 * (p.of.g % 4) + hh
                    o = aps[HD1 * hh:HD1 * hh + HD1, 0, 0:S]
                    mm(o, v[:, 0, h * HD1:(h + 1) * HD1], PTb[:, hh * 2 * S:hh * 2 * S + S], start=True, stop=False)
                    t = mm(o[:, P:S], v[:, 1, h * HD1:(h + 1) * HD1], PTb[:, hh * 2 * S + S:hh * 2 * S + S + P],
                           start=False, stop=True)
                t.then_inc(sem["ba_pv"], 1)

            def y_norm(p):
                pe.wait_ge(sem["ones_ready"], 1)
                for half in range(2):
                    pe.wait_ge(sem["yn_sq"], half + 1)
                    wait(pe, p.bank_free[2 + half])
                    sq = Pb[:, :, :].rearrange("p a b -> p (a b)") if half == 0 else PTb[:]
                    for k in range(4):
                        t = mm(aps[:, 2 + half, 0:S], ones[:], sq[:, k * S:(k + 1) * S], start=k == 0, stop=k == 3)
                    t.then_inc(sem["yn_ss"], 1)

            def ma(p):
                free(p)
                wait(pe, *p.ready)
                for m in range(2):
                    for i in range(2):
                        k = 2 * p.h + i
                        t = mm(aps[:, 0, m * S:(m + 1) * S], qT[:, k * S + m * P:k * S + m * P + P],
                               kmT[:, k // 4, (k % 4) * S:(k % 4) * S + S], start=i == 0, stop=i == 1)
                t.then_inc(sem["ma_s"], 1)

            def maT(p):
                free(p)
                wait(pe, ev("ma_pn", p.of))
                for kb in range(2):
                    for m in range(2):
                        t = nc.tensor.transpose(aps[:, 1, kb * S + m * P:kb * S + m * P + P],
                                                Pb[:, m, kb * P:(kb + 1) * P], ident[:])
                t.then_inc(sem["ma_tp"], 1)

            def maV(p):
                free(p)
                wait(pe, ev("ma_pt", p.of))
                h = p.of.h
                for i in range(2):
                    for kb in range(2):
                        t = mm(aps[:, 2, i * S:(i + 1) * S], vm[:, kb, h * HD_MEM + i * P:h * HD_MEM + (i + 1) * P],
                               PTb[:, kb * S:(kb + 1) * S], start=kb == 0, stop=kb == 1)
                t.then_inc(sem["ma_pv"], 1)

            def modfin(p):
                free(p)
                wait(pe, ev("mf_sum", p))
                nc.tensor.transpose(aps[:, 3, 0:48], MF[:, 0, :], ident[0:48, 0:48]).then_inc(sem["mf_pe"], 1)

            def tq(p):
                free(p)
                wait(pe, ev("rq_done", p.of))
                c = p.of.of.c
                q_ = rows(RA)
                for h in range(4):
                    for m in range(2):
                        t = nc.tensor.transpose(aps[:, h // 2, (h % 2) * S + m * P:(h % 2) * S + m * P + P],
                                                q_[:, m, (4 * c + h) * P:(4 * c + h + 1) * P], ident[:])
                t.then_inc(sem["tq_pe"], 1)

            def tk(p):
                free(p)
                wait(pe, ev("rk_done", p.of))
                k_ = tiles(Yc[:, 0:2 * S], 2)
                for h in range(2):
                    for m in range(2):
                        t = nc.tensor.transpose(aps[:, 2, h * S + m * P:h * S + m * P + P], k_[:, m, h * P:(h + 1) * P],
                                                ident[:])
                t.then_inc(sem["tk_pe"], 1)

            def at(p):
                wait(pe, ev("tk_cp", p.tk), ev("tq_cp", p.rq))
                kv = p.h // (QH // KVH)
                for m in range(2):
                    wait(pe, p.bank_free[m])
                    q_ = qT[:, p.h * S + m * P:p.h * S + m * P + P]
                    if p.s == "x":
                        mm(aps[:, m, 0:S], q_, kvb[:, 2 * p.l, kv * S:(kv + 1) * S], start=True, stop=True)
                        t = mm(aps[:, m, S:2 * S], q_, kvb[:, 4, kv * S:(kv + 1) * S], start=True, stop=True)
                    else:
                        t = mm(aps[:, m, 0:S], q_, kvb[:, p.own, kv * S:(kv + 1) * S], start=True, stop=True)
                    t.then_inc(sem["at_s"], 1)

            def atT(p):
                free(p)
                a = p.of
                wait(pe, ev("at_pn", a, 2, 2))
                for kb in range(4 if a.s == "x" else 2):
                    for m in range(2):
                        t = nc.tensor.transpose(aps[:, 2 + kb // 2, (kb % 2) * S + m * P:(kb % 2) * S + m * P + P],
                                                Pb[:, m, kb * P:(kb + 1) * P], ident[:])
                t.then_inc(sem["at_tp"], 1)

            def atV(p):
                free(p)
                a = p.of
                wait(pe, ev("at_pt", a))
                kv = a.h // (QH // KVH)
                srcs = [2 * a.l + 1, 5] if a.s == "x" else [a.own + 1]
                n = 2 * len(srcs)
                for kb in range(n):
                    v = kvb[:, srcs[kb // 2], (kb % 2) * S + kv * P:(kb % 2) * S + kv * P + P]
                    t = mm(aps[:, 0, 0:S], v, PTb[:, kb * S:(kb + 1) * S], start=kb == 0, stop=kb == n - 1)
                t.then_inc(sem["at_pv"], 1)

            def spatial(p):
                wait(pe, ev("gn_done", p.of))
                g_ = rows(RA)
                for g in range(4):
                    wait(pe, p.bank_free[g])
                    for m in range(2):
                        t = mm(aps[:, g, m * S:(m + 1) * S], wsT[:, g, :], g_[:, m, g * S:(g + 1) * S], start=True, stop=True)
                    t.then_inc(sem["sp_pe"], 1)

            def ws_t(p):
                free(p)
                pe.wait_ge(sem["ws_in"], 16 * (p.n + 1))
                for g in range(4):
                    t = nc.tensor.transpose(aps[:, 3, g * P:(g + 1) * P], Pb[:, 0, g * P:(g + 1) * P], ident[:])
                t.then_inc(sem["ws_pe"], 1)

            def ln_sum(p, src, b):
                for k in range(KT):
                    t = mm(aps[:, b, 0:S], ones[:], src[:, k * S:(k + 1) * S], start=k == 0, stop=k == KT - 1)
                return t

            def ln_mu(p):
                free(p)
                wait(pe, ev("cv_done", None, 0, p.conv_after))
                ln_sum(p, Yc, 2).then_inc(sem["ln_mean"], 1)

            def ln_var(p):
                free(p)
                wait(pe, ev("ln_sq", p.of))
                ln_sum(p, RB, 3).then_inc(sem["ln_vs"], 1)

            stages = dict(pp_c=pp_c, pp=pp, toep=toep, T=T, ba=ba, baT=baT, baV=baV, y_norm=y_norm, ma=ma, maT=maT, maV=maV,
                          modfin=modfin, tq=tq, tk=tk, at=at, atT=atT, atV=atV, spatial=spatial, wsT=ws_t,
                          ln_mu=ln_mu, ln_var=ln_var)

            def unit(jb, q):
                pe.wait_ge(lo_done[q], jb.i + 1)
                wait(pe, *jb.ready.get(q, []))
                if q == 0 and jb.two_back:
                    wait(pe, jb.two_back.free)
                o = psum_job(jb)
                ks = jb.units[q]
                for i, k in enumerate(ks):
                    first, last = q == 0 and i == 0, q == NQ - 1 and i == len(ks) - 1
                    if jb.typ == "C":
                        mm(o[:, 0:NW], chi[:, k, :], whi[:, q, i, :], start=first, stop=False)
                        t = mm(o[:, 0:NW], chi[:, k, :], wlo[:, q, i, :], start=False, stop=last)
                    elif jb.typ == "A":
                        for m in range(2):
                            om = o[:, m * NW:(m + 1) * NW]
                            ah, al = ohi[:, jb.slot, k, m * P:(m + 1) * P], olo[:, jb.slot, k, m * P:(m + 1) * P]
                            mm(om, ah, whi[:, q, i, :], start=first, stop=False)
                            mm(om, ah, wlo[:, q, i, :], start=False, stop=False)
                            t = mm(om, al, whi[:, q, i, :], start=False, stop=last)
                    else:
                        for n in range(jb.cols // P):
                            on = o[:, n * S:(n + 1) * S]
                            wh, wl = whi[:, q, i, n * P:(n + 1) * P], wlo[:, q, i, n * P:(n + 1) * P]
                            mm(on, wh, ohi[:, jb.slot, k, :], start=first and n % 2 == 0, stop=False, skip_group_check=True)
                            mm(on, wh, olo[:, jb.slot, k, :], start=False, stop=False, skip_group_check=True)
                            t = mm(on, wl, ohi[:, jb.slot, k, :], start=False, stop=last, skip_group_check=True)
                t.then_inc(used[q], 1)

            for jb in jobs:
                for q in range(NQ):
                    for p in jb.aux[q]:
                        if p.kind in stages:
                            stages[p.kind](p)
                    unit(jb, q)

        @block.scalar
        def _(act):
            A_ = nc.scalar.activation
            steps = [0]

            def link(ins):
                steps[0] += 1
                ins.then_inc(sem["act_step"], 1)
                act.wait_ge(sem["act_step"], steps[0])

            def squares(src, junk, line, name):
                for m in range(2):
                    A_(junk[:, m, :], src[:, m, :], ACT.Square, accum_out=st[:, line, m:m + 1]).then_inc(sem[name], 1)

            def pn_stat(p):
                wait(act, *p.after["act"])
                squares(rows(res[p.res]), rows(flat[p.xn]), p.n % 2, "pn_ss")

            def final(p):
                wait(act, *p.after["act"])
                squares(rows(res["x"]), rows(RB), 4, "fin_ss")

            def po(p):
                wait(act, *p.after.get("act", []))
                wait(act, p.wait.free)
                squares(rows(RB), TT, 5, "po_ss")

            def T(p):
                if p.scale:
                    wait(act, ("pp_cols", None, 0, 1) if p.scale[0] == "C1" else ("mf_c", None, 0, MODS[p.scale[1:3]] + 1))
                for b in p.banks:
                    wait(act, ev("t_pe", p, 4, b + 1))
                    if p.scale:
                        for i in range(2):
                            k = 2 * b + i
                            t = A_(ohi[:, p.slot, k, :], aps[:, b, i * S:(i + 1) * S], ACT.Identity,
                                   scale=column(p.scale, k), bias=column(p.shift, k) if p.shift else 0.0)
                    else:
                        t = A_(ohi[:, p.slot, 2 * b:2 * b + 2, :], tiles(bank(b), 2), ACT.Copy, scale=p.imm)
                    t.then_inc(sem["t_hi"], t_step(p, b))

            def pp_c(p):
                act.wait_ge(sem["pp_pc"], 1)
                A_(csb[:, 0, :], aps[:, 3, 0:16], ACT.Tanh, scale=0.5).then_inc(sem["pp_th"], 1)

            def ba(p):
                d0 = 16 + (p.n % 2) * 16
                for hh in range(2):
                    wait(act, ev("ba_nm", p, 2, hh + 1))
                    for m in range(2):
                        x = Pb[:, hh, 0:P] if m == 0 else Pb[:, hh, P:3 * P]
                        t = A_(x, x, ACT.Exp, bias=den[:, d0 + 2 * hh + m:d0 + 2 * hh + m + 1],
                               accum_out=den[:, d0 + 4 + 2 * hh + m:d0 + 5 + 2 * hh + m])
                    t.then_inc(sem["ba_p"], 1)

            def baT(p):
                for hh in range(2):
                    wait(act, ev("ba_tp", p.of, 2, hh + 1))
                    if p.n:
                        act.wait_ge(sem["ba_pv"], p.n)
                    A_(PTb[:, hh * 2 * S:hh * 2 * S + 3 * P], aps[:, 2 + hh, 0:3 * P], ACT.Copy).then_inc(sem["ba_pt"], 1)

            def baV(p):
                wait(act, ev("ba_pv", p.of))
                A_(RB[:, p.of.g * S:(p.of.g + 1) * S], aps[:, 0, 0:S], ACT.Copy).then_inc(sem["ba_y"], 1)

            def y_norm(p):
                act.wait_ge(sem["ba_y"], 8)
                for half, sq in ((0, Pb[:, :, :].rearrange("p a b -> p (a b)")), (1, PTb[:])):
                    A_(sq, RB[:, half * 4 * S:(half + 1) * 4 * S], ACT.Square).then_inc(sem["yn_sq"], 1)
                for half in range(2):
                    act.wait_ge(sem["yn_y"], half + 1)
                    A_(ohi[:, p.slot, 4 * half:4 * half + 4, :], tiles(RB[:, half * 4 * S:(half + 1) * 4 * S], 4),
                       ACT.Copy).then_inc(sem["yn_hi"], 1)

            def ma(p):
                d0 = (p.n % 2) * 8
                wait(act, ev("ma_nm", p))
                if p.n:
                    act.wait_ge(sem["ma_tp"], p.n)
                for m in range(2):
                    t = A_(Pb[:, m, 0:S], aps[:, 0, m * S:(m + 1) * S], ACT.Exp, scale=HD_MEM ** -0.5,
                           bias=den[:, d0 + 2 + m:d0 + 3 + m], accum_out=den[:, d0 + 4 + m:d0 + 5 + m])
                t.then_inc(sem["ma_p"], 1)

            def maT(p):
                wait(act, ev("ma_tp", p.of))
                if p.n:
                    act.wait_ge(sem["ma_pv"], p.n)
                A_(PTb[:, 0:2 * S], bank(1), ACT.Copy).then_inc(sem["ma_pt"], 1)

            def maV(p):
                wait(act, ev("ma_pv", p.of))
                A_(ohi[:, p.of.slot, 2 * p.of.h:2 * p.of.h + 2, :], tiles(bank(2), 2), ACT.Copy).then_inc(sem["ma_hi"], 1)

            def wsT_(p):
                act.wait_ge(sem["ws_pe"], p.n + 1)
                A_(wsT[:, :, :], tiles(bank(3), 4), ACT.Copy).then_inc(sem["ws_cp"], 1)

            def tq(p):
                wait(act, ev("tq_pe", p))
                c = p.of.of.c
                A_(qT[:, c * 4 * S:(c + 1) * 4 * S], aps[:, 0:2, :].rearrange("p a b -> p (a b)"),
                   ACT.Copy).then_inc(sem["tq_cp"], 1)

            def tk(p):
                wait(act, ev("tk_pe", p))
                A_(kvb[:, p.own, :], bank(2), ACT.Copy).then_inc(sem["tk_cp"], 1)

            def at(p):
                d0 = (p.n % 2) * 8
                nk = 2 * S if p.s == "x" else S
                for m in range(2):
                    wait(act, ev("at_nb", p, 2, m + 1))
                    if p.n:
                        act.wait_ge(sem["at_tp"], p.n)
                    u = (p.h // 4) * 8 + m * 4 + p.h % 4
                    A_(Pb[:, m, 0:nk], aps[:, m, 0:nk], ACT.Exp, scale=st[:, 3, u:u + 1],
                       bias=den[:, d0 + 2 + m:d0 + 3 + m], accum_out=den[:, d0 + 4 + m:d0 + 5 + m]).then_inc(sem["at_p"], 1)

            def atT(p):
                nk = 4 * S if p.of.s == "x" else 2 * S
                wait(act, ev("at_tp", p.of))
                if p.n:
                    act.wait_ge(sem["at_pv"], p.n)
                A_(PTb[:, 0:nk], aps[:, 2:4, :].rearrange("p a b -> p (a b)")[:, 0:nk], ACT.Copy).then_inc(sem["at_pt"], 1)

            def atV(p):
                wait(act, ev("at_pv", p.of))
                A_(ohi[:, p.of.slot, p.of.h, :], aps[:, 0, 0:S], ACT.Copy).then_inc(sem["at_hi"], 1)

            def gv_norm(p):
                wait(act, ev("ge_out", p.gv[1]))
                squares(rows(RA), TT, 6, "gn_ss")

            def ln_mu(p):
                wait(act, ev("ln_d", p), p.rb_free)
                A_(RB[:], Yc[:], ACT.Square).then_inc(sem["ln_sq"], 1)

            def ln_out(p):
                wait(act, ev("ln_n", p.of))
                for k in range(KT):
                    y = Yc[:, k * S:(k + 1) * S]
                    t = A_(y, y, ACT.Identity, scale=C2[:, 44 * p.l + 16 + k:44 * p.l + 17 + k],
                           bias=C2[:, 44 * p.l + 24 + k:44 * p.l + 25 + k])
                link(t)
                A_(RB[:], Yc[:], ACT.Tanh, scale=0.5).then_inc(sem["ln_th"], 1)
                wait(act, ev("ln_r", p))
                A_(ohi[:, p.slot, :, :], tiles(RB[:], KT), ACT.Copy, scale=0.5).then_inc(sem["ln_hi"], 1)

            stages = dict(pn_stat=pn_stat, final=final, po=po, T=T, pp_c=pp_c, ba=ba, baT=baT, baV=baV, y_norm=y_norm, ma=ma,
                          maT=maT, maV=maV, wsT=wsT_, tq=tq, tk=tk, at=at, atT=atT, atV=atV, gv_norm=gv_norm, ln_mu=ln_mu,
                          ln_out=ln_out)

            def cp(jb, g):
                name, c = jb.dst
                if name == "cres":
                    t = A_(vm[:, :, c * NW:(c + 1) * NW], tiles(g, 2), ACT.Copy)
                elif name == "TT":
                    t = A_(TT[:, c, :], g, ACT.Copy)
                else:
                    t = A_(flat[name][:, c * 2 * NW:(c + 1) * 2 * NW], g, ACT.Copy)
                t.then_inc(sem["cp_done"], 1)

            def q_rows(jb, g):
                if jb.po_before:
                    act.wait_ge(sem["po_ss"], 2 * jb.po_before)
                A_(rows(RA)[:, :, jb.c * NW:(jb.c + 1) * NW], tiles(g, 2), ACT.Copy)
                A_(TT[:, 0, :], g, ACT.Square).then_inc(sem["q_cp"], 1)

            def kv_rows(jb, g):
                gt = tiles(g, 2)
                A_(tiles(Yc[:, 0:2 * S], 2), gt[:, :, 0:S], ACT.Copy)
                A_(tiles(kvb[:, jb.own + 1, :], 2), gt[:, :, S:2 * S], ACT.Copy)
                A_(tiles(Yc[:, 2 * S:4 * S], 2), gt[:, :, 0:S], ACT.Square).then_inc(sem["kv_cp"], 1)

            def gelu(jb, g):
                A_(TT[:, 0, :], g, ACT.Square).then_inc(sem["ge_sq"], 1)
                wait(act, ev("ge_z", jb))
                A_(TT[:, 1, :], TT[:, 0, :], ACT.Tanh).then_inc(sem["ge_t"], 1)

            def glu_a(jb, g):
                A_(AB[:], g, ACT.Copy).then_inc(sem["gl_a"], 1)

            def glu_g(jb, g):
                A_(TT[:, 1, :], g, ACT.Tanh, scale=0.5).then_inc(sem["gl_th"], 1)

            def gate(jb, g):
                A_(AB[:] if jb.n % 2 == 0 else TT[:, 1, :], g, ACT.Tanh, scale=0.5).then_inc(sem["ga_th"], 1)

            def relu2(jb, g):
                t_ = TT[:, jb.n % 2, :]
                if jb.n:
                    act.wait_ge(sem["r2_lo"], jb.n - 1) if jb.n > 1 else None
                A_(t_, g, ACT.Relu).then_inc(sem["r2_relu"], 1)
                wait(act, ev("r2_sq", jb))
                k = (jb.c % 2) * 4
                A_(ohi[:, jb.out, k:k + 4, :], tiles(t_, 4), ACT.Copy).then_inc(sem["r2_hi"], 1)

            def acc0(jb, g):
                A_(rows(RB)[:, :, jb.j * NW:(jb.j + 1) * NW], tiles(g, 2), ACT.Copy).then_inc(sem["ac_cp"], 1)

            def ycp(jb, g):
                A_(rows(RB)[:, :, jb.j * NW:(jb.j + 1) * NW], tiles(g, 2), ACT.Copy).then_inc(sem["y_cp"], 1)

            def cgate(jb, g):
                n = jb.cols // P
                if jb.n:
                    act.wait_ge(sem["cg_s"], jb.n)
                A_(GLP[:, 0:n, PAD2:PAD2 + S], tiles(g[:, 0:n * S], n), ACT.Copy).then_inc(sem["cg_cp"], 1)
                wait(act, ev("cg_v", jb))
                A_(TT[:, 1, 0:n * S], Yc[:, 0:n * S], ACT.Tanh, scale=0.5).then_inc(sem["cg_t"], 1)

            def up(jb, g):
                n = jb.cols // P
                wait(act, ev("up_mul", jb))
                k = (jb.c % 2) * 4
                A_(ohi[:, jb.out, k:k + n, :], tiles(TT[:, 0, 0:n * S], n), ACT.Copy, scale=0.5).then_inc(sem["up_hi"], 1)

            def ada(jb, g):
                if jb.n:
                    act.wait_ge(sem["ad_st"], 16 * jb.n)
                A_(stage[:], g[0:4, 0:NW], ACT.Copy).then_inc(sem["ad_cp"], 1)

            evacs = dict(cp=cp, q=q_rows, kv=kv_rows, gelu=gelu, glu_a=glu_a, glu_g=glu_g, gate=gate, relu2=relu2, acc0=acc0,
                         ycp=ycp, cgate=cgate, up=up, ada=ada)

            def split(jb, q):
                act.wait_ge(loaded[q], 16 * (jb.i + 1))
                if jb.i:
                    act.wait_ge(used[q], jb.i)
                A_(part(whi, jb, q), part(raw, jb, q), ACT.Copy).then_inc(hi_done[q], 1)

            for q in range(NQ):
                split(jobs[0], q)
            for jb in jobs + [None]:
                if jb is None:
                    po(tail[0])
                    break
                nxt = jobs[jb.i + 1] if jb.i + 1 < len(jobs) else None
                for q in range(NQ):
                    for p in jb.aux[q]:
                        if p.kind in stages:
                            stages[p.kind](p)
                    if q == NQ - 1 and jb.evac in evacs:
                        act.wait_ge(used[NQ - 1], jb.i + 1)
                        wait(act, *jb.after.get("act", []))
                        evacs[jb.evac](jb, psum_job(jb))
                    if nxt:
                        split(nxt, q)

        @block.vector
        def _(dve):
            tt, ts, stt = nc.vector.tensor_tensor, nc.vector.tensor_scalar, nc.vector.scalar_tensor_tensor
            steps = [0]
            conv_ops = [0]

            def link(ins):
                steps[0] += 1
                ins.then_inc(sem["dve_step"], 1)
                dve.wait_ge(sem["dve_step"], steps[0])

            def f32(x):
                return x.bitcast(F32)

            def rsqrt(y, x, t):
                link(ts(t.bitcast(I32), x.bitcast(I32), 1, None, ALU.logical_shift_right))
                link(ts(y.bitcast(I32), t.bitcast(I32), -1.0, MAGIC, ALU.mult, ALU.add))
                for _ in range(3):
                    link(tt(t, y, y, ALU.mult))
                    link(stt(t, t, -0.5, x, ALU.mult, ALU.mult))
                    link(stt(y, t, 1.5, y, ALU.add, ALU.mult))

            def rms(line, n, scale, out_scale=None):
                a = st[:, line, 0:n]
                w = st[:, 7 + line, :]
                link(ts(a, a, scale, EPS, ALU.mult, ALU.add))
                rsqrt(w[:, 0:n], a, w[:, 8:8 + n])
                if out_scale:
                    link(ts(w[:, 0:n], w[:, 0:n], out_scale, None, ALU.mult))
                return w

            def pn_stat(p):
                wait(dve, *p.after["dve"])
                wait(dve, ev("pn_ss", p, 2, 2))
                w = rms(p.n % 2, 2, 1.0 / D)
                x, y = rows(res[p.res]), rows(flat[p.xn])
                for m in range(2):
                    t = ts(y[:, m, :], x[:, m, :], w[:, m:m + 1], None, ALU.mult)
                t.then_inc(sem["pn_xn"], 1)

            def final(p):
                wait(dve, *p.after["dve"])
                dve.wait_ge(sem["fin_ss"], 2)
                w = rms(4, 2, 1.0 / D)
                dve.wait_ge(sem["gb_in"], 16 * p.gb)
                x = rows(res["x"])
                for m in range(2):
                    t = stt(x[:, m, :], x[:, m, :], w[:, m:m + 1], GB[:], ALU.mult, ALU.mult)
                t.then_inc(sem["fin_x"], 1)

            def po(p):
                wait(dve, ev("po_ss", p, 2, 2))
                wait(dve, p.wait.free)
                w = rms(5, 2, 1.0 / D)
                dve.wait_ge(sem["gb_in"], 16 * p.gb)
                x, y = rows(res[p.res]), rows(RB)
                for m in range(2):
                    t = stt(y[:, m, :], y[:, m, :], w[:, m:m + 1], GB[:], ALU.mult, ALU.mult)
                link(t)
                if p.n and p.res == "x":
                    dve.wait_ge(sem["po_x"], p.n)
                for m in range(2):
                    t = tt(x[:, m, :], x[:, m, :], y[:, m, :], ALU.add)
                t.then_inc(sem["po_x"], 1)

            def T(p):
                if p.scale:
                    wait(dve, ("pp_cols", None, 0, 1) if p.scale[0] == "C1" else ("mf_c", None, 0, MODS[p.scale[1:3]] + 1))
                for b in p.banks:
                    wait(dve, ev("t_hi", p, 4, b + 1))
                    o = olo[:, p.slot, 2 * b:2 * b + 2, :]
                    if p.shift:
                        for i in range(2):
                            k = 2 * b + i
                            t = ts(aps[:, b, i * S:(i + 1) * S], aps[:, b, i * S:(i + 1) * S], column(p.scale, k),
                                   column(p.shift, k), ALU.mult, ALU.add)
                        link(t)
                        t = tt(o, tiles(bank(b), 2), f32(ohi[:, p.slot, 2 * b:2 * b + 2, :]), ALU.subtract)
                    elif p.scale:
                        for i in range(2):
                            k = 2 * b + i
                            t = stt(olo[:, p.slot, k, :], aps[:, b, i * S:(i + 1) * S], column(p.scale, k),
                                    f32(ohi[:, p.slot, k, :]), ALU.mult, ALU.subtract)
                    else:
                        t = stt(o, tiles(bank(b), 2), p.imm, f32(ohi[:, p.slot, 2 * b:2 * b + 2, :]), ALU.mult, ALU.subtract)
                    t.then_inc(sem["t_lo"], t_step(p, b))

            def pp_c(p):
                link(nc.vector.memset(chi[:, :, :].rearrange("p a b -> p (a b)").bitcast(F32), 0.0))
                dve.wait_ge(sem["pp_th"], 1)
                link(stt(csb[:, 1, :], csb[:, 0, :], 1.0, aps[:, 3, 0:16], ALU.add, ALU.mult))
                link(ts(csb[:, 1, :], csb[:, 1, :], 0.5, None, ALU.mult))
                c = csb[:, 1, :].rearrange("p (v k) -> p k v", v=2)
                link(nc.vector.tensor_copy(chi[:, :, 0:2], c))
                tt(chi[:, :, 2:4], c, f32(chi[:, :, 0:2]), ALU.subtract).then_inc(sem["pp_c4"], 1)

            def pp(p):
                dve.wait_ge(sem["pp_pe"], 1)
                nc.vector.tensor_copy(C1[:], aps[:, 0, 0:P])
                nc.vector.tensor_copy(C2[:], aps[:, 0, P:P + 88])
                for l in range(LAYERS):
                    t = ts(CW[:, l, :], aps[:, 1 + l, 0:TAPS2 * KT], 0.5, None, ALU.mult)
                t.then_inc(sem["pp_cols"], 1)

            def toep(p):
                dve.wait_ge(sem["tp_pe"], 1)
                tt(TR, aps[0:HEADS1, 3, 0:384], MSK, ALU.add).then_inc(sem["tp_r"], 1)

            def ba(p):
                d0 = 16 + (p.n % 2) * 16
                g = p.g // 2
                for hh in range(2):
                    wait(dve, ev("ba_s", p, 2, hh + 1))
                    dve.wait_ge(sem[f"bias_in{g % 2}"], 16 * (g // 2 + 1))
                    if p.n:
                        dve.wait_ge(sem["ba_tp"], 2 * p.n)
                    b = bias[:, g % 2, 2 * (p.g % 2) + hh, :]
                    stt(Pb[:, hh, 0:P], aps[:, hh, 0:P], HD1 ** -0.5, b[:, 0:P][:, ::-1], ALU.mult, ALU.add)
                    t = stt(Pb[:, hh, P:3 * P], aps[:, hh, P:3 * P], HD1 ** -0.5, b[:, ::-1], ALU.mult, ALU.add)
                    t.then_inc(sem["ba_sb"], 1)
                    wait(dve, ev("ba_sb", p, 2, hh + 1))
                    for m in range(2):
                        x = Pb[:, hh, 0:P] if m == 0 else Pb[:, hh, P:3 * P]
                        t = nc.vector.tensor_reduce(den[:, d0 + 2 * hh + m:d0 + 2 * hh + m + 1], x, AX.X, ALU.max, negate=True)
                    t.then_inc(sem["ba_nm"], 1)
                for hh in range(2):
                    wait(dve, ev("ba_p", p, 2, hh + 1))
                    e = d0 + 8 + 2 * hh
                    link(nc.vector.reciprocal(den[:, e:e + 2], den[:, e - 4:e - 2]))
                    for m in range(2):
                        x = Pb[:, hh, 0:P] if m == 0 else Pb[:, hh, P:3 * P]
                        t = ts(x, x, den[:, e + m:e + m + 1], None, ALU.mult)
                    t.then_inc(sem["ba_pn"], 1)

            def y_norm(p):
                rs, x, t_ = GB[:, 0:S], GB[:, S:2 * S], GB[:, 2 * S:3 * S]
                for half in range(2):
                    dve.wait_ge(sem["yn_ss"], half + 1)
                    link(ts(x, aps[:, 2 + half, 0:S], 2.0, EPS, ALU.mult, ALU.add))
                    rsqrt(rs, x, t_)
                    for k in range(4 * half, 4 * half + 4):
                        y = RB[:, k * S:(k + 1) * S]
                        t = stt(y, y, C1[:, 16 + k:17 + k], rs, ALU.mult, ALU.mult)
                    t.then_inc(sem["yn_y"], 1)
                for half in range(2):
                    dve.wait_ge(sem["yn_hi"], half + 1)
                    k = slice(4 * half, 4 * half + 4)
                    tt(olo[:, p.slot, k, :], tiles(RB[:, half * 4 * S:(half + 1) * 4 * S], 4), f32(ohi[:, p.slot, k, :]),
                       ALU.subtract).then_inc(sem["yn_lo"], 1)

            def ma(p):
                d0 = (p.n % 2) * 8
                wait(dve, ev("ma_s", p))
                link(nc.vector.tensor_reduce(den[:, d0:d0 + 2], tiles(bank(0), 2), AX.X, ALU.max, negate=True))
                ts(den[:, d0 + 2:d0 + 4], den[:, d0:d0 + 2], HD_MEM ** -0.5, None, ALU.mult).then_inc(sem["ma_nm"], 1)
                wait(dve, ev("ma_p", p))
                link(nc.vector.reciprocal(den[:, d0 + 6:d0 + 8], den[:, d0 + 4:d0 + 6]))
                for m in range(2):
                    t = ts(Pb[:, m, 0:S], Pb[:, m, 0:S], den[:, d0 + 6 + m:d0 + 7 + m], None, ALU.mult)
                t.then_inc(sem["ma_pn"], 1)

            def maV(p):
                wait(dve, ev("ma_hi", p.of))
                k = slice(2 * p.of.h, 2 * p.of.h + 2)
                tt(olo[:, p.of.slot, k, :], tiles(bank(2), 2), f32(ohi[:, p.of.slot, k, :]),
                   ALU.subtract).then_inc(sem["ma_lo"], 1)

            def modfin(p):
                i = MODS[p.l, p.s]
                dve.wait_ge(sem["mf_in"], 80 * (p.n + 1))
                link(tt(MF[:, 0, :], MF[:, 0, :], MF[:, 1, :], ALU.add))
                tt(MF[:, 0, :], MF[:, 0, :], MF[:, 2, :], ALU.add).then_inc(sem["mf_sum"], 1)
                wait(dve, ev("mf_pe", p), ev("mf_sum", p))
                link(nc.vector.tensor_copy(modc[:, i, :], aps[:, 3, 0:48]))
                for which in range(2):
                    t = stt(gsc[:, i, 8 * which:8 * which + 8], modc[:, i, 8 + 24 * which:16 + 24 * which], 1.0,
                            C2[:, 44 * p.l + 8 * which:44 * p.l + 8 * which + 8], ALU.add, ALU.mult)
                t.then_inc(sem["mf_c"], 1)
                tt(MF[:, 3, :], MF[:, 3, :], MF[:, 0, :], ALU.mult).then_inc(sem["mf_r"], 1)

            def tab(p):
                if p.s == "x":
                    dve.wait_ge(sem["gqk_in"], 32 * (p.n + 1))
                    dve.wait_ge(sem["cst_in"], 32)
                    T4 = AB[:].rearrange("p (t m d) -> p t m d", t=4, m=2)
                    h = HD2 // 2
                    for j in range(2):
                        for m in range(2):
                            tt(T4[:, 2 * j, m, :], cos2[:, m, :], GQK[:, j, :], ALU.mult)
                            tt(T4[:, 2 * j + 1, m, 0:h], sinpm[:, m, 0:h], GQK[:, j, h:HD2], ALU.mult)
                            t = tt(T4[:, 2 * j + 1, m, h:HD2], sinpm[:, m, h:HD2], GQK[:, j, 0:h], ALU.mult)
                    link(t)

            def turn(x, nh, j, p, t1, t2):
                h = HD2 // 2
                for m in range(2):
                    xm = x[:, m, :].rearrange("p (h d) -> p h d", d=HD2)
                    if p.s == "c":
                        g = GQK[:, j, :].unsqueeze(1).to_broadcast([P, nh, HD2])
                        t = tt(xm, xm, g, ALU.mult)
                        continue
                    T4 = AB[:].rearrange("p (t m d) -> p t m d", t=4, m=2)
                    a, b = t1[:, m, :].rearrange("p (h d) -> p h d", d=HD2), t2[:, m, :].rearrange("p (h d) -> p h d", d=HD2)
                    cc = T4[:, 2 * j, m, :].unsqueeze(1).to_broadcast([P, nh, HD2])
                    s0 = T4[:, 2 * j + 1, m, 0:h].unsqueeze(1).to_broadcast([P, nh, h])
                    s1 = T4[:, 2 * j + 1, m, h:HD2].unsqueeze(1).to_broadcast([P, nh, h])
                    tt(a, xm, cc, ALU.mult)
                    tt(b[:, :, 0:h], xm[:, :, h:HD2], s0, ALU.mult)
                    t = tt(b[:, :, h:HD2], xm[:, :, 0:h], s1, ALU.mult)
                if p.s == "x":
                    link(t)
                    t = tt(x, t1, t2, ALU.add)
                return t

            def rq(p):
                c = p.of.c
                wait(dve, ev("q_cp", p.of))
                dve.wait_ge(sem["gqk_in"], 32 * (p.tab.n + 1))
                link(nc.vector.tensor_reduce(st[:, 2, 0:8], TT[:, 0, :].rearrange("p (u d) -> p u d", d=HD2), AX.X, ALU.add))
                w = rms(2, 8, 1.0 / HD2)
                ts(st[:, 3, 8 * c:8 * c + 8], w[:, 0:8], HD2 ** -0.5, None, ALU.mult)
                x = rows(RA)[:, :, c * NW:(c + 1) * NW]
                turn(x, 4, 0, p, tiles(TT[:, 0, :], 2), tiles(TT[:, 1, :], 2)).then_inc(sem["rq_done"], 1)

            def rk(p):
                wait(dve, ev("kv_cp", p.of))
                dve.wait_ge(sem["gqk_in"], 32 * (p.tab.n + 1))
                k_ = Yc[:, 0:2 * S]
                link(nc.vector.tensor_reduce(st[:, 2, 0:4], Yc[:, 2 * S:4 * S].rearrange("p (u d) -> p u d", d=HD2),
                                             AX.X, ALU.add))
                w = rms(2, 4, 1.0 / HD2)
                ku = k_.rearrange("p (u d) -> p u d", d=HD2)
                link(tt(ku, ku, w[:, 0:4].unsqueeze(2).to_broadcast([P, 4, HD2]), ALU.mult))
                turn(tiles(k_, 2), 2, 1, p, tiles(Yc[:, 4 * S:6 * S], 2), tiles(Yc[:, 6 * S:8 * S], 2)).then_inc(sem["rk_done"], 1)

            def at(p):
                d0 = (p.n % 2) * 8
                nk = 2 * S if p.s == "x" else S
                for m in range(2):
                    u = (p.h // 4) * 8 + m * 4 + p.h % 4
                    wait(dve, ev("at_s", p, 2, m + 1))
                    link(nc.vector.tensor_reduce(den[:, d0 + m:d0 + m + 1], aps[:, m, 0:nk], AX.X, ALU.max, negate=True))
                    tt(den[:, d0 + 2 + m:d0 + 3 + m], den[:, d0 + m:d0 + m + 1], st[:, 3, u:u + 1],
                       ALU.mult).then_inc(sem["at_nb"], 1)
                for m in range(2):
                    wait(dve, ev("at_p", p, 2, m + 1))
                    link(nc.vector.reciprocal(den[:, d0 + 6 + m:d0 + 7 + m], den[:, d0 + 4 + m:d0 + 5 + m]))
                    ts(Pb[:, m, 0:nk], Pb[:, m, 0:nk], den[:, d0 + 6 + m:d0 + 7 + m], None, ALU.mult).then_inc(sem["at_pn"], 1)

            def atV(p):
                wait(dve, ev("at_hi", p.of))
                tt(olo[:, p.of.slot, p.of.h, :], aps[:, 0, 0:S], f32(ohi[:, p.of.slot, p.of.h, :]),
                   ALU.subtract).then_inc(sem["at_lo"], 1)

            def gv_norm(p):
                wait(dve, ev("gn_ss", p, 2, 2))
                w = rms(6, 2, 0.25 / D, 0.5)
                dve.wait_ge(sem["gb_in"], 16 * p.gb)
                x = rows(RA)
                for m in range(2):
                    t = stt(x[:, m, :], x[:, m, :], w[:, m:m + 1], GB[:], ALU.mult, ALU.mult)
                t.then_inc(sem["gn_done"], 1)

            def spatial(p):
                wait(dve, ev("ge_out", p.gu[1]))
                x = rows(RB)
                for g in range(4):
                    wait(dve, ev("sp_pe", p, 4, g + 1))
                    xg = x[:, :, g * S:(g + 1) * S]
                    t = stt(xg, tiles(bank(g), 2), C2[:, 44 * p.l + 40 + g:44 * p.l + 41 + g], xg, ALU.add, ALU.mult)
                t.then_inc(sem["sp_done"], 1)

            def conv(p):
                for tap in p.taps:
                    if tap == 0:
                        wait(dve, ev("gl_o", p.job), ev("tk_pe", p.tk))
                    for i in range(4):
                        k = 4 * p.half + i
                        y, x = Yc[:, k * S:(k + 1) * S], GLP[:, i, tap:tap + S]
                        w = CW[:, p.l, tap * KT + k:tap * KT + k + 1]
                        if tap == 0:
                            t = ts(y, x, w, C2[:, 44 * p.l + 32 + k:44 * p.l + 33 + k], ALU.mult, ALU.add)
                        else:
                            dve.wait_ge(sem["cv_done"], conv_ops[0] - 3)
                            t = stt(y, x, w, y, ALU.mult, ALU.add)
                        t.then_inc(sem["cv_done"], 1)
                        conv_ops[0] += 1

            def ln_mu(p):
                wait(dve, ev("ln_mean", p))
                y = tiles(Yc[:], KT)
                tt(y, y, aps[:, 2, 0:S].unsqueeze(1).to_broadcast([P, KT, S]), ALU.subtract).then_inc(sem["ln_d"], 1)

            def ln_var(p):
                wait(dve, ev("ln_vs", p))
                x, r, t_ = TT[:, 0, 0:S], TT[:, 0, S:2 * S], TT[:, 0, 2 * S:3 * S]
                link(ts(x, aps[:, 3, 0:S], EPS, None, ALU.add))
                rsqrt(r, x, t_)
                y = tiles(Yc[:], KT)
                tt(y, y, r.unsqueeze(1).to_broadcast([P, KT, S]), ALU.mult).then_inc(sem["ln_n"], 1)

            def ln_out(p):
                wait(dve, ev("ln_th", p))
                stt(RB[:], RB[:], 1.0, Yc[:], ALU.add, ALU.mult).then_inc(sem["ln_r"], 1)
                wait(dve, ev("ln_hi", p))
                stt(olo[:, p.slot, :, :], tiles(RB[:], KT), 0.5, f32(ohi[:, p.slot, :, :]), ALU.mult,
                    ALU.subtract).then_inc(sem["ln_lo"], 1)

            stages = dict(pn_stat=pn_stat, final=final, po=po, T=T, pp_c=pp_c, pp=pp, toep=toep, ba=ba, y_norm=y_norm, ma=ma,
                          maV=maV, modfin=modfin, tab=tab, rq=rq, rk=rk, at=at, atV=atV, gv_norm=gv_norm, spatial=spatial,
                          conv=conv, ln_mu=ln_mu, ln_var=ln_var, ln_out=ln_out)

            def res_add(jb, g):
                dve.wait_ge(used[NQ - 1], jb.i + 1)
                x = rows(res[jb.res])[:, :, jb.n0:jb.n0 + NW]
                if jb.n:
                    dve.wait_ge(sem["res_done"], jb.n)
                tt(x, x, tiles(g, 2), ALU.add).then_inc(sem["res_done"], 1)

            def gelu(jb, g):
                t0 = TT[:, 0, :]
                wait(dve, ev("ge_sq", jb))
                link(ts(t0, t0, GELU_A * GELU_B, GELU_A, ALU.mult, ALU.add))
                tt(t0, t0, g, ALU.mult).then_inc(sem["ge_z"], 1)
                wait(dve, ev("ge_t", jb))
                stt(rows(flat[jb.dst[0]])[:, :, jb.dst[1] * NW:(jb.dst[1] + 1) * NW], tiles(TT[:, 1, :], 2), 1.0, tiles(g, 2),
                    ALU.add, ALU.mult).then_inc(sem["ge_out"], 1)

            def glu_g(jb, g):
                wait(dve, ev("gl_th", jb), ev("gl_a", jb.of))
                stt(GLP[:, :, PAD2:PAD2 + S], tiles(TT[:, 1, :], 4), 1.0, tiles(AB[:], 4), ALU.add,
                    ALU.mult).then_inc(sem["gl_o"], 1)

            def branch(jb, g):
                dve.wait_ge(used[NQ - 1], jb.i + 1)
                wait(dve, ev("ga_th", jb.gate))
                gt = tiles(AB[:] if jb.gate.n % 2 == 0 else TT[:, 1, :], 2)
                x = rows(RA)[:, :, jb.j * NW:(jb.j + 1) * NW]
                if jb.first:
                    stt(x, gt, 1.0, tiles(g, 2), ALU.add, ALU.mult).then_inc(sem["br_out"], 1)
                else:
                    link(stt(tiles(TT[:, 0, :], 2), gt, 1.0, tiles(g, 2), ALU.add, ALU.mult))
                    dve.wait_ge(sem["br_out"], jb.n)
                    tt(x, x, tiles(TT[:, 0, :], 2), ALU.add).then_inc(sem["br_out"], 1)

            def relu2(jb, g):
                t_ = TT[:, jb.n % 2, :]
                wait(dve, ev("r2_relu", jb))
                tt(t_, t_, t_, ALU.mult).then_inc(sem["r2_sq"], 1)
                wait(dve, ev("r2_hi", jb), ev("r2_sq", jb))
                k = (jb.c % 2) * 4
                tt(olo[:, jb.out, k:k + 4, :], tiles(t_, 4), f32(ohi[:, jb.out, k:k + 4, :]), ALU.subtract).then_inc(sem["r2_lo"], 1)

            def acc(jb, g):
                dve.wait_ge(used[NQ - 1], jb.i + 1)
                wait(dve, ("ac_cp", jb.first_of, 1, 1))
                if jb.n:
                    dve.wait_ge(sem["ac_add"], jb.n)
                y = rows(RB)[:, :, jb.j * NW:(jb.j + 1) * NW]
                tt(y, y, tiles(g, 2), ALU.add).then_inc(sem["ac_add"], 1)

            def cgate(jb, g):
                n = jb.cols // P
                wait(dve, ev("cg_cp", jb))
                for tap in (2, 1, 0):
                    for i in range(n):
                        k = 4 * jb.c + i
                        y, x = Yc[:, i * S:(i + 1) * S], GLP[:, i, PAD2 - 2 + tap:PAD2 - 2 + tap + S]
                        w = C1[:, 62 + tap * NT1 + k:63 + tap * NT1 + k]
                        if tap == 2:
                            t = ts(y, x, w, C1[:, 40 + k:41 + k], ALU.mult, ALU.add)
                        else:
                            t = stt(y, x, w, y, ALU.mult, ALU.add)
                        if tap and i == n - 1:
                            link(t)
                t.then_inc(sem["cg_v"], 1)
                wait(dve, ev("cg_t", jb), ev("cg_v", jb))
                stt(AB[:, 0:n * S], TT[:, 1, 0:n * S], 1.0, Yc[:, 0:n * S], ALU.add, ALU.mult).then_inc(sem["cg_s"], 1)

            def up(jb, g):
                n = jb.cols // P
                dve.wait_ge(used[NQ - 1], jb.i + 1)
                wait(dve, ev("cg_s", jb.gate))
                t0 = TT[:, 0, 0:n * S]
                tt(t0, AB[:, 0:n * S], g[:, 0:n * S], ALU.mult).then_inc(sem["up_mul"], 1)
                wait(dve, ev("up_hi", jb), ev("up_mul", jb))
                k = (jb.c % 2) * 4
                stt(olo[:, jb.out, k:k + n, :], tiles(t0, n), 0.5, f32(ohi[:, jb.out, k:k + n, :]), ALU.mult,
                    ALU.subtract).then_inc(sem["up_lo"], 1)

            evacs = dict(res=res_add, gelu=gelu, glu_g=glu_g, branch=branch, relu2=relu2, acc=acc, cgate=cgate, up=up)

            def split(jb, q):
                dve.wait_ge(hi_done[q], jb.i + 1)
                tt(part(wlo, jb, q), part(raw, jb, q), f32(part(whi, jb, q)), ALU.subtract).then_inc(lo_done[q], 1)

            link(nc.vector.memset(GLP[:, :, :].rearrange("p a b -> p (a b)"), 0.0))
            link(nc.vector.memset(MF[:, :, :].rearrange("p a b -> p (a b)"), 1.0))
            for q in range(NQ):
                split(jobs[0], q)
            for jb in jobs + [None]:
                if jb is None:
                    po(tail[0])
                    break
                nxt = jobs[jb.i + 1] if jb.i + 1 < len(jobs) else None
                for q in range(NQ):
                    for p in jb.aux[q]:
                        if p.kind in stages:
                            stages[p.kind](p)
                    if q == NQ - 1 and jb.evac in evacs:
                        wait(dve, *jb.after.get("dve", []))
                        evacs[jb.evac](jb, psum_job(jb))
                    if nxt:
                        split(nxt, q)


FIRST = ["x", "mem", "w_in", "g_mix", "g_out_dil", "g_out_moba", "w_out", "rel_bias", "g_cross", "g_mem", "w_q_mem", "w_kv_mem",
         "w_o_mem", "g_ffn", "w_gate", "w_up", "conv_w", "conv_b", "w_down", "g_final"]
SECOND = ["c_2", "ctx_2", "c_ctx_2", "ada_w_2", "ada_b_2", "mix_pre_g_2", "mix_post_g_2", "w_in_2", "q_norm_g_2", "k_norm_g_2",
          "w_attn_o_2", "gmlp_norm_g_2", "gmlp_ws_2", "gmlp_bs_2", "w_gmlp_o_2", "conv_w_2", "conv_b_2", "conv_norm_g_2",
          "conv_norm_b_2", "w_conv_o_2", "w_out_2", "ffn_pre_g_2", "ffn_post_g_2", "w_ff1_2", "w_ff2_2"]


def views(t):
    A = {k: t[k] for k in ("rel_bias", "g_final", "onehot", "mask", "cos2", "sinpm")}
    for k in ("x", "mem", "w_in", "g_mix", "g_out_dil", "g_out_moba", "w_out", "g_cross", "g_mem", "g_ffn", "w_gate", "w_up",
              "conv_w", "conv_b", "w_down"):
        A[k] = t[k][0]
    A["w_q"], A["w_kv"], A["w_o"] = t["w_q_mem"][0], t["w_kv_mem"][0], t["w_o_mem"][0]
    A["c"], A["ctx"], A["c_ctx"] = t["c_2"], t["ctx_2"][0], t["c_ctx_2"]
    for k in ("ada_b", "mix_pre_g", "mix_post_g", "q_norm_g", "k_norm_g", "gmlp_norm_g", "gmlp_ws", "gmlp_bs", "conv_norm_g",
              "conv_norm_b", "ffn_pre_g", "ffn_post_g"):
        A[k] = t[k + "_2"]
    A["conv_w_2"], A["conv_b_2"] = t["conv_w_2"], t["conv_b_2"]
    for l in range(LAYERS):
        for k, name in (("ada", "ada_w_2"), ("win", "w_in_2"), ("attn", "w_attn_o_2"), ("gmlp", "w_gmlp_o_2"),
                        ("conv", "w_conv_o_2"), ("out", "w_out_2"), ("ff1", "w_ff1_2"), ("ff2", "w_ff2_2")):
            A[f"{k}{l}"] = t[name][l]
    return A


def kernel(**inputs):
    import concourse.bacc as bacc
    from concourse.bass_utils import run_bass_kernel_spmd

    nc = bacc.Bacc("TRN2", target_bir_lowering=False, num_devices=1)
    arrays = {k: np.ascontiguousarray(inputs[k]) for k in FIRST + SECOND}
    arrays["onehot"], arrays["mask"] = toeplitz_constants()
    arrays["cos2"], arrays["sinpm"] = rope_constants()
    t = {k: nc.dram_tensor(k, a.shape, mybir.dt.from_np(a.dtype), kind="ExternalInput").ap() for k, a in arrays.items()}
    out = nc.dram_tensor("out", (1, S, D), F32, kind="ExternalOutput").ap()
    build(nc, views(t), out)
    return run_bass_kernel_spmd(nc, [arrays], core_ids=[0]).results[0]["out"]
```

```python
import math
from contextlib import ExitStack

import numpy as np
import concourse.bass as bass
from concourse import mybir

F32 = mybir.dt.float32
F32R = mybir.dt.float32r
I32 = mybir.dt.int32
ALU = mybir.AluOpType
ACT = mybir.ActivationFunctionType
AX = mybir.AxisListType

P = 128
S = 256
D = 1024
KT = D // P
NQ = 4
NW = 512
EPS = 1e-6
NEG = -1e30
MAGIC = 1597463007.0

N_BUCKETS, MAX_DISTANCE = 32, 2048
HEADS1, HD1 = 16, 64
FF1 = 2816
NT1 = FF1 // P
HEADS_MEM, HD_MEM = 4, 256
GRID_W, ROPE_THETA = 64, 10000.0
HD2, QH, KVH = 128, 8, 2
Q_OFF, K_OFF = 0, 1024
GU_OFF, GV_OFF, CG_OFF, GATE_OFF = 1536, 2560, 3584, 5632
TAPS2, PAD2 = 31, 15
GELU_A, GELU_B = 0.7978845608028654, 0.044715
LAYERS = 2


class Step:

    def __init__(self, kind, after=None, **args):
        self.kind, self.after = kind, after or {}
        self.of = args.get("of")
        self.l, self.s, self.h, self.g = args.get("l"), args.get("s"), args.get("h"), args.get("g")
        self.c, self.j, self.half = args.get("c"), args.get("j"), args.get("half")
        self.res, self.xn, self.src, self.dst = args.get("res"), args.get("xn"), args.get("src"), args.get("dst")
        self.slot, self.own, self.out = args.get("slot"), args.get("own"), args.get("out")
        self.scale, self.shift, self.imm, self.banks = (args.get(k) for k in ("scale", "shift", "imm", "banks"))
        self.ready, self.wait, self.tab, self.tk = (args.get(k) for k in ("ready", "wait", "tab", "tk"))
        self.rq, self.rk, self.gv, self.gu = (args.get(k) for k in ("rq", "rk", "gv", "gu"))
        self.job, self.taps, self.rb_free = (args.get(k) for k in ("job", "taps", "rb_free"))
        self.tap, self.last = args.get("tap"), args.get("last")
        self.po = args.get("po")
        self.then = []
        self.gate, self.first = args.get("gate"), args.get("first")
        self.evac, self.w, self.n0, self.typ = (args.get(k) for k in ("evac", "w", "n0", "typ"))
        self.k0, self.nk, self.cols, self.units, self.aux = (args.get(k) for k in ("k0", "nk", "cols", "units", "aux"))


def toeplitz_constants():
    d = np.arange(384) - (P - 1)
    n = np.maximum(d, 0)
    exact = N_BUCKETS // 2
    nf = np.maximum(n, 1).astype(np.float32)
    large = exact + (np.log(nf / np.float32(exact)).astype(np.float32)
                     / np.float32(math.log(MAX_DISTANCE / exact)) * np.float32(N_BUCKETS - exact)).astype(np.int32)
    bucket = np.where(n < exact, n, np.minimum(large, N_BUCKETS - 1))
    onehot = (np.arange(N_BUCKETS)[:, None] == bucket[None, :]).astype(np.float32)
    times = (d <= 128).astype(int) + (d % 4 == 0) + (d % 16 == 0)
    dil = np.where((d >= 0) & (times > 0), np.log(np.maximum(times, 1)), NEG)
    moba = np.where(d >= 0, 0.0, NEG)
    mask = np.concatenate([np.tile(dil, (8, 1)), np.tile(moba, (8, 1))]).astype(np.float32)
    return onehot, mask


def rope_constants():
    freqs = HD2 // 4
    row = np.repeat(np.arange(S // GRID_W), GRID_W).astype(np.float32)
    col = np.tile(np.arange(GRID_W), S // GRID_W).astype(np.float32)
    inv = (np.float32(ROPE_THETA) ** (-np.arange(freqs, dtype=np.float32) / np.float32(freqs))).astype(np.float32)
    ang = np.concatenate([row[:, None] * inv, col[:, None] * inv], axis=-1)
    c, s = np.cos(ang).astype(np.float32), np.sin(ang).astype(np.float32)
    return np.concatenate([c, c], axis=-1), np.concatenate([-s, s], axis=-1)


def make_plan():
    jobs = []

    def job(evac, w, n0, typ, slot, k0=0, nk=KT, n=NW, ready=None, **args):
        units = [[0, 1], [2, 3], [4, 5], [6, 7]] if nk == 8 else [[0, 1], [2, 3], [4], [5]]
        jb = Step("job", evac=evac, w=w, n0=n0, typ=typ, slot=slot, k0=k0, nk=nk, cols=n, units=units,
                             ready=ready or {}, aux=[[], [], [], []], **args)
        jobs.append(jb)
        return jb

    def put(jb, q, kind, **args):
        p = Step(kind, **args)
        jb.aux[q].append(p)
        return p

    def lo_of(t, i=4):
        return ("t_lo", t, 4, i)

    def quarters(t):
        return {q: [lo_of(t, q + 1)] for q in range(NQ)}

    def transposed(jb, q, src, slot, ready, scale=None, shift=None, imm=1.0, banks=(0, 1, 2, 3)):
        return put(jb, q, "T", src=src, slot=slot, scale=scale, shift=shift, imm=imm, banks=banks,
                   after={"pe": ready})

    ada = [dict(l=l, c=c) for l in range(LAYERS) for c in range(6 * D // NW)]
    n_ada = [0]

    def ada_job():
        a = ada[n_ada[0]]
        n_ada[0] += 1
        return job("ada", f"ada{a['l']}", a["c"] * NW, "C", None, l=a["l"], c=a["c"], ready={0: [("pp_c4", None, 0, 1)]})

    j_qa = job("cp", "w_in", 0, "W", 0, dst=("qT", 0))
    st_x = put(j_qa, 0, "pn_stat", res="x", xn="RB", after={"act": [("x_in", None, 0, 16)], "dve": [("x_in", None, 0, 16)]})
    put(j_qa, 0, "pp")
    t_x = transposed(j_qa, 0, "RB", 0, [("pn_xn", st_x, 2, 2)], scale=("C1", 0))
    u = quarters(t_x)
    j_qa.ready = u
    j_qa.first, j_qa.aux[0] = [j_qa.aux[0][:1], [], j_qa.aux[0][1:], []], []
    put(j_qa, 1, "pp_c")
    j_ka = job("cp", "w_in", 512, "W", 0, ready=u, dst=("qT", 1))
    st_m = put(j_ka, 0, "pn_stat", res="c", xn="RA", after={"act": [("m_in", None, 0, 16)], "dve": [("m_in", None, 0, 16)]})
    put(j_ka, 1, "toep")
    t_m = transposed(j_ka, 3, "RA", 1, [("pn_xn", st_m, 2, 2)], scale=("C1", 8))
    ada_job()
    j_va = job("cp", "w_in", 1024, "A", 0, ready=u, dst=("Yc", 0))
    put(j_va, 1, "pp2")
    j_va.after = {"act": [("pp_cols2", None, 0, 1)]}
    ada_job()
    j_qb = job("cp", "w_in", 1536, "W", 0, ready=u, dst=("RA", 0))
    j_qb.after = {"act": [("t_pe", t_m, 4, 4)]}
    j_kb = job("cp", "w_in", 2048, "W", 0, ready=u, dst=("RA", 1))
    j_vb = job("cp", "w_in", 2560, "A", 0, ready=u, dst=("Yc", 1))
    ada_job()
    um = quarters(t_m)
    j_km0 = job("cp", "w_kv", 0, "W", 1, ready=um, dst=("TT", 0))
    j_km1 = job("cp", "w_kv", 512, "W", 1, ready=um, dst=("TT", 1))
    j_vm0 = job("cp", "w_kv", 1024, "A", 1, ready=um, dst=("cres", 0))
    j_vm0.after = {"act": [("pn_xn", st_m, 2, 2)]}
    srcs = {0: [("cp_done", j_va, 1, 1)], 1: [("cp_done", j_vb, 1, 1)]}
    for group, hosts in enumerate(((j_qb, j_kb, j_vb), (j_km0, j_km1, j_vm0))):
        slots = [(jb, q) for jb in hosts for q in range(NQ)]
        pair = {}
        for i, (jb, q) in enumerate(slots):
            if i % 2 == 0 and 1 <= i // 2 <= 4:
                put(jb, q, "baT", of=pair[i // 2 - 1])
            if i % 2 == 0 and i // 2 < 4:
                pair[i // 2] = put(jb, q, "ba", g=4 * group + i // 2, ready=srcs[group])
            if i % 2 == 1 and 1 <= i // 2 <= 4:
                put(jb, q, "baV", of=pair[i // 2 - 1])
        put(hosts[2], 1, "ynS", half=group)
        put(hosts[2], 2, "ynM", half=group)
    put(j_km0, 1, "ynL", slot=2, half=0)
    put(j_vm0, 3, "ynL", slot=2, half=1)
    y_ready = {0: [("yn_lo", None, 0, 1)], 2: [("yn_lo", None, 0, 2)]}
    j_o0 = job("res", "w_out", 0, "A", 2, ready=y_ready, res="x")
    ada_job()
    j_o1 = job("res", "w_out", 512, "A", 2, res="x")
    j_vm1 = job("cp", "w_kv", 1536, "A", 1, ready=um, dst=("cres", 1))

    def cross_norm(col, jb, wait_job):
        st = put(jb, 0, "pn_stat", res="x", xn="RB",
                 after={"act": [("res_done", wait_job, 1, 1)], "dve": []})
        return transposed(jb, 2, "RB", 0, [("pn_xn", st, 2, 2)], scale=("C1", col))

    t_c = cross_norm(24, j_vm1, j_o1)
    j_q0 = job("cp", "w_q", 0, "W", 0, ready=quarters(t_c), dst=("qT", 0))
    ada_job()
    j_q1 = job("cp", "w_q", 512, "W", 0, dst=("qT", 1))
    mh = [ada_job() for _ in range(5)]
    mas = []
    for h in range(HEADS_MEM):
        m = put(mh[h], 0, "ma", h=h, slot=1, ready=[("cp_done", j_q1, 1, 1)])
        put(mh[h], 3, "maT", of=m)
        put(mh[h + 1], 1, "maV", of=m)
        mas.append(m)
    j_mo0 = job("res", "w_o", 0, "A", 1, ready={q: [("ma_lo", mas[q], 1, 1)] for q in range(4)}, res="x")
    ada_job()
    j_mo1 = job("res", "w_o", 512, "A", 1, res="x")
    put(mh[4], 3, "ctx_load", after={"pool": [("ma_pv", mas[3], 1, 1)]})
    t_f = cross_norm(32, ada_job(), j_mo1)

    def gate_up(c):
        n = min(NW, FF1 - c * NW)
        slot = 1 + (c // 2) % 2
        gj = job("cgate", "w_gate", c * NW, "W", 0, n=n, ready=quarters(t_f), c=c)
        uj = job("up", "w_up", c * NW, "W", 0, n=n, c=c, out=slot)
        uj.gate = gj
        return uj

    def down(k, ups, nk):
        r = {0: [("up_lo", ups[0], 1, 1)], 2: [("up_lo", ups[1], 1, 1)]}
        jbs = []
        for n in range(2):
            jbs.append(job("res", "w_down", n * NW, "A", 1 + k % 2, k0=k * KT, nk=nk, ready=r, res="x"))
            ada_job()
        return jbs

    def mods(jb, jt, l, s):
        m = put(jb, 0, "modfin", l=l, s=s)
        put(jt, 0, "modT", of=m)

    ups = [gate_up(c) for c in range(4)]
    mods(ups[2].gate, ups[2], 0, "c")
    mods(ups[3].gate, ups[3], 0, "x")
    d0 = down(0, ups[0:2], 8)
    ups += [gate_up(c) for c in range(4, 6)]
    d1 = down(1, ups[2:4], 8)
    d2 = down(2, ups[4:6], 6)

    def prenorm(jb, q, jt, qt, l, s, which, xn, slot, wait=(), po=None):
        st = put(jb, q, "pn_stat", res=s, xn=xn, after={"act": wait, "dve": wait}, po=po)
        return transposed(jt, qt, xn, slot, [("pn_xn", st, 2, 2)], scale=("gs", l, s, which), shift=("sh", l, s, which))

    CONV_NAMES = ["kv", "q0", "q1", "ga1", "gg1", "gv0", "gv1", "gu0", "gu1", "gate0", "gate1", "branch0", "branch1", "gate2",
                  "gate3", "branch2"]
    CONV_AT = {"x": [0, 0, 1, 2, 1, 3, 3, 0, 3, 4, 5, 5, 6, 6, 6, 6], "c": [2, 2, 0, 2, 1, 3, 3, 0, 2, 4, 4, 6, 6, 5, 6, 5]}
    CONV_PE_AT = [(name, q) for name in ("gate2", "gate3", "branch2") for q in range(3)]

    def glu_jobs(l, t_h, slot, half):
        a = job("glu_a", f"win{l}", CG_OFF + half * NW, "W", slot, half=half, ready=quarters(t_h))
        return a, job("glu_g", f"win{l}", CG_OFF + D + half * NW, "W", slot, half=half, of=a)

    def mixer(l, s, t_h, slots, tab=None, kvc=None, first=None):
        w = f"win{l}"
        own = 2 if s == "x" else 0
        h_, a_, b_ = slots
        J = {}

        def add(name, *args, **kw):
            J[name] = job(*args, **kw)
            return J[name]

        J["ga0"], J["gg0"] = ga0, gg0 = first or glu_jobs(l, t_h, h_, 0)
        kv = add("kv", "kv", w, K_OFF, "A", h_, own=own)
        q0 = add("q0", "q", w, Q_OFF, "A", h_, c=0)
        q1 = add("q1", "q", w, Q_OFF + NW, "A", h_, c=1)
        J["ga1"], J["gg1"] = ga1, gg1 = glu_jobs(l, t_h, h_, 1)
        gv = [add(f"gv{c}", "gelu", w, GV_OFF + c * NW, "A", h_, dst=("RA", c)) for c in range(2)]
        gu = [add(f"gu{c}", "gelu", w, GU_OFF + c * NW, "A", h_, dst=("RB", c)) for c in range(2)]
        gates, branches = [], []

        def pair(b, name, slot):
            for j in range(2):
                n = len(gates)
                gates.append(add(f"gate{n}", "gate", w, GATE_OFF + b * D + j * NW, "A", h_))
            for j in range(2):
                n = len(branches)
                branches.append(add(f"branch{n}", "branch", f"{name}{l}", j * NW, "A", slot, j=j, gate=gates[n], first=b == 0))
            return branches[-2:]

        ba, bg, co = pair(0, "attn", a_), pair(1, "gmlp", b_), pair(2, "conv", b_)
        wo = [job("ycp", f"out{l}", j * NW, "A", a_, j=j) for j in range(2)]

        if kvc:
            rkc = put(ga0, 0, "rk", of=kvc, s="c", tab=tab)
            tkc = put(ga0, 3, "tk", of=rkc, own=0)
            ga0.after = {"act": [("tk_pe", tkc, 1, 1)]}
        else:
            tab = tab or put(gg0, 0, "tab", l=l, s=s)
        if s == "x":
            put(kv if first else gg0, 1 if first else 0, "rope", tab=tab)
        put(gv[0], 0, "gb", src=("gmlp_g", l))
        if (l, s) != (0, "x"):
            put(kv, 2, "wsT", l=l)
        kv.after = {"act": [("gl_o", gg0, 1, 1)]}
        rk = put(q0, 0, "rk", of=kv, s=s, tab=tab)
        q0.after = {"act": [("rk_done", rk, 1, 1)]}
        tk = put(q1, 2, "tk", of=rk, own=own)
        rq0 = put(q1, 0, "rq", of=q0, s=s, tab=tab)
        q1.after = {"act": [("rq_done", rq0, 1, 1)]}
        tq0 = put(ga1, 1, "tq", of=rq0, banks=(0, 1))
        rq1 = put(gg1, 0, "rq", of=q1, s=s, tab=tab)
        ga1.after = {"act": [("tk_pe", tk, 1, 1)]}
        gg1.after = {"act": [("rq_done", rq1, 1, 1)]}

        hosts = [ga1, gg1, gv[0], gv[1], gu[0], gu[1], gates[0], gates[1], ba[0]]
        at, tq = [], [tq0]
        for h in range(QH + 1):
            t, e = (0, 1) if h > 1 else (1, 2)
            if h == 1:
                put(hosts[h], 0, "atR", of=at[0])
                put(hosts[h], 0, "atS", of=at[0])
            if h < QH:
                p = put(hosts[h], 0 if h else 2, "at", h=h, s=s, own=own, l=l, slot=a_, tk=tk, rq=tq[h // 4])
            if h:
                put(hosts[h], t, "atT", of=at[h - 1])
                put(hosts[h], e, "atV", of=at[h - 1])
                put(hosts[h], 2 if h < QH else 1, "atH", of=at[h - 1])
                put(hosts[h], (3 if h == 1 else 2) if h < QH else 1, "atL", of=at[h - 1])
            if h < QH:
                put(hosts[h], e if h else 3, "atE", of=p)
                if h:
                    put(hosts[h], 2 if h > 1 else 3, "atR", of=p)
                    put(hosts[h], 3, "atS", of=p)
                at.append(p)
            if h == 2:
                tq.append(put(gv[0], 3, "tq", of=rq1, banks=(0, 1)))
        ba[0].ready = ba[1].ready = {q: [("at_lo", at[2 * q + 1], 1, 1)] for q in range(NQ)}

        for c in range(2):
            gv[c].after = {"dve": [("tq_pe", tq[c], 1, 1)]}
        put(gv[1], 1, "gv_sq", gv=gv, half=0)
        put(gu[0], 1, "gv_sq", gv=gv, half=1)
        gvr = put(gu[0], 2, "gv_rms")
        gvn = [put(gu[0], 3, "gv_norm", of=gvr, half=0), put(gu[1], 1, "gv_norm", of=gvr, half=1)]
        put(gates[0], 0, "gb", src=("grow", l, s, 0))
        sp = put(ba[0], 3, "spatial", l=l, of=gvn[1], gu=gu)
        ba[0].after = {"dve": [("sp_done", sp, 1, 1)]}
        t_g = transposed(ba[1], 2, "RB", b_, [("sp_done", sp, 1, 1)], imm=0.5)
        bg[0].ready = bg[1].ready = quarters(t_g)
        gates[0].after = {"act": [("gl_o", gg1, 1, 1)]}

        cv0 = [put(kv, 0, "conv0", half=0, l=l, job=gg0), put(gv[1], 2, "conv0", half=1, l=l, job=gg1)]
        pe_taps = range(TAPS2 - len(CONV_PE_AT), TAPS2)
        ops = [(half, tap) for half in range(2) for tap in range(1, TAPS2) if half == 0 or tap not in pe_taps]
        slots = [(J[name], q) for name in ("gate2", "gate3", "branch2", "branch3") for q in range(NQ)]
        for tap, (name, q) in zip(pe_taps, CONV_PE_AT):
            jb, at_q = slots[slots.index((J[name], q)) + 2]
            dg = put(J[name], q, "diag", l=l, tap=tap)
            put(jb, at_q, "diag_mm", of=dg, job=gg1, first=tap == pe_taps[0], last=tap == pe_taps[-1])
        for name, n in zip(CONV_NAMES, CONV_AT[s]):
            for q in range(NQ):
                for half, tap in ops[n * q // NQ:n * (q + 1) // NQ]:
                    put(J[name], q, "conv", half=half, l=l, of=cv0[half], taps=[tap])
            ops = ops[n:]
        put(bg[1], 0, "diag_add", of=dg)
        lm = put(gates[4], 0, "ln_mu", l=l, rb_free=("t_pe", t_g, 4, 4))
        put(gates[4], 3, "ln_var", of=lm)
        lo = [put(gates[5], 1 + 2 * h, "ln_out", of=lm, l=l, slot=b_, half=h) for h in range(2)]
        co[0].ready = co[1].ready = {0: [("ln_lo", lo[0], 1, 1)], 2: [("ln_lo", lo[1], 1, 1)]}
        t1 = transposed(co[1], 2, "RA", a_, [("br_out", co[0], 1, 1)], imm=0.5, banks=(0, 1))
        t2 = transposed(wo[0], 1, "RA", a_, [("br_out", co[1], 1, 1)], imm=0.5, banks=(2, 3))
        wo[0].ready = {q: [lo_of(t1 if q < 2 else t2, q + 1)] for q in range(NQ)}
        wo[0].after = {"dve": [("ln_lo", lo[1], 1, 1)]}
        return J, co, wo

    def ffn(l, s, host, wait, slot, qs=(0, 1, 2), jt=None):
        po = put(host, qs[0], "po", res=s, wait=wait)
        wait.then.append(po)
        put(host, qs[0], "gb", src=("grow", l, s, 1))
        return prenorm(host, qs[1], jt or host, qs[2], l, s, 1, "RB", slot, po=po)

    def mlp_jobs(l, s, t, slots, f10=None):
        i_, o1, o2 = slots
        f1, f2 = [], []

        def up2(c):
            f1.append(f10 if f10 and c == 0 else job("relu2", f"ff1{l}", c * NW, "W", i_, c=c, out=(o1, o2)[(c // 2) % 2], ready=quarters(t)))

        def dn(k):
            rr = {0: [("r2_lo", f1[2 * k], 1, 1)], 2: [("r2_lo", f1[2 * k + 1], 1, 1)]}
            for n in range(2):
                f2.append(job("acc0" if k == 0 else "accy" if k == 3 else "acc", f"ff2{l}", n * NW, "A", (o1, o2)[k % 2], k0=k * KT, ready=rr, j=n))
                f2[-1].first_of, f2[-1].before = f2[n], f2[max(0, len(f2) - 3)]
                if o1 == o2 and (k < 2 or k == 2 and n == 0):
                    ada_job()

        if f10:
            f10.ready = quarters(t)
        order = ((0, 1, 2, 3), "d0", (4, 5), "d1", (6, 7), "d2", "d3")
        if o1 == o2:
            order = ((0, 1), "d0", (2, 3), "d1", (4, 5), "d2", (6, 7), "d3")
        for step in order:
            if step[0] == "d":
                dn(int(step[1]))
            else:
                for c in step:
                    up2(c)
        return f1, f2

    t_next = prenorm(d1[1], 2, d2[0], 2, 0, "c", 0, "RA", 0, [("ctx_in", None, 0, 16), ("cp_done", j_q0, 1, 1)])
    put(d2[1], 1, "gb", src=("g_final",))
    J, co, wo = mixer(0, "c", t_next, (0, 1, 2))
    fin = Step("final", after={"act": [("res_done", d2[1], 1, 1)], "dve": [("res_done", d2[1], 1, 1)]})
    J["ga0"].aux[2].insert(0, fin)
    t_next = prenorm(co[0], 0, wo[0], 3, 0, "x", 0, "qT", 2, [("fin_x", None, 0, 1)])
    first = glu_jobs(0, t_next, 2, 0)
    t = ffn(0, "c", first[0], wo[1], 0, (0, 1, 1), first[1])
    f1, f2 = mlp_jobs(0, "c", t, (0, 1, 1))
    tab = put(f2[6], 0, "tab", l=0, s="x")
    f1[0].after = {"act": [("gl_o", first[1], 1, 1)]}
    last_f2 = f2[-1]
    J, _, wo = mixer(0, "x", t_next, (2, 1, 0), tab, first=first)
    po_c = Step("po", res="c", wait=last_f2)
    J["kv"].aux[0].insert(0, po_c)
    t = ffn(0, "x", ada_job(), wo[1], 2)
    f1, f2 = mlp_jobs(0, "x", t, (2, 1, 0))
    mods(f1[4], f1[5], 1, "c")
    mods(f2[2], f2[3], 1, "x")
    t_c1 = prenorm(f2[4], 0, f2[5], 0, 1, "c", 0, "RA", 2, po=po_c)
    kvc = job("kv", "win1", K_OFF, "A", 2, ready=quarters(t_c1), own=0)
    tab = put(f2[6], 0, "tab", l=1, s="x")
    po = put(kvc, 0, "po", res="x", wait=f2[-1])
    f2[-1].then.append(po)
    t_next = prenorm(kvc, 1, kvc, 3, 1, "x", 0, "RB", 1, po=po)
    J, _, wo = mixer(1, "x", t_next, (1, 0, 2), tab, kvc)
    f10 = job("relu2", "ff11", 0, "W", 1, c=0, out=0)
    t = ffn(1, "x", f10, wo[1], 1, (0, 0, 0))
    f1, f2 = mlp_jobs(1, "x", t, (1, 0, 2), f10)
    tail = [Step("po", res="x", wait=f2[-1])]

    count = {}
    frees = dict(cp="cp_done", q="q_cp", kv="kv_cp", res="res_done", gelu="ge_out", glu_a="gl_a", glu_g="gl_th",
                 gate="ga_th", branch="br_out", relu2="r2_relu", acc0="ac_cp", acc="ac_add", accy="y_cp", ycp="y_cp",
                 cgate="cg_cp", up="up_mul", ada="ad_cp")
    bank = {}

    def number(x, kind):
        x.n = count.get(kind, 0)
        count[kind] = x.n + 1

    def use(p, banks, after):
        p.bank_free = {b: bank[b] for b in banks if b in bank}
        for b in banks:
            bank[b] = after

    gb_reader, gb_count, conv_ops = None, 0, 0
    for jb in jobs + [None]:
        for p in ([x for q in (jb.first if jb is jobs[0] else []) + jb.aux for x in q] if jb else tail):
            number(p, p.kind)
            k = p.kind
            if k == "gb":
                p.free, gb_count = gb_reader, gb_count + 1
            elif k in ("final", "gv_norm"):
                p.gb = gb_count
                gb_reader = {"final": ("fin_x", None, 0, 1), "gv_norm": ("gn_done", p, 1, 1)}[k]
            elif k == "T":
                p.bank_free = {b: bank[b] for b in p.banks if b in bank}
                for b in p.banks:
                    bank[b] = ("t_lo", p, 4, b + 1)
            elif k == "pp_c":
                use(p, (3,), ("pp_c4", None, 0, 1))
            elif k == "pp":
                use(p, (0,), ("pp_cols", None, 0, 1))
            elif k == "pp2":
                use(p, (0, 1, 2), ("pp_cols2", None, 0, 1))
            elif k == "toep":
                use(p, (3,), ("tp_r", None, 0, 1))
            elif k == "ba":
                use(p, (0, 1), ("ba_sb", p, 2, 2))
            elif k == "baT":
                use(p, (2, 3), ("ba_pt", p.of, 2, 2))
            elif k == "baV":
                use(p, (0,), ("ba_y", p.of, 1, 1))
            elif k == "ynM":
                use(p, (2,), ("yn_ms", None, 0, p.half + 1))
            elif k == "ma":
                use(p, (0,), ("ma_p", p, 1, 1))
            elif k == "maT":
                use(p, (1,), ("ma_pt", p.of, 1, 1))
            elif k == "maV":
                use(p, (2,), ("ma_lo", p.of, 1, 1))
            elif k == "modT":
                use(p, (3,), ("mf_c", p.of, 1, 1))
            elif k == "rq":
                if p.s == "x":
                    gb_reader = ("rq_done", p, 1, 1)
            elif k == "tq":
                use(p, p.banks, ("tq_cp", p, 1, 1))
            elif k == "tk":
                use(p, (2,), ("tk_cp", p, 1, 1))
            elif k == "at":
                use(p, (0, 1), ("at_p", p, 2, 2))
            elif k == "atT":
                use(p, (2, 3), ("at_pt", p.of, 1, 1))
            elif k == "atV":
                use(p, (2,), ("at_lo", p.of, 1, 1))
            elif k == "spatial":
                use(p, (0, 1, 2, 3), ("sp_done", p, 1, 1))
            elif k == "rope":
                p.free = gb_reader
            elif k == "wsT":
                p.at_before, p.po_before = count.get("atT", 0), count.get("po", 0)
                use(p, (3,), ("ws_cp", p, 1, 1))
            elif k == "conv":
                conv_ops += 4 * len(p.taps)
            elif k == "diag_mm":
                p.bank_free = {}
                if p.first:
                    use(p, (0, 1), ("dg_add", None, 0, count.get("diag_add", 0) + 1))
            elif k == "diag":
                p.at_before = count["atT"]
            elif k == "diag_add":
                p.conv_after = conv_ops
            elif k == "ln_mu":
                p.conv_after = conv_ops
                use(p, (2,), ("ln_d", p, 1, 1))
            elif k == "ln_var":
                use(p, (3,), ("ln_n", p.of, 1, 1))
        if jb:
            number(jb, jb.evac)
            jb.po_before = count.get("po", 0)
            if jb.evac in ("ycp", "accy"):
                jb.gb, jb.y = gb_count, count.get("y", 0)
                count["y"] = jb.y + 1
                jb.free = gb_reader = ("y_cp", None, 0, jb.y + 1)
            else:
                jb.free = (frees[jb.evac], jb, 1, 1)
    for i, jb in enumerate(jobs):
        jb.i = i
        jb.two_back = jobs[i - 2] if i >= 2 else None
    return jobs, tail


SEMS = """x_in m_in ctx_in pr_in pr_in2 c_in rb_in cst_in tables_in ident_ready ones_ready c4_zeroed glp_zeroed
pp_pc pp_th pp_c4 pp_pe pp_cols pp_pe2 pp_cols2 tp_tab tp_pe tp_r tp_st bias_in0 bias_in1
pn_ss pn_xn t_pe t_hi t_lo
ba_s ba_sb ba_nm ba_p ba_pn ba_tp ba_pt ba_pv ba_y yn_sq yn_ss yn_ms yn_y yn_hi yn_lo
ma_s ma_nm ma_p ma_pn ma_tp ma_pt ma_pv ma_hi ma_lo
cp_done res_done cg_cp cg_v cg_t cg_s up_mul up_hi up_lo ad_cp ad_st fin_ss fin_x
mf_in mf_sum mf_pe mf_c mf_r mf_st gb_in q_cp kv_cp gqk_in tab_done rq_done rk_done tq_pe tq_cp tk_pe tk_cp
at_s at_nb at_p at_r at_pn at_tp at_pt at_pv at_hi at_lo
ge_sq ge_z ge_t ge_out gl_a gl_th gl_o gn_ss gn_done sp_pe sp_done
ln_mean ln_d ln_sq ln_vs ln_n ln_s ln_th ln_r ln_hi ln_lo ga_th br_out cv_first cv_done dg_ready dg_used dg_add ws_in ws_pe ws_cp
r2_relu r2_sq r2_hi r2_lo ac_cp ac_add y_add y_sq y_cp po_x out_st
act_step dve_step""".split()


def value(e):
    name, x, per, i = e
    return i if x is None else x.n * per + i


def build(nc, A, out):
    jobs, tail = make_plan()
    with ExitStack() as ctx:
        def sb(name, shape, dt=F32):
            return ctx.enter_context(nc.sbuf_tensor(name, shape, dt))

        sem = {n: ctx.enter_context(nc.semaphore(n)) for n in SEMS}
        loaded = [ctx.enter_context(nc.semaphore(f"unit_loaded{q}")) for q in range(NQ)]
        hi_done = [ctx.enter_context(nc.semaphore(f"unit_hi{q}")) for q in range(NQ)]
        lo_done = [ctx.enter_context(nc.semaphore(f"unit_lo{q}")) for q in range(NQ)]
        used = [ctx.enter_context(nc.semaphore(f"unit_used{q}")) for q in range(NQ)]

        raw = sb("raw", [P, NQ, 2, NW])
        whi = sb("whi", [P, NQ, 2, NW], F32R)
        wlo = sb("wlo", [P, NQ, 2, NW], F32R)
        ohi = sb("ohi", [P, 3, KT, S], F32R)
        olo = sb("olo", [P, 3, KT, S], F32R)
        chi = sb("chi", [P, KT, P], F32R)
        res = {"x": sb("xres", [P, 2 * D]), "c": sb("cres", [P, 2 * D])}
        RA, RB = sb("RA", [P, 2 * D]), sb("RB", [P, 2 * D])
        qT = sb("qT", [P, 8 * S])
        kvb = sb("kvb", [P, 4, 2 * S])
        Pb, PTb = sb("Pb", [P, 2, 2 * S]), sb("PTb", [P, 4 * S])
        AB = sb("AB", [P, 4 * S])
        GLP = sb("GLP", [P, KT, S + 2 * PAD2])
        Yc = sb("Yc", [P, 8 * S])
        TT = sb("TT", [P, 2, 4 * S])
        GB = sb("GB", [P, D])
        ident, ones = sb("ident", [P, P]), sb("ones", [P, P])
        C1, C2, CW = sb("C1", [P, P]), sb("C2", [P, 88]), sb("CW", [P, LAYERS, TAPS2 * KT])
        wsT = sb("wsT", [P, 4, P])
        cos2, sinpm = sb("cos_rows", [P, 2, HD2]), sb("sin_rows", [P, 2, HD2])
        GQK = sb("GQK", [P, 2, HD2])
        stage = sb("stage", [4, NW])
        csb = sb("csb", [P, 2, 16])
        MF = sb("MF", [48, 4, P])
        modc = sb("modc", [P, 4, 48])
        gsc = sb("gsc", [P, 4, 16])
        st = sb("st", [P, 16, 16])
        den = sb("den", [P, 64])
        tabT = sb("tabT", [N_BUCKETS, HEADS1])

        gps = ctx.enter_context(nc.psum_tensor("gps", [P, 2, 2 * NW], F32))
        aps = ctx.enter_context(nc.psum_tensor("aps", [P, 4, NW], F32))
        mod_dram = nc.dram_tensor("mod_dram", [LAYERS, 4, 6 * D], F32)
        grow_dram = nc.dram_tensor("grow_dram", [LAYERS, 2, 2, D], F32)
        toep_dram = nc.dram_tensor("toep_dram", [HEADS1, 384], F32)

        flat = {"RA": RA, "RB": RB, "qT": qT, "Yc": Yc, "xres": res["x"], "cres": res["c"]}

        def rows(t):
            return t[:, :].rearrange("p (m d) -> p m d", m=2)

        def bank(b):
            return aps[:, b, :]

        PR = Yc[:, 0:7 * P].rearrange("p (i c) -> p i c", i=7)
        bias = kvb[:, :, :].rearrange("p a b -> p (a b)")[:, 0:2 * 4 * S].rearrange("p (g h j) -> p g h j", g=2, h=4)
        kmT, vm = TT, rows(res["c"])
        OH = AB[0:N_BUCKETS, 0:384]
        MSK = GB[0:HEADS1, 0:384]
        TR = GB[0:HEADS1, 384:768]
        MODS = {(0, "c"): 0, (0, "x"): 1, (1, "c"): 2, (1, "x"): 3}

        def column(spec, kt):
            if spec is None:
                return None
            if spec[0] == "C1":
                return C1[:, spec[1] + kt:spec[1] + kt + 1]
            _, l, s, which = spec
            i = MODS[l, s]
            if spec[0] == "gs":
                return gsc[:, i, 8 * which + kt:8 * which + kt + 1]
            return modc[:, i, 24 * which + kt:24 * which + kt + 1]

        def wait(eng, *events):
            for e in events:
                eng.wait_ge(sem[e[0]], value(e))

        def ev(name, x, per=1, i=1):
            return (name, x, per, i)

        def weight(jb, q):
            ks = jb.units[q]
            r0 = (jb.k0 + ks[0]) * P
            return A[jb.w][r0:r0 + len(ks) * P, jb.n0:jb.n0 + jb.cols].rearrange("(k p) n -> p k n", p=P)

        def part(t, jb, q):
            return t[:, q, 0:len(jb.units[q]), 0:jb.cols]

        def psum_job(jb):
            return gps[:, jb.i % 2, :]

        def tiles(ap, a):
            return ap.rearrange("p (a b) -> p a b", a=a)

        def t_step(p, b):
            if len(p.banks) == 4:
                return 1
            return 1 if b in (0, 3) else 3

        block = ctx.enter_context(nc.Block())

        @block.sync
        def _(sp):
            def load(dst, src, name):
                sp.dma_start(dst, src).then_inc(sem[name], 16)

            load(rows(res["x"]), A["x"].rearrange("(m p) d -> p m d", p=P), "x_in")
            for jb in jobs:
                if jb.i == 1:
                    load(PR[0:8, 6, :], A["c"][0].rearrange("(k p) -> k p", p=P), "c_in")
                    load(PR[8:16, 6, :], A["c_ctx"].rearrange("(k p) -> k p", p=P), "c_in")
                    load(rows(res["c"]), A["mem"].rearrange("(m p) d -> p m d", p=P), "m_in")
                for q in range(NQ):
                    if jb.i:
                        sp.wait_ge(lo_done[q], jb.i)
                    sp.dma_start(part(raw, jb, q), weight(jb, q)).then_inc(loaded[q], 16)
            for m in range(2):
                wait(sp, ev("po_x", tail[0], 2, m + 1))
                sp.dma_start(out[0][m * P:(m + 1) * P, :], rows(res["x"])[:, m, :]).then_inc(sem["out_st"], 16)
            sp.wait_ge(sem["out_st"], 32)

        @block.gpsimd
        def _(pool):
            def load(dst, src, name):
                pool.dma_start(dst, src).then_inc(sem[name], 16)

            pool.memset(ident[:], 0.0).then_inc(sem["ident_ready"], 1)
            pool.wait_ge(sem["ident_ready"], 1)
            pool.affine_select(out=ident[:], in_=ident[:], compare_op=ALU.not_equal, fill=1.0, base=0,
                               pattern=[[-1, P]], channel_multiplier=1).then_inc(sem["ident_ready"], 1)
            pool.memset(ones[:], 1.0 / D).then_inc(sem["ones_ready"], 1)
            r = 0
            for name in ("g_mix", "g_mem", "g_out_dil", "g_out_moba", "g_cross", "g_ffn", "conv_b"):
                n = A[name].shape[0] // P
                load(PR[r:r + n, 0, :], A[name].rearrange("(k p) -> k p", p=P), "pr_in")
                r += n
            load(PR[r:r + 3 * NT1, 0, :], A["conv_w"].rearrange("t (k p) -> (t k) p", p=P), "pr_in")
            pool.dma_start(tabT[:], A["rel_bias"].rearrange("h b -> b h"),
                           allow_slow_non_contiguous=True).then_inc(sem["rb_in"], 16)
            load(OH, A["onehot"], "rb_in")
            load(MSK, A["mask"], "rb_in")
            for l in range(LAYERS):
                r = 44 * l
                for name in ("mix_pre_g", "ffn_pre_g", "conv_norm_g", "conv_norm_b", "conv_b_2"):
                    load(PR[r:r + 8, 1, :], A[name][l].rearrange("(k p) -> k p", p=P), "pr_in2")
                    r += 8
                load(PR[r:r + 4, 1, :], A["gmlp_bs"][l], "pr_in2")
                cw = A["conv_w_2"][l].rearrange("t (k p) -> (t k) p", p=P)
                for h in range(2):
                    load(PR[0:124, 2 + 2 * l + h, :], cw[124 * h:124 * h + 124, :], "pr_in2")
            load(cos2[:], A["cos2"].rearrange("(m p) d -> p m d", p=P), "cst_in")
            load(sinpm[:], A["sinpm"].rearrange("(m p) d -> p m d", p=P), "cst_in")

            def toep(p):
                pool.wait_ge(sem["tp_r"], 1)
                pool.dma_start(toep_dram.ap(), TR).then_inc(sem["tp_st"], 16)
                pool.wait_ge(sem["tp_st"], 16)
                for g in range(2):
                    bias_load(g)

            def bias_load(g):
                src = bass.AP(tensor=toep_dram, offset=g * 4 * 384, ap=[[1, P], [384, 4], [1, S]])
                load(bias[:, g % 2], src, f"bias_in{g % 2}")

            def ba(p):
                if p.g in (2, 4):
                    g = p.g // 2 + 1
                    pool.wait_ge(sem["ba_sb"], 4 * (g - 1))
                    bias_load(g)

            def ctx_load(p):
                wait(pool, *p.after["pool"])
                load(rows(res["c"]), A["ctx"].rearrange("(m p) d -> p m d", p=P), "ctx_in")

            def modfin(p):
                pool.wait_ge(sem["ad_st"], 16 * 12 * (p.l + 1))
                if p.n:
                    pool.wait_ge(sem["mf_st"], 32 * p.n)
                v = 1 if p.s == "c" else 0
                load(MF[:, 0, :], mod_dram.ap()[p.l, v].rearrange("(r c) -> r c", c=P), "mf_in")
                load(MF[:, 1, :], mod_dram.ap()[p.l, 2 + v].rearrange("(r c) -> r c", c=P), "mf_in")
                load(MF[:, 2, :], A["ada_b"][p.l].rearrange("(r c) -> r c", c=P), "mf_in")
                load(MF[16:24, 3, :], A["mix_post_g"][p.l].rearrange("(r c) -> r c", c=P), "mf_in")
                load(MF[40:48, 3, :], A["ffn_post_g"][p.l].rearrange("(r c) -> r c", c=P), "mf_in")

            def mod_t(p):
                p = p.of
                v = 1 if p.s == "c" else 0
                wait(pool, ev("mf_r", p))
                for k in range(2):
                    pool.dma_start(grow_dram.ap()[p.l, v, k].rearrange("(r c) -> r c", c=P),
                                   MF[16 + 24 * k:24 + 24 * k, 3, :]).then_inc(sem["mf_st"], 16)
                pool.wait_ge(sem["mf_st"], 32 * (p.n + 1))

            def gb(p):
                if p.free:
                    wait(pool, p.free)
                if p.src[0] == "g_final":
                    src = A["g_final"]
                elif p.src[0] == "gmlp_g":
                    src = A["gmlp_norm_g"][p.src[1]]
                else:
                    _, l, s, k = p.src
                    src = grow_dram.ap()[l, 1 if s == "c" else 0, k]
                load(GB[:], src.partition_broadcast(P), "gb_in")

            def tab(p):
                if p.n:
                    pool.wait_ge(sem["rk_done"], p.n)
                load(GQK[:, 0, :], A["q_norm_g"][p.l].partition_broadcast(P), "gqk_in")
                load(GQK[:, 1, :], A["k_norm_g"][p.l].partition_broadcast(P), "gqk_in")

            def ws_load(p):
                if p.n:
                    pool.wait_ge(sem["at_tp"], p.at_before)
                    pool.wait_ge(sem["po_x"], 2 * p.po_before)
                else:
                    pool.wait_ge(sem["ma_tp"], HEADS_MEM)
                load(tiles(Pb[:, 0, :], 4), A["gmlp_ws"][p.l].rearrange("g p q -> p g q"), "ws_in")

            stages = dict(wsT=ws_load, toep=toep, ba=ba, ctx_load=ctx_load, modfin=modfin, modT=mod_t, gb=gb, tab=tab)
            for jb in jobs:
                for q in range(NQ):
                    for p in jb.aux[q]:
                        if p.kind in stages:
                            stages[p.kind](p)
                if jb.evac == "ada":
                    wait(pool, ev("ad_cp", jb))
                    pool.dma_start(mod_dram.ap()[jb.l, :, jb.n0:jb.n0 + NW], stage[:]).then_inc(sem["ad_st"], 16)

        @block.tensor
        def _(pe):
            mm = nc.tensor.matmul

            def free(p):
                for e in p.bank_free.values():
                    wait(pe, e)

            def pp_c(p):
                free(p)
                pe.wait_ge(sem["c_in"], 32)
                nc.tensor.transpose(aps[:, 3, 0:16], PR[0:16, 6, :], ident[0:16, 0:16]).then_inc(sem["pp_pc"], 1)

            def pp(p):
                free(p)
                pe.wait_ge(sem["ident_ready"], 2)
                pe.wait_ge(sem["pr_in"], 16 * 8)
                nc.tensor.transpose(aps[:, 0, 0:P], PR[:, 0, :], ident[:]).then_inc(sem["pp_pe"], 1)

            def pp2(p):
                free(p)
                pe.wait_ge(sem["pr_in2"], 16 * 16)
                nc.tensor.transpose(aps[:, 0, 0:88], PR[0:88, 1, :], ident[0:88, 0:88])
                for i in range(4):
                    t = nc.tensor.transpose(aps[:, 1 + i // 2, 124 * (i % 2):124 * (i % 2) + 124], PR[0:124, 2 + i, :],
                                            ident[0:124, 0:124])
                t.then_inc(sem["pp_pe2"], 1)

            def toep(p):
                free(p)
                pe.wait_ge(sem["rb_in"], 48)
                mm(aps[0:HEADS1, 3, 0:384], tabT[:], OH, start=True, stop=True).then_inc(sem["tp_pe"], 1)

            def T(p):
                src = rows(flat[p.src])
                for b, m in [(b, m) for b in p.banks for m in range(2)]:
                    for name, x, per, i in p.after["pe"]:
                        wait(pe, ev(name, x, 2, m + 1) if name == "pn_xn" else ev(name, x, per, i))
                    if m == 0 and b in p.bank_free:
                        wait(pe, p.bank_free[b])
                    for i in range(2):
                        t = nc.tensor.transpose(aps[:, b, i * S + m * P:i * S + m * P + P],
                                                src[:, m, (2 * b + i) * P:(2 * b + i + 1) * P], ident[:])
                    if m:
                        t.then_inc(sem["t_pe"], t_step(p, b))

            def ba(p):
                free(p)
                wait(pe, *p.ready)
                q_, k_ = (qT[:, 0:4 * S], qT[:, 4 * S:8 * S]) if p.g < 4 else (RA[:, 0:4 * S], RA[:, 4 * S:8 * S])
                c = (p.g % 4) * S
                for hh in range(2):
                    r = slice(HD1 * hh, HD1 * hh + HD1)
                    mm(aps[:, hh, 0:P], q_[r, c:c + P], k_[r, c:c + P], start=True, stop=True)
                    mm(aps[:, hh, P:3 * P], q_[r, c + P:c + S], k_[r, c:c + S], start=True,
                       stop=True).then_inc(sem["ba_s"], 1)

            def baT(p):
                free(p)
                for hh in range(2):
                    wait(pe, ev("ba_pn", p.of, 2, hh + 1))
                    for k in range(3):
                        t = nc.tensor.transpose(aps[:, 2 + hh, k * P:(k + 1) * P], Pb[:, hh, k * P:(k + 1) * P], ident[:])
                    t.then_inc(sem["ba_tp"], 1)

            def baV(p):
                free(p)
                v = tiles(Yc[:, (p.of.g // 4) * 4 * S:(p.of.g // 4 + 1) * 4 * S], 2)
                for hh in range(2):
                    wait(pe, ev("ba_pt", p.of, 2, hh + 1))
                    h = 2 * (p.of.g % 4) + hh
                    o = aps[HD1 * hh:HD1 * hh + HD1, 0, 0:S]
                    mm(o, v[:, 0, h * HD1:(h + 1) * HD1], PTb[:, hh * 2 * S:hh * 2 * S + S], start=True, stop=False)
                    t = mm(o[:, P:S], v[:, 1, h * HD1:(h + 1) * HD1], PTb[:, hh * 2 * S + S:hh * 2 * S + S + P],
                           start=False, stop=True)
                t.then_inc(sem["ba_pv"], 1)

            def yn_sum(p):
                pe.wait_ge(sem["ones_ready"], 1)
                pe.wait_ge(sem["yn_sq"], p.half + 1)
                free(p)
                for k in range(4):
                    t = mm(aps[:, 2, 0:S], ones[:], AB[:, k * S:(k + 1) * S], start=k == 0, stop=k == 3)
                t.then_inc(sem["yn_ss"], 1)

            def ma(p):
                free(p)
                wait(pe, *p.ready)
                for m in range(2):
                    for i in range(2):
                        k = 2 * p.h + i
                        t = mm(aps[:, 0, m * S:(m + 1) * S], qT[:, k * S + m * P:k * S + m * P + P],
                               kmT[:, k // 4, (k % 4) * S:(k % 4) * S + S], start=i == 0, stop=i == 1)
                t.then_inc(sem["ma_s"], 1)

            def maT(p):
                free(p)
                wait(pe, ev("ma_pn", p.of))
                for kb in range(2):
                    for m in range(2):
                        t = nc.tensor.transpose(aps[:, 1, kb * S + m * P:kb * S + m * P + P],
                                                Pb[:, m, kb * P:(kb + 1) * P], ident[:])
                t.then_inc(sem["ma_tp"], 1)

            def maV(p):
                free(p)
                wait(pe, ev("ma_pt", p.of))
                h = p.of.h
                for i in range(2):
                    for kb in range(2):
                        t = mm(aps[:, 2, i * S:(i + 1) * S], vm[:, kb, h * HD_MEM + i * P:h * HD_MEM + (i + 1) * P],
                               PTb[:, kb * S:(kb + 1) * S], start=kb == 0, stop=kb == 1)
                t.then_inc(sem["ma_pv"], 1)

            def mod_t(p):
                free(p)
                wait(pe, ev("mf_sum", p.of))
                nc.tensor.transpose(aps[:, 3, 0:48], MF[:, 0, :], ident[0:48, 0:48]).then_inc(sem["mf_pe"], 1)

            def tq(p):
                free(p)
                wait(pe, ev("rq_done", p.of))
                c = p.of.of.c
                q_ = rows(RA)
                for h in range(4):
                    for m in range(2):
                        t = nc.tensor.transpose(aps[:, p.banks[h // 2], (h % 2) * S + m * P:(h % 2) * S + m * P + P],
                                                q_[:, m, (4 * c + h) * P:(4 * c + h + 1) * P], ident[:])
                t.then_inc(sem["tq_pe"], 1)

            def tk(p):
                free(p)
                wait(pe, ev("rk_done", p.of))
                k_ = tiles(AB[:, 0:2 * S], 2)
                for h in range(2):
                    for m in range(2):
                        t = nc.tensor.transpose(aps[:, 2, h * S + m * P:h * S + m * P + P], k_[:, m, h * P:(h + 1) * P],
                                                ident[:])
                t.then_inc(sem["tk_pe"], 1)

            def at(p):
                wait(pe, ev("tk_cp", p.tk), ev("tq_cp", p.rq))
                kv = p.h // (QH // KVH)
                for m in range(2):
                    wait(pe, p.bank_free[m])
                    q_ = qT[:, p.h * S + m * P:p.h * S + m * P + P]
                    if p.s == "x":
                        mm(aps[:, m, 0:S], q_, kvb[:, 0, kv * S:(kv + 1) * S], start=True, stop=True)
                        t = mm(aps[:, m, S:2 * S], q_, kvb[:, 2, kv * S:(kv + 1) * S], start=True, stop=True)
                    else:
                        t = mm(aps[:, m, 0:S], q_, kvb[:, p.own, kv * S:(kv + 1) * S], start=True, stop=True)
                    t.then_inc(sem["at_s"], 1)

            def atT(p):
                free(p)
                a = p.of
                wait(pe, ev("at_pn", a))
                for kb in range(4 if a.s == "x" else 2):
                    for m in range(2):
                        t = nc.tensor.transpose(aps[:, 2 + kb // 2, (kb % 2) * S + m * P:(kb % 2) * S + m * P + P],
                                                Pb[:, m, kb * P:(kb + 1) * P], ident[:])
                t.then_inc(sem["at_tp"], 1)

            def atV(p):
                free(p)
                a = p.of
                wait(pe, ev("at_pt", a))
                kv = a.h // (QH // KVH)
                srcs = [1, 3] if a.s == "x" else [a.own + 1]
                n = 2 * len(srcs)
                for kb in range(n):
                    v = kvb[:, srcs[kb // 2], (kb % 2) * S + kv * P:(kb % 2) * S + kv * P + P]
                    t = mm(aps[:, 2, 0:S], v, PTb[:, kb * S:(kb + 1) * S], start=kb == 0, stop=kb == n - 1)
                t.then_inc(sem["at_pv"], 1)

            def spatial(p):
                wait(pe, ev("gn_done", p.of))
                g_ = rows(RA)
                for g in range(4):
                    wait(pe, p.bank_free[g])
                    for m in range(2):
                        t = mm(aps[:, g, m * S:(m + 1) * S], wsT[:, g, :], g_[:, m, g * S:(g + 1) * S], start=True, stop=True)
                    t.then_inc(sem["sp_pe"], 1)

            def ws_t(p):
                free(p)
                pe.wait_ge(sem["ws_in"], 16 * (p.n + 1))
                for g in range(4):
                    t = nc.tensor.transpose(aps[:, 3, g * P:(g + 1) * P], Pb[:, 0, g * P:(g + 1) * P], ident[:])
                t.then_inc(sem["ws_pe"], 1)

            def diag_mm(p):
                free(p)
                wait(pe, ev("gl_o", p.job), ev("dg_ready", p.of))
                for i in range(4):
                    t = mm(aps[:, i // 2, (i % 2) * S:(i % 2 + 1) * S], Pb[:, p.of.n % 2, i * P:(i + 1) * P],
                           GLP[:, 4 + i, p.of.tap:p.of.tap + S], start=p.first and i % 2 == 0, stop=p.last,
                           skip_group_check=True)
                t.then_inc(sem["dg_used"], 1)

            def ln_sum(p, src, b):
                for k in range(KT):
                    t = mm(aps[:, b, 0:S], ones[:], src[:, k * S:(k + 1) * S], start=k == 0, stop=k == KT - 1)
                return t

            def ln_mu(p):
                free(p)
                wait(pe, ev("cv_done", None, 0, p.conv_after), ("dg_add", None, 0, p.n + 1))
                ln_sum(p, Yc, 2).then_inc(sem["ln_mean"], 1)

            def ln_var(p):
                free(p)
                wait(pe, ev("ln_sq", p.of))
                ln_sum(p, RB, 3).then_inc(sem["ln_vs"], 1)

            stages = dict(pp_c=pp_c, pp=pp, pp2=pp2, toep=toep, T=T, ba=ba, baT=baT, baV=baV, ynM=yn_sum, ma=ma, maT=maT, maV=maV,
                          modT=mod_t, tq=tq, tk=tk, at=at, atT=atT, atV=atV, spatial=spatial, wsT=ws_t,
                          diag_mm=diag_mm, ln_mu=ln_mu, ln_var=ln_var)

            def unit(jb, q):
                pe.wait_ge(lo_done[q], jb.i + 1)
                wait(pe, *jb.ready.get(q, []))
                if q == 0 and jb.two_back:
                    wait(pe, jb.two_back.free)
                o = psum_job(jb)
                ks = jb.units[q]
                for i, k in enumerate(ks):
                    first, last = q == 0 and i == 0, q == NQ - 1 and i == len(ks) - 1
                    if jb.typ == "C":
                        mm(o[:, 0:NW], chi[:, k, :], whi[:, q, i, :], start=first, stop=False)
                        t = mm(o[:, 0:NW], chi[:, k, :], wlo[:, q, i, :], start=False, stop=last)
                    elif jb.typ == "A":
                        for m in range(2):
                            om = o[:, m * NW:(m + 1) * NW]
                            ah, al = ohi[:, jb.slot, k, m * P:(m + 1) * P], olo[:, jb.slot, k, m * P:(m + 1) * P]
                            mm(om, ah, whi[:, q, i, :], start=first, stop=False)
                            mm(om, ah, wlo[:, q, i, :], start=False, stop=False)
                            t = mm(om, al, whi[:, q, i, :], start=False, stop=last)
                    else:
                        for n in range(jb.cols // P):
                            on = o[:, n * S:(n + 1) * S]
                            wh, wl = whi[:, q, i, n * P:(n + 1) * P], wlo[:, q, i, n * P:(n + 1) * P]
                            mm(on, wh, ohi[:, jb.slot, k, :], start=first and n % 2 == 0, stop=False, skip_group_check=True)
                            mm(on, wh, olo[:, jb.slot, k, :], start=False, stop=False, skip_group_check=True)
                            t = mm(on, wl, ohi[:, jb.slot, k, :], start=False, stop=last, skip_group_check=True)
                t.then_inc(used[q], 1)

            for p in jobs[0].first[2]:
                stages[p.kind](p)
            for jb in jobs:
                for q in range(NQ):
                    for p in jb.aux[q]:
                        if p.kind in stages:
                            stages[p.kind](p)
                    unit(jb, q)

        @block.scalar
        def _(act):
            A_ = nc.scalar.activation
            steps = [0]

            def link(ins):
                steps[0] += 1
                ins.then_inc(sem["act_step"], 1)
                act.wait_ge(sem["act_step"], steps[0])

            def squares(src, junk, line, name):
                for m in range(2):
                    A_(junk[:, m, :], src[:, m, :], ACT.Square, accum_out=st[:, line, m:m + 1]).then_inc(sem[name], 1)

            def pn_stat(p):
                wait(act, *p.after["act"])
                x, junk = rows(res[p.res]), rows(flat[p.xn])
                for m in range(2):
                    if p.po:
                        wait(act, ev("po_x", p.po, 2, m + 1))
                    A_(junk[:, m, :], x[:, m, :], ACT.Square, accum_out=st[:, p.n % 2, m:m + 1]).then_inc(sem["pn_ss"], 1)

            def final(p):
                wait(act, *p.after["act"])
                squares(rows(res["x"]), rows(RB), 4, "fin_ss")

            def T(p):
                if p.scale:
                    wait(act, ("pp_cols", None, 0, 1) if p.scale[0] == "C1" else ("mf_c", None, 0, MODS[p.scale[1:3]] + 1))
                for b in p.banks:
                    wait(act, ev("t_pe", p, 4, b + 1))
                    if p.scale:
                        for i in range(2):
                            k = 2 * b + i
                            t = A_(ohi[:, p.slot, k, :], aps[:, b, i * S:(i + 1) * S], ACT.Identity,
                                   scale=column(p.scale, k), bias=column(p.shift, k) if p.shift else 0.0)
                    else:
                        t = A_(ohi[:, p.slot, 2 * b:2 * b + 2, :], tiles(bank(b), 2), ACT.Copy, scale=p.imm)
                    t.then_inc(sem["t_hi"], t_step(p, b))

            def pp_c(p):
                act.wait_ge(sem["pp_pc"], 1)
                A_(csb[:, 0, :], aps[:, 3, 0:16], ACT.Tanh, scale=0.5).then_inc(sem["pp_th"], 1)

            def ba(p):
                d0 = 16 + (p.n % 2) * 16
                for hh in range(2):
                    wait(act, ev("ba_nm", p, 2, hh + 1))
                    for m in range(2):
                        x = Pb[:, hh, 0:P] if m == 0 else Pb[:, hh, P:3 * P]
                        t = A_(x, x, ACT.Exp, bias=den[:, d0 + 2 * hh + m:d0 + 2 * hh + m + 1],
                               accum_out=den[:, d0 + 4 + 2 * hh + m:d0 + 5 + 2 * hh + m])
                    t.then_inc(sem["ba_p"], 1)

            def baT(p):
                for hh in range(2):
                    wait(act, ev("ba_tp", p.of, 2, hh + 1))
                    if p.n:
                        act.wait_ge(sem["ba_pv"], p.n)
                    A_(PTb[:, hh * 2 * S:hh * 2 * S + 3 * P], aps[:, 2 + hh, 0:3 * P], ACT.Copy).then_inc(sem["ba_pt"], 1)

            def baV(p):
                wait(act, ev("ba_pv", p.of))
                A_(RB[:, p.of.g * S:(p.of.g + 1) * S], aps[:, 0, 0:S], ACT.Copy).then_inc(sem["ba_y"], 1)

            def yn_squares(p):
                y = RB[:, p.half * 4 * S:(p.half + 1) * 4 * S]
                act.wait_ge(sem["ba_y"], 4 * (p.half + 1))
                if p.half:
                    act.wait_ge(sem["yn_ss"], 1)
                else:
                    act.wait_ge(sem["tp_pe"], 1)
                A_(AB[:], y, ACT.Square).then_inc(sem["yn_sq"], 1)

            def yn_hi(p):
                y = RB[:, p.half * 4 * S:(p.half + 1) * 4 * S]
                act.wait_ge(sem["yn_y"], p.half + 1)
                A_(ohi[:, p.slot, 4 * p.half:4 * p.half + 4, :], tiles(y, 4), ACT.Copy).then_inc(sem["yn_hi"], 1)

            def ma(p):
                d0 = (p.n % 2) * 8
                wait(act, ev("ma_nm", p))
                if p.n:
                    act.wait_ge(sem["ma_tp"], p.n)
                for m in range(2):
                    t = A_(Pb[:, m, 0:S], aps[:, 0, m * S:(m + 1) * S], ACT.Exp, scale=HD_MEM ** -0.5,
                           bias=den[:, d0 + 2 + m:d0 + 3 + m], accum_out=den[:, d0 + 4 + m:d0 + 5 + m])
                t.then_inc(sem["ma_p"], 1)

            def maT(p):
                wait(act, ev("ma_tp", p.of))
                if p.n:
                    act.wait_ge(sem["ma_pv"], p.n)
                A_(PTb[:, 0:2 * S], bank(1), ACT.Copy).then_inc(sem["ma_pt"], 1)

            def maV(p):
                wait(act, ev("ma_pv", p.of))
                A_(ohi[:, p.of.slot, 2 * p.of.h:2 * p.of.h + 2, :], tiles(bank(2), 2), ACT.Copy).then_inc(sem["ma_hi"], 1)

            def wsT_(p):
                act.wait_ge(sem["ws_pe"], p.n + 1)
                A_(wsT[:, :, :], tiles(bank(3), 4), ACT.Copy).then_inc(sem["ws_cp"], 1)

            def tq(p):
                wait(act, ev("tq_pe", p))
                c = p.of.of.c
                A_(qT[:, c * 4 * S:(c + 1) * 4 * S], aps[:, p.banks[0]:p.banks[0] + 2, :].rearrange("p a b -> p (a b)"),
                   ACT.Copy).then_inc(sem["tq_cp"], 1)

            def tk(p):
                wait(act, ev("tk_pe", p))
                A_(kvb[:, p.own, :], bank(2), ACT.Copy).then_inc(sem["tk_cp"], 1)

            def atE(p):
                p = p.of
                d0 = (p.n % 2) * 8
                nk = 2 * S if p.s == "x" else S
                wait(act, ev("at_nb", p))
                if p.n:
                    act.wait_ge(sem["at_tp"], p.n)
                for m in range(2):
                    u = (p.h // 4) * 8 + m * 4 + p.h % 4
                    A_(Pb[:, m, 0:nk], aps[:, m, 0:nk], ACT.Exp, scale=st[:, 3, u:u + 1],
                       bias=den[:, d0 + 2 + m:d0 + 3 + m], accum_out=den[:, d0 + 4 + m:d0 + 5 + m]).then_inc(sem["at_p"], 1)

            def atS(p):
                p = p.of
                d0 = (p.n % 2) * 8
                nk = 2 * S if p.s == "x" else S
                wait(act, ev("at_r", p), ev("at_p", p, 2, 2))
                for m in range(2):
                    t = A_(Pb[:, m, 0:nk], Pb[:, m, 0:nk], ACT.Identity, scale=den[:, d0 + 6 + m:d0 + 7 + m], bias=0.0)
                t.then_inc(sem["at_pn"], 1)

            def atT(p):
                nk = 4 * S if p.of.s == "x" else 2 * S
                wait(act, ev("at_tp", p.of))
                if p.n:
                    act.wait_ge(sem["at_pv"], p.n)
                A_(PTb[:, 0:nk], aps[:, 2:4, :].rearrange("p a b -> p (a b)")[:, 0:nk], ACT.Copy).then_inc(sem["at_pt"], 1)

            def atH(p):
                wait(act, ev("at_pv", p.of))
                A_(ohi[:, p.of.slot, p.of.h, :], aps[:, 2, 0:S], ACT.Copy).then_inc(sem["at_hi"], 1)

            def gv_sq(p):
                wait(act, ev("ge_out", p.gv[p.half]))
                j = slice(p.half * NW, (p.half + 1) * NW)
                for m in range(2):
                    A_(rows(RB)[:, m, j], rows(RA)[:, m, j], ACT.Square,
                       accum_out=st[:, 6, 2 * p.half + m:2 * p.half + m + 1]).then_inc(sem["gn_ss"], 1)

            def conv0(p):
                wait(act, ev("gl_o", p.job))
                for k in range(4 * p.half, 4 * p.half + 4):
                    t = A_(Yc[:, k * S:(k + 1) * S], GLP[:, k, 0:S], ACT.Identity, scale=CW[:, p.l, k:k + 1],
                           bias=C2[:, 44 * p.l + 32 + k:44 * p.l + 33 + k])
                t.then_inc(sem["cv_first"], 1)

            def diag(p):
                act.wait_ge(sem["at_tp"], p.at_before)
                if p.n >= 2:
                    act.wait_ge(sem["dg_used"], p.n - 1)
                for i in range(4):
                    t = A_(Pb[:, p.n % 2, i * P:(i + 1) * P], ident[:], ACT.Copy,
                           scale=CW[:, p.l, p.tap * KT + 4 + i:p.tap * KT + 5 + i])
                t.then_inc(sem["dg_ready"], 1)

            def ln_mu(p):
                wait(act, ev("ln_d", p), p.rb_free)
                A_(RB[:], Yc[:], ACT.Square).then_inc(sem["ln_sq"], 1)

            def ln_out(p):
                wait(act, ev("ln_n", p.of, 2, p.half + 1))
                half = slice(p.half * 4 * S, (p.half + 1) * 4 * S)
                for k in range(4 * p.half, 4 * p.half + 4):
                    y = Yc[:, k * S:(k + 1) * S]
                    t = A_(y, y, ACT.Identity, scale=C2[:, 44 * p.l + 16 + k:44 * p.l + 17 + k],
                           bias=C2[:, 44 * p.l + 24 + k:44 * p.l + 25 + k])
                link(t)
                A_(RB[:, half], Yc[:, half], ACT.Tanh, scale=0.5).then_inc(sem["ln_th"], 1)
                wait(act, ev("ln_r", p))
                A_(ohi[:, p.slot, 4 * p.half:4 * p.half + 4, :], tiles(RB[:, half], 4), ACT.Copy,
                   scale=0.5).then_inc(sem["ln_hi"], 1)

            stages = dict(pn_stat=pn_stat, final=final, T=T, pp_c=pp_c, ba=ba, baT=baT, baV=baV, ynS=yn_squares, ynL=yn_hi, ma=ma,
                          maT=maT, maV=maV, wsT=wsT_, tq=tq, tk=tk, atE=atE, atS=atS, atT=atT, atH=atH, gv_sq=gv_sq,
                          conv0=conv0, diag=diag, ln_mu=ln_mu, ln_out=ln_out)
            LATE = ("conv0", "diag")

            def cp(jb, g):
                name, c = jb.dst
                if name == "cres":
                    t = A_(vm[:, :, c * NW:(c + 1) * NW], tiles(g, 2), ACT.Copy)
                elif name == "TT":
                    t = A_(TT[:, c, :], g, ACT.Copy)
                else:
                    t = A_(flat[name][:, c * 2 * NW:(c + 1) * 2 * NW], g, ACT.Copy)
                t.then_inc(sem["cp_done"], 1)

            def q_rows(jb, g):
                A_(rows(RA)[:, :, jb.c * NW:(jb.c + 1) * NW], tiles(g, 2), ACT.Copy)
                A_(TT[:, 0, :], g, ACT.Square).then_inc(sem["q_cp"], 1)

            def kv_rows(jb, g):
                gt = tiles(g, 2)
                A_(tiles(AB[:, 0:2 * S], 2), gt[:, :, 0:S], ACT.Copy)
                A_(tiles(kvb[:, jb.own + 1, :], 2), gt[:, :, S:2 * S], ACT.Copy)
                A_(tiles(AB[:, 2 * S:4 * S], 2), gt[:, :, 0:S], ACT.Square).then_inc(sem["kv_cp"], 1)

            def gelu(jb, g):
                link(A_(TT[:, 0, :], g, ACT.Square))
                A_(TT[:, 0, :], TT[:, 0, :], ACT.Copy, scale=GELU_A * GELU_B, bias=GELU_A).then_inc(sem["ge_sq"], 1)

            def gelu_tanh(jb, g):
                wait(act, ev("ge_z", jb))
                A_(TT[:, 1, :], TT[:, 0, :], ACT.Tanh).then_inc(sem["ge_t"], 1)

            def glu_a(jb, g):
                A_(AB[:], g, ACT.Copy).then_inc(sem["gl_a"], 1)

            def glu_g(jb, g):
                A_(TT[:, 1, :], g, ACT.Tanh, scale=0.5).then_inc(sem["gl_th"], 1)

            def gate(jb, g):
                A_(AB[:] if jb.n % 2 == 0 else TT[:, 1, :], g, ACT.Tanh, scale=0.5).then_inc(sem["ga_th"], 1)

            def relu2(jb, g):
                t_ = TT[:, jb.n % 2, :]
                if jb.n:
                    act.wait_ge(sem["r2_lo"], jb.n - 1) if jb.n > 1 else None
                A_(t_, g, ACT.Relu).then_inc(sem["r2_relu"], 1)

            def relu2_hi(jb, g):
                t_ = TT[:, jb.n % 2, :]
                wait(act, ev("r2_sq", jb))
                k = (jb.c % 2) * 4
                A_(ohi[:, jb.out, k:k + 4, :], tiles(t_, 4), ACT.Copy).then_inc(sem["r2_hi"], 1)

            def acc0(jb, g):
                A_(rows(RB)[:, :, jb.j * NW:(jb.j + 1) * NW], tiles(g, 2), ACT.Copy).then_inc(sem["ac_cp"], 1)

            def sum_squares(jb, src):
                for m in range(2):
                    A_(Pb[:, m, :], src[:, m, :], ACT.Square,
                       accum_out=st[:, 5, 2 * jb.j + m:2 * jb.j + m + 1]).then_inc(sem["y_sq"], 1)

            def ycp(jb, g):
                if jb.po_before:
                    act.wait_ge(sem["po_x"], 2 * jb.po_before)
                sum_squares(jb, tiles(g, 2))

            def accy(jb, g):
                act.wait_ge(sem["y_add"], jb.n + 1)
                act.wait_ge(sem["po_x"], 2 * jb.po_before)
                sum_squares(jb, rows(RB)[:, :, jb.j * NW:(jb.j + 1) * NW])

            def cgate(jb, g):
                n = jb.cols // P
                if jb.n:
                    act.wait_ge(sem["cg_s"], jb.n)
                A_(GLP[:, 0:n, PAD2:PAD2 + S], tiles(g[:, 0:n * S], n), ACT.Copy).then_inc(sem["cg_cp"], 1)

            def cgate_tanh(jb, g):
                n = jb.cols // P
                wait(act, ev("cg_v", jb))
                A_(TT[:, 1, 0:n * S], Yc[:, 0:n * S], ACT.Tanh, scale=0.5).then_inc(sem["cg_t"], 1)

            def up(jb, g):
                n = jb.cols // P
                wait(act, ev("up_mul", jb))
                k = (jb.c % 2) * 4
                A_(ohi[:, jb.out, k:k + n, :], tiles(TT[:, 0, 0:n * S], n), ACT.Copy, scale=0.5).then_inc(sem["up_hi"], 1)

            def ada(jb, g):
                if jb.n:
                    act.wait_ge(sem["ad_st"], 16 * jb.n)
                A_(stage[:], g[0:4, 0:NW], ACT.Copy).then_inc(sem["ad_cp"], 1)

            evacs = dict(cp=cp, q=q_rows, kv=kv_rows, gelu=gelu, glu_a=glu_a, glu_g=glu_g, gate=gate, relu2=relu2, acc0=acc0,
                         ycp=ycp, accy=accy, cgate=cgate, ada=ada)
            second = dict(gelu=gelu_tanh, relu2=relu2_hi, cgate=cgate_tanh, up=up)

            def split(jb, q):
                act.wait_ge(loaded[q], 16 * (jb.i + 1))
                if jb.i:
                    act.wait_ge(used[q], jb.i)
                A_(part(whi, jb, q), part(raw, jb, q), ACT.Copy).then_inc(hi_done[q], 1)

            for q in range(NQ):
                for p in jobs[0].first[q]:
                    if p.kind in stages:
                        stages[p.kind](p)
                split(jobs[0], q)
            for jb in jobs + [None]:
                if jb is None:
                    break
                nxt = jobs[jb.i + 1] if jb.i + 1 < len(jobs) else None
                for q in range(NQ):
                    for p in jb.aux[q]:
                        if p.kind in stages and p.kind not in LATE:
                            stages[p.kind](p)
                    if q == NQ - 1 and jb.evac in evacs:
                        act.wait_ge(used[NQ - 1], jb.i + 1)
                        wait(act, *jb.after.get("act", []))
                        evacs[jb.evac](jb, psum_job(jb))
                    if nxt:
                        split(nxt, q)
                    if q == NQ - 1 and jb.evac in second:
                        act.wait_ge(used[NQ - 1], jb.i + 1)
                        second[jb.evac](jb, psum_job(jb))
                    for p in jb.aux[q]:
                        if p.kind in LATE:
                            stages[p.kind](p)

        @block.vector
        def _(dve):
            tt, ts, stt = nc.vector.tensor_tensor, nc.vector.tensor_scalar, nc.vector.scalar_tensor_tensor
            steps = [0]
            conv_ops = [0]

            def link(ins):
                steps[0] += 1
                ins.then_inc(sem["dve_step"], 1)
                dve.wait_ge(sem["dve_step"], steps[0])

            def f32(x):
                return x.bitcast(F32)

            def rsqrt(y, x, t):
                link(ts(t.bitcast(I32), x.bitcast(I32), 1, None, ALU.logical_shift_right))
                link(ts(y.bitcast(I32), t.bitcast(I32), -1.0, MAGIC, ALU.mult, ALU.add))
                for _ in range(3):
                    link(tt(t, y, y, ALU.mult))
                    link(stt(t, t, -0.5, x, ALU.mult, ALU.mult))
                    link(stt(y, t, 1.5, y, ALU.add, ALU.mult))

            def rms(line, n, scale, out_scale=None):
                a = st[:, line, 0:n]
                w = st[:, 7 + line, :]
                link(ts(a, a, scale, EPS, ALU.mult, ALU.add))
                rsqrt(w[:, 0:n], a, w[:, 8:8 + n])
                if out_scale:
                    link(ts(w[:, 0:n], w[:, 0:n], out_scale, None, ALU.mult))
                return w

            def pn_stat(p):
                wait(dve, *p.after["dve"])
                if p.po:
                    wait(dve, ev("po_x", p.po, 2, 2))
                wait(dve, ev("pn_ss", p, 2, 2))
                w = rms(p.n % 2, 2, 1.0 / D)
                x, y = rows(res[p.res]), rows(flat[p.xn])
                for m in range(2):
                    ts(y[:, m, :], x[:, m, :], w[:, m:m + 1], None, ALU.mult).then_inc(sem["pn_xn"], 1)

            def final(p):
                wait(dve, *p.after["dve"])
                dve.wait_ge(sem["fin_ss"], 2)
                w = rms(4, 2, 1.0 / D)
                dve.wait_ge(sem["gb_in"], 16 * p.gb)
                x = rows(res["x"])
                for m in range(2):
                    t = stt(x[:, m, :], x[:, m, :], w[:, m:m + 1], GB[:], ALU.mult, ALU.mult)
                t.then_inc(sem["fin_x"], 1)

            def po(p):
                wait(dve, p.wait.free)
                dve.wait_ge(sem["y_sq"], 4 * (p.n + 1))
                link(tt(st[:, 5, 0:2], st[:, 5, 0:2], st[:, 5, 2:4], ALU.add))
                w = rms(5, 2, 1.0 / D)
                x, y = rows(res[p.res]), rows(RB)
                if p.n and p.res == "x":
                    dve.wait_ge(sem["po_x"], 2 * p.n)
                for m in range(2):
                    stt(x[:, m, :], y[:, m, :], w[:, m:m + 1], x[:, m, :], ALU.mult, ALU.add).then_inc(sem["po_x"], 1)

            def T(p):
                if p.scale:
                    wait(dve, ("pp_cols", None, 0, 1) if p.scale[0] == "C1" else ("mf_c", None, 0, MODS[p.scale[1:3]] + 1))
                for b in p.banks:
                    wait(dve, ev("t_hi", p, 4, b + 1))
                    o = olo[:, p.slot, 2 * b:2 * b + 2, :]
                    if p.shift:
                        for i in range(2):
                            k = 2 * b + i
                            t = ts(aps[:, b, i * S:(i + 1) * S], aps[:, b, i * S:(i + 1) * S], column(p.scale, k),
                                   column(p.shift, k), ALU.mult, ALU.add)
                        link(t)
                        t = tt(o, tiles(bank(b), 2), f32(ohi[:, p.slot, 2 * b:2 * b + 2, :]), ALU.subtract)
                    elif p.scale:
                        for i in range(2):
                            k = 2 * b + i
                            t = stt(olo[:, p.slot, k, :], aps[:, b, i * S:(i + 1) * S], column(p.scale, k),
                                    f32(ohi[:, p.slot, k, :]), ALU.mult, ALU.subtract)
                    else:
                        t = stt(o, tiles(bank(b), 2), p.imm, f32(ohi[:, p.slot, 2 * b:2 * b + 2, :]), ALU.mult, ALU.subtract)
                    t.then_inc(sem["t_lo"], t_step(p, b))

            def pp_c(p):
                dve.wait_ge(sem["pp_th"], 1)
                link(stt(csb[:, 1, :], csb[:, 0, :], 1.0, aps[:, 3, 0:16], ALU.add, ALU.mult))
                link(ts(csb[:, 1, :], csb[:, 1, :], 0.5, None, ALU.mult))
                c = csb[:, 1, :].rearrange("p (v k) -> p k v", v=2)
                link(nc.vector.tensor_copy(chi[:, :, 0:2], c))
                tt(chi[:, :, 2:4], c, f32(chi[:, :, 0:2]), ALU.subtract).then_inc(sem["pp_c4"], 1)

            def pp(p):
                dve.wait_ge(sem["pp_pe"], 1)
                nc.vector.tensor_copy(C1[:], aps[:, 0, 0:P]).then_inc(sem["pp_cols"], 1)

            def pp2(p):
                link(nc.vector.memset(GLP[:, :, :].rearrange("p a b -> p (a b)"), 0.0))
                dve.wait_ge(sem["pp_pe2"], 1)
                nc.vector.tensor_copy(C2[:], aps[:, 0, 0:88])
                for l in range(LAYERS):
                    t = ts(CW[:, l, :], aps[:, 1 + l, 0:TAPS2 * KT], 0.5, None, ALU.mult)
                t.then_inc(sem["pp_cols2"], 1)

            def toep(p):
                dve.wait_ge(sem["tp_pe"], 1)
                tt(TR, aps[0:HEADS1, 3, 0:384], MSK, ALU.add).then_inc(sem["tp_r"], 1)

            def ba(p):
                d0 = 16 + (p.n % 2) * 16
                g = p.g // 2
                for hh in range(2):
                    wait(dve, ev("ba_s", p, 2, hh + 1))
                    dve.wait_ge(sem[f"bias_in{g % 2}"], 16 * (g // 2 + 1))
                    if p.n:
                        dve.wait_ge(sem["ba_tp"], 2 * p.n)
                    b = bias[:, g % 2, 2 * (p.g % 2) + hh, :]
                    stt(Pb[:, hh, 0:P], aps[:, hh, 0:P], HD1 ** -0.5, b[:, 0:P][:, ::-1], ALU.mult, ALU.add)
                    t = stt(Pb[:, hh, P:3 * P], aps[:, hh, P:3 * P], HD1 ** -0.5, b[:, ::-1], ALU.mult, ALU.add)
                    t.then_inc(sem["ba_sb"], 1)
                    wait(dve, ev("ba_sb", p, 2, hh + 1))
                    for m in range(2):
                        x = Pb[:, hh, 0:P] if m == 0 else Pb[:, hh, P:3 * P]
                        t = nc.vector.tensor_reduce(den[:, d0 + 2 * hh + m:d0 + 2 * hh + m + 1], x, AX.X, ALU.max, negate=True)
                    t.then_inc(sem["ba_nm"], 1)
                for hh in range(2):
                    wait(dve, ev("ba_p", p, 2, hh + 1))
                    e = d0 + 8 + 2 * hh
                    link(nc.vector.reciprocal(den[:, e:e + 2], den[:, e - 4:e - 2]))
                    for m in range(2):
                        x = Pb[:, hh, 0:P] if m == 0 else Pb[:, hh, P:3 * P]
                        t = ts(x, x, den[:, e + m:e + m + 1], None, ALU.mult)
                    t.then_inc(sem["ba_pn"], 1)

            def yn_scale(p):
                rs, x, t_ = GB[:, 0:S], GB[:, S:2 * S], GB[:, 2 * S:3 * S]
                dve.wait_ge(sem["yn_ss"], p.half + 1)
                dve.wait_ge(sem["tp_st"], 16)
                ts(x, aps[:, 2, 0:S], 2.0, EPS, ALU.mult, ALU.add).then_inc(sem["yn_ms"], 1)
                dve.wait_ge(sem["yn_ms"], p.half + 1)
                rsqrt(rs, x, t_)
                for k in range(4 * p.half, 4 * p.half + 4):
                    y = RB[:, k * S:(k + 1) * S]
                    t = stt(y, y, C1[:, 16 + k:17 + k], rs, ALU.mult, ALU.mult)
                t.then_inc(sem["yn_y"], 1)

            def yn_lo(p):
                wait(dve, ("yn_y", None, 0, p.half + 1), ("yn_hi", None, 0, p.half + 1))
                k = slice(4 * p.half, 4 * p.half + 4)
                tt(olo[:, p.slot, k, :], tiles(RB[:, p.half * 4 * S:(p.half + 1) * 4 * S], 4), f32(ohi[:, p.slot, k, :]),
                   ALU.subtract).then_inc(sem["yn_lo"], 1)

            def ma(p):
                d0 = (p.n % 2) * 8
                wait(dve, ev("ma_s", p))
                link(nc.vector.tensor_reduce(den[:, d0:d0 + 2], tiles(bank(0), 2), AX.X, ALU.max, negate=True))
                ts(den[:, d0 + 2:d0 + 4], den[:, d0:d0 + 2], HD_MEM ** -0.5, None, ALU.mult).then_inc(sem["ma_nm"], 1)
                wait(dve, ev("ma_p", p))
                link(nc.vector.reciprocal(den[:, d0 + 6:d0 + 8], den[:, d0 + 4:d0 + 6]))
                for m in range(2):
                    t = ts(Pb[:, m, 0:S], Pb[:, m, 0:S], den[:, d0 + 6 + m:d0 + 7 + m], None, ALU.mult)
                t.then_inc(sem["ma_pn"], 1)

            def maV(p):
                wait(dve, ev("ma_hi", p.of))
                k = slice(2 * p.of.h, 2 * p.of.h + 2)
                tt(olo[:, p.of.slot, k, :], tiles(bank(2), 2), f32(ohi[:, p.of.slot, k, :]),
                   ALU.subtract).then_inc(sem["ma_lo"], 1)

            def modfin(p):
                dve.wait_ge(sem["mf_in"], 80 * (p.n + 1))
                link(tt(MF[:, 0, :], MF[:, 0, :], MF[:, 1, :], ALU.add))
                tt(MF[:, 0, :], MF[:, 0, :], MF[:, 2, :], ALU.add).then_inc(sem["mf_sum"], 1)

            def mod_t(p):
                p = p.of
                i = MODS[p.l, p.s]
                wait(dve, ev("mf_pe", p), ev("mf_sum", p))
                link(nc.vector.tensor_copy(modc[:, i, :], aps[:, 3, 0:48]))
                for which in range(2):
                    t = stt(gsc[:, i, 8 * which:8 * which + 8], modc[:, i, 8 + 24 * which:16 + 24 * which], 1.0,
                            C2[:, 44 * p.l + 8 * which:44 * p.l + 8 * which + 8], ALU.add, ALU.mult)
                t.then_inc(sem["mf_c"], 1)
                tt(MF[:, 3, :], MF[:, 3, :], MF[:, 0, :], ALU.mult).then_inc(sem["mf_r"], 1)

            def rope(p):
                wait(dve, p.free)
                dve.wait_ge(sem["gqk_in"], 32 * (p.tab.n + 1))
                dve.wait_ge(sem["cst_in"], 32)
                T4 = GB[:].rearrange("p (t m d) -> p t m d", t=4, m=2)
                h = HD2 // 2
                for j in range(2):
                    for m in range(2):
                        tt(T4[:, 2 * j, m, :], cos2[:, m, :], GQK[:, j, :], ALU.mult)
                        tt(T4[:, 2 * j + 1, m, 0:h], sinpm[:, m, 0:h], GQK[:, j, h:HD2], ALU.mult)
                        t = tt(T4[:, 2 * j + 1, m, h:HD2], sinpm[:, m, h:HD2], GQK[:, j, 0:h], ALU.mult)
                link(t)

            def turn(x, nh, j, p, t1, t2):
                h = HD2 // 2
                for m in range(2):
                    xm = x[:, m, :].rearrange("p (h d) -> p h d", d=HD2)
                    if p.s == "c":
                        g = GQK[:, j, :].unsqueeze(1).to_broadcast([P, nh, HD2])
                        t = tt(xm, xm, g, ALU.mult)
                        continue
                    T4 = GB[:].rearrange("p (t m d) -> p t m d", t=4, m=2)
                    a, b = t1[:, m, :].rearrange("p (h d) -> p h d", d=HD2), t2[:, m, :].rearrange("p (h d) -> p h d", d=HD2)
                    cc = T4[:, 2 * j, m, :].unsqueeze(1).to_broadcast([P, nh, HD2])
                    s0 = T4[:, 2 * j + 1, m, 0:h].unsqueeze(1).to_broadcast([P, nh, h])
                    s1 = T4[:, 2 * j + 1, m, h:HD2].unsqueeze(1).to_broadcast([P, nh, h])
                    tt(a, xm, cc, ALU.mult)
                    tt(b[:, :, 0:h], xm[:, :, h:HD2], s0, ALU.mult)
                    t = tt(b[:, :, h:HD2], xm[:, :, 0:h], s1, ALU.mult)
                if p.s == "x":
                    link(t)
                    t = tt(x, t1, t2, ALU.add)
                return t

            def rq(p):
                c = p.of.c
                wait(dve, ev("q_cp", p.of))
                dve.wait_ge(sem["gqk_in"], 32 * (p.tab.n + 1))
                link(nc.vector.tensor_reduce(st[:, 2, 0:8], TT[:, 0, :].rearrange("p (u d) -> p u d", d=HD2), AX.X, ALU.add))
                x = rows(RA)[:, :, c * NW:(c + 1) * NW]
                turn(x, 4, 0, p, tiles(TT[:, 0, :], 2), tiles(TT[:, 1, :], 2)).then_inc(sem["rq_done"], 1)
                w = rms(2, 8, 1.0 / HD2)
                link(ts(st[:, 3, 8 * c:8 * c + 8], w[:, 0:8], HD2 ** -0.5, None, ALU.mult))

            def rk(p):
                wait(dve, ev("kv_cp", p.of))
                dve.wait_ge(sem["gqk_in"], 32 * (p.tab.n + 1))
                k_ = AB[:, 0:2 * S]
                link(nc.vector.tensor_reduce(st[:, 2, 0:4], AB[:, 2 * S:4 * S].rearrange("p (u d) -> p u d", d=HD2),
                                             AX.X, ALU.add))
                w = rms(2, 4, 1.0 / HD2)
                ku = k_.rearrange("p (u d) -> p u d", d=HD2)
                link(tt(ku, ku, w[:, 0:4].unsqueeze(2).to_broadcast([P, 4, HD2]), ALU.mult))
                turn(tiles(k_, 2), 2, 1, p, tiles(TT[:, 1, 0:2 * S], 2), tiles(TT[:, 1, 2 * S:4 * S], 2)).then_inc(sem["rk_done"], 1)

            def at(p):
                d0 = (p.n % 2) * 8
                nk = 2 * S if p.s == "x" else S
                u = (p.h // 4) * 8 + p.h % 4
                wait(dve, ev("at_s", p, 2, 2))
                link(nc.vector.tensor_reduce(den[:, d0:d0 + 2], aps[:, 0:2, 0:nk], AX.X, ALU.max, negate=True))
                tt(den[:, d0 + 2:d0 + 4], den[:, d0:d0 + 2], st[:, 3, u:u + 5:4], ALU.mult).then_inc(sem["at_nb"], 1)

            def atR(p):
                p = p.of
                d0 = (p.n % 2) * 8
                wait(dve, ev("at_p", p, 2, 2))
                nc.vector.reciprocal(den[:, d0 + 6:d0 + 8], den[:, d0 + 4:d0 + 6]).then_inc(sem["at_r"], 1)

            def atL(p):
                wait(dve, ev("at_hi", p.of))
                tt(olo[:, p.of.slot, p.of.h, :], aps[:, 2, 0:S], f32(ohi[:, p.of.slot, p.of.h, :]),
                   ALU.subtract).then_inc(sem["at_lo"], 1)

            def gv_rms(p):
                wait(dve, ev("gn_ss", p, 4, 4))
                link(tt(st[:, 6, 0:2], st[:, 6, 0:2], st[:, 6, 2:4], ALU.add))
                rms(6, 2, 0.25 / D, 0.5)

            def gv_norm(p):
                dve.wait_ge(sem["gb_in"], 16 * p.gb)
                m = p.half
                x = rows(RA)[:, m, :]
                stt(x, x, st[:, 13, m:m + 1], GB[:], ALU.mult, ALU.mult).then_inc(sem["gn_done"], 1)

            def spatial(p):
                wait(dve, ev("ge_out", p.gu[1]))
                x = rows(RB)
                for g in range(4):
                    wait(dve, ev("sp_pe", p, 4, g + 1))
                    xg = x[:, :, g * S:(g + 1) * S]
                    t = stt(xg, tiles(bank(g), 2), C2[:, 44 * p.l + 40 + g:44 * p.l + 41 + g], xg, ALU.add, ALU.mult)
                t.then_inc(sem["sp_done"], 1)

            def conv(p):
                for tap in p.taps:
                    for i in range(4):
                        k = 4 * p.half + i
                        y, x = Yc[:, k * S:(k + 1) * S], GLP[:, k, tap:tap + S]
                        if tap == 1:
                            wait(dve, ev("cv_first", p.of))
                        else:
                            dve.wait_ge(sem["cv_done"], conv_ops[0] - 3)
                        stt(y, x, CW[:, p.l, tap * KT + k:tap * KT + k + 1], y, ALU.mult, ALU.add).then_inc(sem["cv_done"], 1)
                        conv_ops[0] += 1

            def diag_add(p):
                wait(dve, ev("dg_used", p.of), ("cv_done", None, 0, p.conv_after))
                tt(Yc[:, 4 * S:8 * S], Yc[:, 4 * S:8 * S], aps[:, 0:2, :].rearrange("p a b -> p (a b)"),
                   ALU.add).then_inc(sem["dg_add"], 1)

            def ln_mu(p):
                wait(dve, ev("ln_mean", p))
                y = tiles(Yc[:], KT)
                tt(y, y, aps[:, 2, 0:S].unsqueeze(1).to_broadcast([P, KT, S]), ALU.subtract).then_inc(sem["ln_d"], 1)

            def ln_var(p):
                wait(dve, ev("ln_vs", p))
                x, r, t_ = PTb[:, 0:S], PTb[:, S:2 * S], PTb[:, 2 * S:3 * S]
                link(ts(x, aps[:, 3, 0:S], EPS, None, ALU.add))
                rsqrt(r, x, t_)
                for half in range(2):
                    y = tiles(Yc[:, half * 4 * S:(half + 1) * 4 * S], 4)
                    tt(y, y, r.unsqueeze(1).to_broadcast([P, 4, S]), ALU.mult).then_inc(sem["ln_n"], 1)

            def ln_out(p):
                half, ks = slice(p.half * 4 * S, (p.half + 1) * 4 * S), slice(4 * p.half, 4 * p.half + 4)
                wait(dve, ev("ln_th", p))
                stt(RB[:, half], RB[:, half], 1.0, Yc[:, half], ALU.add, ALU.mult).then_inc(sem["ln_r"], 1)
                wait(dve, ev("ln_hi", p))
                stt(olo[:, p.slot, ks, :], tiles(RB[:, half], 4), 0.5, f32(ohi[:, p.slot, ks, :]), ALU.mult,
                    ALU.subtract).then_inc(sem["ln_lo"], 1)

            stages = dict(pn_stat=pn_stat, final=final, po=po, T=T, pp_c=pp_c, pp=pp, pp2=pp2, toep=toep, ba=ba, ynM=yn_scale, ynL=yn_lo, ma=ma,
                          maV=maV, modfin=modfin, modT=mod_t, rope=rope, rq=rq, rk=rk, at=at, atR=atR, atL=atL, gv_rms=gv_rms, gv_norm=gv_norm, spatial=spatial,
                          conv=conv, diag_add=diag_add, ln_mu=ln_mu, ln_var=ln_var, ln_out=ln_out)
            LATE = ("conv", "ynM", "diag_add", "rq", "rk", "gv_rms", "gv_norm", "final")

            def res_add(jb, g):
                dve.wait_ge(used[NQ - 1], jb.i + 1)
                x = rows(res[jb.res])[:, :, jb.n0:jb.n0 + NW]
                if jb.n:
                    dve.wait_ge(sem["res_done"], jb.n)
                tt(x, x, tiles(g, 2), ALU.add).then_inc(sem["res_done"], 1)

            def gelu(jb, g):
                t0 = TT[:, 0, :]
                wait(dve, ev("ge_sq", jb))
                tt(t0, t0, g, ALU.mult).then_inc(sem["ge_z"], 1)

            def gelu_out(jb, g):
                wait(dve, ev("ge_t", jb))
                stt(rows(flat[jb.dst[0]])[:, :, jb.dst[1] * NW:(jb.dst[1] + 1) * NW], tiles(TT[:, 1, :], 2), 1.0, tiles(g, 2),
                    ALU.add, ALU.mult).then_inc(sem["ge_out"], 1)

            def glu_g(jb, g):
                wait(dve, ev("gl_th", jb), ev("gl_a", jb.of))
                stt(GLP[:, 4 * jb.half:4 * jb.half + 4, PAD2:PAD2 + S], tiles(TT[:, 1, :], 4), 1.0, tiles(AB[:], 4), ALU.add,
                    ALU.mult).then_inc(sem["gl_o"], 1)

            def branch(jb, g):
                dve.wait_ge(used[NQ - 1], jb.i + 1)
                wait(dve, ev("ga_th", jb.gate))
                gt = tiles(AB[:] if jb.gate.n % 2 == 0 else TT[:, 1, :], 2)
                x = rows(RA)[:, :, jb.j * NW:(jb.j + 1) * NW]
                if jb.first:
                    stt(x, gt, 1.0, tiles(g, 2), ALU.add, ALU.mult).then_inc(sem["br_out"], 1)
                else:
                    link(stt(tiles(TT[:, 0, :], 2), gt, 1.0, tiles(g, 2), ALU.add, ALU.mult))
                    dve.wait_ge(sem["br_out"], jb.n)
                    tt(x, x, tiles(TT[:, 0, :], 2), ALU.add).then_inc(sem["br_out"], 1)

            def relu2(jb, g):
                t_ = TT[:, jb.n % 2, :]
                wait(dve, ev("r2_relu", jb))
                tt(t_, t_, t_, ALU.mult).then_inc(sem["r2_sq"], 1)

            def relu2_lo(jb, g):
                t_ = TT[:, jb.n % 2, :]
                wait(dve, ev("r2_hi", jb), ev("r2_sq", jb))
                k = (jb.c % 2) * 4
                tt(olo[:, jb.out, k:k + 4, :], tiles(t_, 4), f32(ohi[:, jb.out, k:k + 4, :]), ALU.subtract).then_inc(sem["r2_lo"], 1)

            def acc(jb, g):
                dve.wait_ge(used[NQ - 1], jb.i + 1)
                wait(dve, ("ac_cp", jb.first_of, 1, 1))
                if jb.n:
                    dve.wait_ge(sem["ac_add"], jb.n)
                y = rows(RB)[:, :, jb.j * NW:(jb.j + 1) * NW]
                tt(y, y, tiles(g, 2), ALU.add).then_inc(sem["ac_add"], 1)

            def gain(jb, src):
                j = slice(jb.j * NW, (jb.j + 1) * NW)
                dve.wait_ge(sem["gb_in"], 16 * jb.gb)
                for m in range(2):
                    dve.wait_ge(sem["y_sq"], 2 * jb.y + m + 1)
                    t = tt(rows(RB)[:, m, j], src[:, m, :], GB[:, j], ALU.mult)
                t.then_inc(sem["y_cp"], 1)
                for p in jb.then:
                    po(p)

            def ycp(jb, g):
                gain(jb, tiles(g, 2))

            def accy(jb, g):
                dve.wait_ge(used[NQ - 1], jb.i + 1)
                y = rows(RB)[:, :, jb.j * NW:(jb.j + 1) * NW]
                wait(dve, ("ac_add", jb.before, 1, 1))
                tt(y, y, tiles(g, 2), ALU.add).then_inc(sem["y_add"], 1)
                dve.wait_ge(sem["y_add"], jb.n + 1)
                gain(jb, y)

            def cgate(jb, g):
                n = jb.cols // P
                wait(dve, ev("cg_cp", jb))
                for tap in (2, 1, 0):
                    for i in range(n):
                        k = 4 * jb.c + i
                        y, x = Yc[:, i * S:(i + 1) * S], GLP[:, i, PAD2 - 2 + tap:PAD2 - 2 + tap + S]
                        w = C1[:, 62 + tap * NT1 + k:63 + tap * NT1 + k]
                        if tap == 2:
                            t = ts(y, x, w, C1[:, 40 + k:41 + k], ALU.mult, ALU.add)
                        else:
                            t = stt(y, x, w, y, ALU.mult, ALU.add)
                        if tap and i == n - 1:
                            link(t)
                t.then_inc(sem["cg_v"], 1)

            def cgate_silu(jb, g):
                n = jb.cols // P
                wait(dve, ev("cg_t", jb), ev("cg_v", jb))
                stt(AB[:, 0:n * S], TT[:, 1, 0:n * S], 1.0, Yc[:, 0:n * S], ALU.add, ALU.mult).then_inc(sem["cg_s"], 1)

            def up(jb, g):
                n = jb.cols // P
                dve.wait_ge(used[NQ - 1], jb.i + 1)
                wait(dve, ev("cg_s", jb.gate))
                t0 = TT[:, 0, 0:n * S]
                tt(t0, AB[:, 0:n * S], g[:, 0:n * S], ALU.mult).then_inc(sem["up_mul"], 1)

            def up_lo(jb, g):
                n = jb.cols // P
                t0 = TT[:, 0, 0:n * S]
                wait(dve, ev("up_hi", jb), ev("up_mul", jb))
                k = (jb.c % 2) * 4
                stt(olo[:, jb.out, k:k + n, :], tiles(t0, n), 0.5, f32(ohi[:, jb.out, k:k + n, :]), ALU.mult,
                    ALU.subtract).then_inc(sem["up_lo"], 1)

            evacs = dict(res=res_add, gelu=gelu, branch=branch, relu2=relu2, acc=acc, accy=accy, ycp=ycp, cgate=cgate, up=up)
            second = dict(gelu=gelu_out, relu2=relu2_lo, cgate=cgate_silu, up=up_lo, glu_g=glu_g)

            def split(jb, q):
                dve.wait_ge(hi_done[q], jb.i + 1)
                tt(part(wlo, jb, q), part(raw, jb, q), f32(part(whi, jb, q)), ALU.subtract).then_inc(lo_done[q], 1)

            link(nc.vector.memset(MF[:, :, :].rearrange("p a b -> p (a b)"), 1.0))
            link(nc.vector.memset(chi[:, :, :].rearrange("p a b -> p (a b)").bitcast(F32), 0.0))
            for q in range(NQ):
                for p in jobs[0].first[q]:
                    stages[p.kind](p)
                split(jobs[0], q)
            for jb in jobs + [None]:
                if jb is None:
                    po(tail[0])
                    break
                nxt = jobs[jb.i + 1] if jb.i + 1 < len(jobs) else None
                for q in range(NQ):
                    for p in jb.aux[q]:
                        if p.kind in stages and p.kind not in LATE and not (p.kind == "po" and p in p.wait.then):
                            stages[p.kind](p)
                    if q == NQ - 1 and jb.evac in evacs:
                        wait(dve, *jb.after.get("dve", []))
                        evacs[jb.evac](jb, psum_job(jb))
                    if nxt:
                        split(nxt, q)
                    if q == NQ - 1 and jb.evac in second:
                        second[jb.evac](jb, psum_job(jb))
                    for p in jb.aux[q]:
                        if p.kind in LATE:
                            stages[p.kind](p)


FIRST = ["x", "mem", "w_in", "g_mix", "g_out_dil", "g_out_moba", "w_out", "rel_bias", "g_cross", "g_mem", "w_q_mem", "w_kv_mem",
         "w_o_mem", "g_ffn", "w_gate", "w_up", "conv_w", "conv_b", "w_down", "g_final"]
SECOND = ["c_2", "ctx_2", "c_ctx_2", "ada_w_2", "ada_b_2", "mix_pre_g_2", "mix_post_g_2", "w_in_2", "q_norm_g_2", "k_norm_g_2",
          "w_attn_o_2", "gmlp_norm_g_2", "gmlp_ws_2", "gmlp_bs_2", "w_gmlp_o_2", "conv_w_2", "conv_b_2", "conv_norm_g_2",
          "conv_norm_b_2", "w_conv_o_2", "w_out_2", "ffn_pre_g_2", "ffn_post_g_2", "w_ff1_2", "w_ff2_2"]


def views(t):
    A = {k: t[k] for k in ("rel_bias", "g_final", "onehot", "mask", "cos2", "sinpm")}
    for k in ("x", "mem", "w_in", "g_mix", "g_out_dil", "g_out_moba", "w_out", "g_cross", "g_mem", "g_ffn", "w_gate", "w_up",
              "conv_w", "conv_b", "w_down"):
        A[k] = t[k][0]
    A["w_q"], A["w_kv"], A["w_o"] = t["w_q_mem"][0], t["w_kv_mem"][0], t["w_o_mem"][0]
    A["c"], A["ctx"], A["c_ctx"] = t["c_2"], t["ctx_2"][0], t["c_ctx_2"]
    for k in ("ada_b", "mix_pre_g", "mix_post_g", "q_norm_g", "k_norm_g", "gmlp_norm_g", "gmlp_ws", "gmlp_bs", "conv_norm_g",
              "conv_norm_b", "ffn_pre_g", "ffn_post_g"):
        A[k] = t[k + "_2"]
    A["conv_w_2"], A["conv_b_2"] = t["conv_w_2"], t["conv_b_2"]
    for l in range(LAYERS):
        for k, name in (("ada", "ada_w_2"), ("win", "w_in_2"), ("attn", "w_attn_o_2"), ("gmlp", "w_gmlp_o_2"),
                        ("conv", "w_conv_o_2"), ("out", "w_out_2"), ("ff1", "w_ff1_2"), ("ff2", "w_ff2_2")):
            A[f"{k}{l}"] = t[name][l]
    return A


def kernel(**inputs):
    import concourse.bacc as bacc
    from concourse.bass_utils import run_bass_kernel_spmd

    nc = bacc.Bacc("TRN2", target_bir_lowering=False, num_devices=1)
    arrays = {k: np.ascontiguousarray(inputs[k]) for k in FIRST + SECOND}
    arrays["onehot"], arrays["mask"] = toeplitz_constants()
    arrays["cos2"], arrays["sinpm"] = rope_constants()
    t = {k: nc.dram_tensor(k, a.shape, mybir.dt.from_np(a.dtype), kind="ExternalInput").ap() for k, a in arrays.items()}
    out = nc.dram_tensor("out", (1, S, D), F32, kind="ExternalOutput").ap()
    build(nc, views(t), out)
    return run_bass_kernel_spmd(nc, [arrays], core_ids=[0]).results[0]["out"]
```
